# Optimizing a Trainium2 kernel written in Bass

```python
import jax, jax.numpy as jnp
from jax import lax
import numpy as np
import math

D_MODEL = 1024
BATCH = 1
SEQ = 512
DEPTH = 1

GRID_W = 64
CTX_LEN = 256
N_FOURIER_GROUPS = 4
FOURIER_GROUP_W = 128
FOURIER_W = N_FOURIER_GROUPS * FOURIER_GROUP_W
N_HEADS = 8
QK_NOPE = 64
QK_ROPE = 32
HEAD_QK = QK_NOPE + QK_ROPE
V_DIM = 64
Q_LORA = 256
KV_LORA = 128
MLA_W = N_HEADS * V_DIM
N_BRANCH = 2
D_FF = 4 * D_MODEL
D_IN = FOURIER_W + Q_LORA + KV_LORA + QK_ROPE + N_BRANCH * D_MODEL
ROPE_THETA = 10000.0
Q_BLOCK = 128
EPS = 1e-6


def rmsnorm(x, g):
    xf = x.astype(jnp.float32)
    y = xf * lax.rsqrt(jnp.mean(xf * xf, axis=-1, keepdims=True) + EPS)
    return (y * g.astype(jnp.float32)).astype(x.dtype)

def modulate(h, shift, scale):
    return h * (1 + scale) + shift

def axial_rope_tables(n):
    rows = n // GRID_W
    row = jnp.repeat(jnp.arange(rows, dtype=jnp.float32), GRID_W)
    col = jnp.tile(jnp.arange(GRID_W, dtype=jnp.float32), rows)
    n_freq = QK_ROPE // 4
    freqs = ROPE_THETA ** (-jnp.arange(n_freq, dtype=jnp.float32) / n_freq)
    ang_r = row[:, None] * freqs[None, :]
    ang_c = col[:, None] * freqs[None, :]
    ang = jnp.concatenate([ang_r, ang_r, ang_c, ang_c], axis=-1)
    return jnp.cos(ang), jnp.sin(ang)

def apply_rope(x, cos, sin):
    a1, a2, b1, b2 = jnp.split(x, 4, axis=-1)
    rot = jnp.concatenate([-a2, a1, -b2, b1], axis=-1)
    return x * cos[None, :, None, :].astype(x.dtype) + rot * sin[None, :, None, :].astype(x.dtype)

def split_proj(p):
    o1 = FOURIER_W
    o2 = o1 + Q_LORA
    o3 = o2 + KV_LORA
    o4 = o3 + QK_ROPE
    return p[..., :o1], p[..., o1:o2], p[..., o2:o3], p[..., o3:o4], p[..., o4:]

def fourier_mix(f):
    B, N, _ = f.shape
    fg = f.reshape(B, N, N_FOURIER_GROUPS, FOURIER_GROUP_W).astype(jnp.float32)
    y = jnp.fft.fft2(fg, axes=(1, 3), norm="ortho").real
    return y.reshape(B, N, FOURIER_W).astype(f.dtype)

def mla_kv(kv_lat, k_rope, kv_norm_g, w_kvb, k_gain, rope):
    B, N, _ = kv_lat.shape
    kv = (rmsnorm(kv_lat, kv_norm_g) @ w_kvb).reshape(B, N, N_HEADS, QK_NOPE + V_DIM)
    k_nope, v = kv[..., :QK_NOPE], kv[..., QK_NOPE:]
    k_r = jnp.broadcast_to(k_rope[:, :, None, :], (B, N, N_HEADS, QK_ROPE))
    k = rmsnorm(jnp.concatenate([k_nope, k_r], axis=-1), k_gain)
    if rope is not None:
        k = jnp.concatenate([k[..., :QK_NOPE], apply_rope(k[..., QK_NOPE:], *rope)], axis=-1)
    return k, v

def mla_q(q_lat, q_norm_g, w_qb, q_gain, rope):
    B, N, _ = q_lat.shape
    q = (rmsnorm(q_lat, q_norm_g) @ w_qb).reshape(B, N, N_HEADS, HEAD_QK)
    q = rmsnorm(q, q_gain)
    if rope is not None:
        q = jnp.concatenate([q[..., :QK_NOPE], apply_rope(q[..., QK_NOPE:], *rope)], axis=-1)
    return q

def latent_attention(q, k_all, v_all):
    B, S, H, Dh = q.shape
    nb = S // Q_BLOCK
    qb = q.reshape(B, nb, Q_BLOCK, H, Dh).transpose(1, 0, 2, 3, 4)
    scale = HEAD_QK ** -0.5

    def one_block(qblk):
        s = jnp.einsum('bqhd,bkhd->bhqk', qblk, k_all, preferred_element_type=jnp.float32) * scale
        p = jax.nn.softmax(s, axis=-1).astype(v_all.dtype)
        return jnp.einsum('bhqk,bkhd->bqhd', p, v_all)

    o = lax.map(one_block, qb)
    return o.transpose(1, 0, 2, 3, 4).reshape(B, S, H * V_DIM)

def context_attention(q, k, v):
    B, N = q.shape[0], q.shape[1]
    s = jnp.einsum('bqhd,bkhd->bhqk', q, k, preferred_element_type=jnp.float32) * (HEAD_QK ** -0.5)
    p = jax.nn.softmax(s, axis=-1).astype(v.dtype)
    return jnp.einsum('bhqk,bkhd->bqhd', p, v).reshape(B, N, N_HEADS * V_DIM)

def merge_branches(f_mix, att, gates, w_fourier, w_mla_o, b_gate, w_out):
    g = jax.nn.sigmoid(gates + b_gate)
    g_f, g_a = g[..., :D_MODEL], g[..., D_MODEL:]
    y = g_f * (f_mix @ w_fourier) + g_a * (att @ w_mla_o)
    return y @ w_out

def sq_relu_mlp(h, w_up, w_down):
    return jnp.square(jax.nn.relu(h @ w_up)) @ w_down

def first_inputs(seed: int = 0) -> dict:
    key = jax.random.key(seed)
    ks = jax.random.split(key, 24)
    D, L = D_MODEL, DEPTH

    def w(k, shape, fan_in, mult=1.0):
        return jax.random.normal(k, shape, jnp.float32) * (mult * fan_in ** -0.5)

    def gain(k, shape):
        return 1.0 + 0.05 * jax.random.normal(k, shape, jnp.float32)

    return {
        "x": jax.random.normal(ks[0], (BATCH, SEQ, D), jnp.float32),
        "c": jax.random.normal(ks[1], (BATCH, D), jnp.float32),
        "ctx": jax.random.normal(ks[2], (BATCH, CTX_LEN, D), jnp.float32),
        "c_ctx": jax.random.normal(ks[3], (D,), jnp.float32),
        "ada_w": w(ks[4], (L, D, 6 * D), D, 0.5),
        "ada_b": 0.02 * jax.random.normal(ks[5], (L, 6 * D), jnp.float32),
        "norm1_g": gain(ks[6], (L, D)),
        "norm2_g": gain(ks[7], (L, D)),
        "w_in": w(ks[8], (L, D, D_IN), D),
        "b_gate": 0.02 * jax.random.normal(ks[9], (L, N_BRANCH * D), jnp.float32),
        "w_fourier": w(ks[10], (L, FOURIER_W, D), FOURIER_W),
        "q_norm_g": gain(ks[11], (L, Q_LORA)),
        "w_qb": w(ks[12], (L, Q_LORA, N_HEADS * HEAD_QK), Q_LORA),
        "kv_norm_g": gain(ks[13], (L, KV_LORA)),
        "w_kvb": w(ks[14], (L, KV_LORA, N_HEADS * (QK_NOPE + V_DIM)), KV_LORA),
        "q_gain": gain(ks[15], (L, HEAD_QK)),
        "k_gain": gain(ks[16], (L, HEAD_QK)),
        "w_mla_o": w(ks[17], (L, MLA_W, D), MLA_W),
        "w_out": w(ks[18], (L, D, D), D),
        "w_up": w(ks[19], (L, D, D_FF), D),
        "w_down": w(ks[20], (L, D_FF, D), D_FF),
    }

def first_block(x, c, ctx, c_ctx, ada_w, ada_b, norm1_g, norm2_g, w_in, b_gate, w_fourier, q_norm_g, w_qb,
              kv_norm_g, w_kvb, q_gain, k_gain, w_mla_o, w_out, w_up, w_down):
    rope = axial_rope_tables(x.shape[1])
    for l in range(DEPTH):
        last = l == DEPTH - 1
        mod_x = jax.nn.silu(c) @ ada_w[l] + ada_b[l]
        sh1, sc1, g1, sh2, sc2, g2 = jnp.split(mod_x[:, None, :], 6, axis=-1)
        mod_c = jax.nn.silu(c_ctx) @ ada_w[l] + ada_b[l]
        csh1, csc1, cg1, csh2, csc2, cg2 = jnp.split(mod_c, 6, axis=-1)

        hc = modulate(rmsnorm(ctx, norm1_g[l]), csh1, csc1)
        pc = hc @ w_in[l]
        fc, qlc, kvlc, krc, gc = split_proj(pc)
        kc, vc = mla_kv(kvlc, krc, kv_norm_g[l], w_kvb[l], k_gain[l], None)

        hx = modulate(rmsnorm(x, norm1_g[l]), sh1, sc1)
        px = hx @ w_in[l]
        fx, qlx, kvlx, krx, gx = split_proj(px)
        kx, vx = mla_kv(kvlx, krx, kv_norm_g[l], w_kvb[l], k_gain[l], rope)
        qx = mla_q(qlx, q_norm_g[l], w_qb[l], q_gain[l], rope)
        att_x = latent_attention(qx, jnp.concatenate([kx, kc], axis=1), jnp.concatenate([vx, vc], axis=1))
        y_x = merge_branches(fourier_mix(fx), att_x, gx, w_fourier[l], w_mla_o[l], b_gate[l], w_out[l])

        if not last:
            qc = mla_q(qlc, q_norm_g[l], w_qb[l], q_gain[l], None)
            att_c = context_attention(qc, kc, vc)
            y_c = merge_branches(fourier_mix(fc), att_c, gc, w_fourier[l], w_mla_o[l], b_gate[l], w_out[l])
            ctx = ctx + cg1 * y_c
            hc2 = modulate(rmsnorm(ctx, norm2_g[l]), csh2, csc2)
            ctx = ctx + cg2 * sq_relu_mlp(hc2, w_up[l], w_down[l])

        x = x + g1 * y_x
        h2 = modulate(rmsnorm(x, norm2_g[l]), sh2, sc2)
        x = x + g2 * sq_relu_mlp(h2, w_up[l], w_down[l])
    return x


CHUNK = 64
A_HEADS = 8
A_DK = 128
A_DV = 128
A_QK = A_HEADS * A_DK
A_VW = A_HEADS * A_DV
CONV_K = 4
A_CONV_CH = 2 * A_QK + A_VW
B_HEADS = 16
B_DH = 64
B_W = B_HEADS * B_DH
BAND_CHUNKS = 8
BAND_LEN = (BAND_CHUNKS + 1) * CHUNK
MAX_REL = 256
N_REL = (CHUNK - 1) + MAX_REL + 1
MEM_LEN = 256
M_HEADS = 4
M_DH = D_MODEL // M_HEADS
D_FF_2 = ((8 * D_MODEL + 3 * 256 - 1) // (3 * 256)) * 256
IN_SPLITS = (A_QK, A_QK, A_VW, A_VW, A_HEADS, A_HEADS, B_W, B_W, B_W, D_MODEL, D_MODEL)
N_IN = sum(IN_SPLITS)


def rmsnorm_2(x, g):
    xf = x.astype(jnp.float32)
    y = xf * lax.rsqrt(jnp.mean(xf * xf, axis=-1, keepdims=True) + EPS)
    return (y * g.astype(jnp.float32)).astype(x.dtype)

def _l2norm(x):
    return x * lax.rsqrt(jnp.sum(x * x, axis=-1, keepdims=True) + EPS)

def _split_cols(t, sizes):
    outs, start = [], 0
    for n in sizes:
        outs.append(t[..., start:start + n])
        start += n
    return outs

def _to_chunks(t, h, d):
    b, s, _ = t.shape
    return t.reshape(b, s // CHUNK, CHUNK, h, d).transpose(0, 3, 1, 2, 4)

def _heads_to_chunks(t):
    b, s, h = t.shape
    return t.reshape(b, s // CHUNK, CHUNK, h).transpose(0, 3, 1, 2)

def _causal_dwconv(t, w):
    return lax.conv_general_dilated(
        t, w[:, None, :], window_strides=(1,), padding=[(CONV_K - 1, 0)],
        dimension_numbers=("NWC", "WIO", "NWC"), feature_group_count=t.shape[-1])

def _gated_deltanet(q, k, v, alpha, beta, a_log, dt_bias):
    dtype = v.dtype
    b, s, _ = v.shape
    f32 = jnp.float32
    q = _l2norm(_to_chunks(q.astype(f32), A_HEADS, A_DK)) * (A_DK ** -0.5)
    k = _l2norm(_to_chunks(k.astype(f32), A_HEADS, A_DK))
    v = _to_chunks(v.astype(f32), A_HEADS, A_DV)
    beta = _heads_to_chunks(jax.nn.sigmoid(beta.astype(f32)))
    g = -jnp.exp(a_log.astype(f32)) * jax.nn.softplus(alpha.astype(f32) + dt_bias.astype(f32))
    G = jnp.cumsum(_heads_to_chunks(g), axis=-1)
    incl = jnp.tril(jnp.ones((CHUNK, CHUNK), dtype=bool))
    strict = jnp.tril(jnp.ones((CHUNK, CHUNK), dtype=bool), -1)
    diff = G[..., :, None] - G[..., None, :]
    decay = jnp.where(incl, jnp.exp(jnp.where(incl, diff, 0.0)), 0.0)
    kk = jnp.einsum("bhncd,bhnjd->bhncj", k, k)
    L = jnp.where(strict, beta[..., :, None] * kk * decay, 0.0)
    rhs = jnp.concatenate([beta[..., None] * v, (beta * jnp.exp(G))[..., None] * k], axis=-1)
    sol = lax.linalg.triangular_solve(jnp.eye(CHUNK, dtype=f32) + L, rhs, left_side=True,
                                      lower=True, unit_diagonal=True)
    u_t, w = sol[..., :A_DV], sol[..., A_DV:]
    p_intra = jnp.einsum("bhncd,bhnjd->bhncj", q, k) * decay
    q_dec = q * jnp.exp(G)[..., None]
    g_last = G[..., -1]
    k_dec = k * jnp.exp(g_last[..., None] - G)[..., None]
    xs = tuple(jnp.moveaxis(t, 2, 0) for t in (u_t, w, p_intra, q_dec, k_dec, jnp.exp(g_last)))

    def step(S, inp):
        ut, wt, pt, qt, kt, et = inp
        U = ut - jnp.einsum("bhck,bhkv->bhcv", wt, S)
        o = jnp.einsum("bhck,bhkv->bhcv", qt, S) + jnp.einsum("bhcj,bhjv->bhcv", pt, U)
        S = S * et[..., None, None] + jnp.einsum("bhck,bhcv->bhkv", kt, U)
        return S, o

    S0 = jnp.zeros((b, A_HEADS, A_DK, A_DV), f32)
    _, o = lax.scan(step, S0, xs)
    return o.transpose(1, 0, 3, 2, 4).reshape(b, s, A_HEADS, A_DV).astype(dtype)

def _band_bias(rel_bias):
    i = jnp.arange(CHUNK)[:, None]
    kpos = jnp.arange(BAND_LEN)[None, :]
    r = (BAND_CHUNKS - kpos // CHUNK) * CHUNK + i - kpos % CHUNK
    idx = jnp.clip(r, -(CHUNK - 1), MAX_REL) + (CHUNK - 1)
    return rel_bias[:, idx].astype(jnp.float32)

def _chunk_band_attention(q, k, v, bias):
    b, s, _ = q.shape
    q = _to_chunks(q, B_HEADS, B_DH)
    pad = ((0, 0), (0, 0), (BAND_CHUNKS, 0), (0, 0), (0, 0))
    kp = jnp.pad(_to_chunks(k, B_HEADS, B_DH), pad)
    vp = jnp.pad(_to_chunks(v, B_HEADS, B_DH), pad)
    key_chunk_off = jnp.repeat(jnp.arange(BAND_CHUNKS + 1), CHUNK) - BAND_CHUNKS
    scale = B_DH ** -0.5

    def one_chunk(n):
        qn = lax.dynamic_index_in_dim(q, n, axis=2, keepdims=False)
        kb = lax.dynamic_slice_in_dim(kp, n, BAND_CHUNKS + 1, axis=2).reshape(b, B_HEADS, BAND_LEN, B_DH)
        vb = lax.dynamic_slice_in_dim(vp, n, BAND_CHUNKS + 1, axis=2).reshape(b, B_HEADS, BAND_LEN, B_DH)
        sc = jnp.einsum("bhqd,bhkd->bhqk", qn, kb).astype(jnp.float32) * scale + bias
        sc = jnp.where((n + key_chunk_off) >= 0, sc, -1e30)
        p = jax.nn.softmax(sc, axis=-1).astype(vb.dtype)
        return jnp.einsum("bhqk,bhkd->bhqd", p, vb)

    o = lax.map(one_chunk, jnp.arange(s // CHUNK))
    return o.transpose(1, 0, 3, 2, 4).reshape(b, s, B_W)

def _memory_xattn(h, memn, w_q, w_kv, w_out):
    b, s, _ = h.shape
    m = memn.shape[1]
    q = (h @ w_q).reshape(b, s, M_HEADS, M_DH)
    kk, vv = _split_cols(memn @ w_kv, (M_HEADS * M_DH, M_HEADS * M_DH))
    kk = kk.reshape(b, m, M_HEADS, M_DH)
    vv = vv.reshape(b, m, M_HEADS, M_DH)
    sc = jnp.einsum("bqhd,bkhd->bhqk", q, kk).astype(jnp.float32) * (M_DH ** -0.5)
    p = jax.nn.softmax(sc, axis=-1).astype(vv.dtype)
    o = jnp.einsum("bhqk,bkhd->bqhd", p, vv).reshape(b, s, M_HEADS * M_DH)
    return o @ w_out

def second_inputs(seed: int = 0) -> dict:
    key = jax.random.key(seed)
    ks = jax.random.split(key, 24)
    f32 = jnp.float32

    def nrm(k, shape, scale):
        return jax.random.normal(k, shape, f32) * scale

    def gain(k, shape):
        return 1.0 + 0.02 * jax.random.normal(k, shape, f32)

    dt = jnp.exp(jax.random.uniform(ks[6], (DEPTH, A_HEADS), f32, math.log(1e-3), math.log(1e-1)))
    return {
        "x": nrm(ks[0], (BATCH, SEQ, D_MODEL), 1.0),
        "mem": nrm(ks[1], (BATCH, MEM_LEN, D_MODEL), 1.0),
        "norm_mix": gain(ks[2], (DEPTH, D_MODEL)),
        "w_in": nrm(ks[3], (DEPTH, D_MODEL, N_IN), D_MODEL ** -0.5),
        "conv_w": nrm(ks[4], (DEPTH, CONV_K, A_CONV_CH), CONV_K ** -0.5),
        "a_log": jnp.log(jax.random.uniform(ks[5], (DEPTH, A_HEADS), f32, 1.0, 16.0)),
        "dt_bias": dt + jnp.log(-jnp.expm1(-dt)),
        "head_norm": gain(ks[7], (DEPTH, A_DV)),
        "w_a_out": nrm(ks[8], (DEPTH, A_VW, D_MODEL), A_VW ** -0.5),
        "w_b_out": nrm(ks[9], (DEPTH, B_W, D_MODEL), B_W ** -0.5),
        "rel_bias": nrm(ks[10], (B_HEADS, N_REL), 0.5),
        "w_o": nrm(ks[11], (DEPTH, D_MODEL, D_MODEL), D_MODEL ** -0.5),
        "norm_xattn": gain(ks[12], (DEPTH, D_MODEL)),
        "norm_mem": gain(ks[13], (DEPTH, D_MODEL)),
        "w_mq": nrm(ks[14], (DEPTH, D_MODEL, M_HEADS * M_DH), D_MODEL ** -0.5),
        "w_mkv": nrm(ks[15], (DEPTH, D_MODEL, 2 * M_HEADS * M_DH), D_MODEL ** -0.5),
        "w_mo": nrm(ks[16], (DEPTH, M_HEADS * M_DH, D_MODEL), (M_HEADS * M_DH) ** -0.5),
        "norm_ffn": gain(ks[17], (DEPTH, D_MODEL)),
        "w_gate_up": nrm(ks[18], (DEPTH, D_MODEL, 2 * D_FF_2), D_MODEL ** -0.5),
        "w_down": nrm(ks[19], (DEPTH, D_FF_2, D_MODEL), D_FF_2 ** -0.5),
        "norm_final": gain(ks[20], (D_MODEL,)),
    }

def second_block(x, mem, norm_mix, w_in, conv_w, a_log, dt_bias, head_norm, w_a_out, w_b_out,
              rel_bias, w_o, norm_xattn, norm_mem, w_mq, w_mkv, w_mo, norm_ffn, w_gate_up,
              w_down, norm_final):
    b, s, _ = x.shape
    band_bias = _band_bias(rel_bias)
    for l in range(DEPTH):
        h = rmsnorm_2(x, norm_mix[l])
        qa, ka, va, za, alpha, beta, qb, kb, vb, ga, gb = _split_cols(h @ w_in[l], IN_SPLITS)
        qkv = jax.nn.silu(_causal_dwconv(jnp.concatenate([qa, ka, va], axis=-1), conv_w[l]))
        qa, ka, va = _split_cols(qkv, (A_QK, A_QK, A_VW))
        oa = _gated_deltanet(qa, ka, va, alpha, beta, a_log[l], dt_bias[l])
        oa = rmsnorm_2(oa, head_norm[l]) * jax.nn.silu(za.reshape(b, s, A_HEADS, A_DV))
        oa = oa.reshape(b, s, A_VW)
        ob = _chunk_band_attention(qb, kb, vb, band_bias)
        y = jax.nn.sigmoid(ga) * (oa @ w_a_out[l]) + jax.nn.sigmoid(gb) * (ob @ w_b_out[l])
        x = x + y @ w_o[l]
        x = x + _memory_xattn(rmsnorm_2(x, norm_xattn[l]), rmsnorm_2(mem, norm_mem[l]),
                              w_mq[l], w_mkv[l], w_mo[l])
        gate, up = _split_cols(rmsnorm_2(x, norm_ffn[l]) @ w_gate_up[l], (D_FF_2, D_FF_2))
        x = x + (jax.nn.silu(gate) * up) @ w_down[l]
    return rmsnorm_2(x, norm_final)


def setup_inputs(seed=0):
    out = dict(first_inputs(seed))
    for name, value in second_inputs(seed + 1).items():
        if name != "x":
            out[name + "_2"] = value
    return out


def reference(
    x, c, ctx, c_ctx, ada_w, ada_b, norm1_g, norm2_g, w_in, b_gate, w_fourier, q_norm_g, w_qb,
    kv_norm_g, w_kvb, q_gain, k_gain, w_mla_o, w_out, w_up, w_down, mem_2, norm_mix_2, w_in_2,
    conv_w_2, a_log_2, dt_bias_2, head_norm_2, w_a_out_2, w_b_out_2, rel_bias_2, w_o_2,
    norm_xattn_2, norm_mem_2, w_mq_2, w_mkv_2, w_mo_2, norm_ffn_2, w_gate_up_2, w_down_2,
    norm_final_2,
):
    x = first_block(
        x, c, ctx, c_ctx, ada_w, ada_b, norm1_g, norm2_g, w_in, b_gate, w_fourier, q_norm_g,
        w_qb, kv_norm_g, w_kvb, q_gain, k_gain, w_mla_o, w_out, w_up, w_down,
    )
    return second_block(
        x, mem_2, norm_mix_2, w_in_2, conv_w_2, a_log_2, dt_bias_2, head_norm_2, w_a_out_2,
        w_b_out_2, rel_bias_2, w_o_2, norm_xattn_2, norm_mem_2, w_mq_2, w_mkv_2, w_mo_2,
        norm_ffn_2, w_gate_up_2, w_down_2, norm_final_2,
    )


_drawn_inputs = setup_inputs


def setup_inputs(seed=0):
    import zlib

    import numpy as np

    out = dict(_drawn_inputs(seed))
    spreads = {}
    factors = {'ctx': 8.0,
     'c_ctx': 3.206,
     'norm1_g': 6.659,
     'b_gate': 8.0,
     'q_norm_g': 8.0,
     'w_qb': 3.071,
     'kv_norm_g': 8.0,
     'q_gain': 8.0,
     'k_gain': 8.0,
     'norm_mix_2': 5.316,
     'head_norm_2': 8.0,
     'norm_xattn_2': 8.0,
     'norm_mem_2': 8.0,
     'norm_ffn_2': 16.367,
     'norm_final_2': 7.992}
    for name, (base, spread) in spreads.items():
        noise = np.random.default_rng([zlib.crc32(name.encode()), seed]).standard_normal(out[name].shape)
        drawn = base * np.exp(spread * noise) if base else spread * noise
        out[name] = __import__('jax').numpy.asarray(drawn.astype(out[name].dtype))
    for name, factor in factors.items():
        out[name] = (out[name] * factor).astype(out[name].dtype)
    return out
```

```python
import math

import numpy as np

import concourse.bass as bass
from concourse import mybir

F32 = mybir.dt.float32
F32R = mybir.dt.float32r
U32 = mybir.dt.uint32
ACT = mybir.ActivationFunctionType
ALU = mybir.AluOpType
AX = mybir.AxisListType

P = 128
D = 1024
KT = D // P
S = 512
NT = S // P
C = 256
EPS = 1e-6
FOUR_W, Q_LORA, KV_LORA, ROPE_W = 512, 256, 128, 32
GATE1_COL = FOUR_W + Q_LORA + KV_LORA + ROPE_W
H1, NOPE, QK1, V1 = 8, 64, 96, 64
D_FF = 4 * D
CHUNK, N_CHUNKS = 64, 8
HA = 8
HB, DB = 16, 64
HM = 4
FF2 = 2816
MAX_REL = 256
COL_AB = 4 * D
COL_BAND = 4 * D + 16
COL_GATE2 = COL_BAND + 3 * D

VEC_ROWS = [("norm1_g", 8), ("norm2_g", 8), ("ada_b", 48), ("b_gate", 16), ("q_norm_g", 2), ("kv_norm_g", 1),
            ("norm_mix_2", 8), ("head_norm_2", 1), ("norm_xattn_2", 8), ("norm_mem_2", 8), ("norm_ffn_2", 8),
            ("norm_final_2", 8), ("c", 8), ("c_ctx", 8), ("conv_w_2", 96)]
VEC_SPLIT = 124
VEC_AT, _n = {}, 0
for _name, _rows in VEC_ROWS:
    VEC_AT[_name] = _n
    _n += _rows
VEC_N = _n

CONST_AT, CONST_N = {}, 0
for _name, _cols in [("ident", P), ("ones", P), ("tri", P), ("same", P), ("incl", P)]:
    CONST_AT[_name] = CONST_N
    CONST_N += _cols
LEVELS = 6


def shape_constants():
    i = np.arange(P)
    same = (i[:, None] // CHUNK) == (i[None, :] // CHUNK)
    cols = {"ident": np.eye(P), "ones": np.ones((P, P)), "tri": same & (i[:, None] <= i[None, :]), "same": same,
            "incl": same & (i[:, None] >= i[None, :])}
    const = np.concatenate([np.asarray(cols[n], np.float32) for n in CONST_AT], axis=1)
    masks = []
    for s in range(LEVELS):
        b = i >> s
        low = (b[:, None] % 2 == 1) & (b[None, :] == b[:, None] - 1)
        masks += [low, low.T]
    masks = np.stack(masks, axis=1).astype(np.uint32).reshape(P, 2 * LEVELS * P)
    n, c = np.arange(S), np.arange(P)
    norm = 1.0 / math.sqrt(S * P)
    an, ac = 2 * np.pi * ((n[:, None] * n[None, :]) % S) / S, 2 * np.pi * ((c[:, None] * c[None, :]) % P) / P
    dft_n = np.stack([np.cos(an), -np.sin(an)], axis=0).reshape(2, NT, P, S).transpose(2, 1, 0, 3)
    dft_c = np.concatenate([np.cos(ac), np.sin(ac)], axis=1) * norm
    dft = np.concatenate([dft_n.reshape(P, -1), dft_c], axis=1).astype(np.float32)
    f = np.float32(10000.0) ** (-np.arange(8, dtype=np.float32) / np.float32(8))
    t = np.arange(S)
    row, col = (t // 64).astype(np.float32)[:, None] * f, (t % 64).astype(np.float32)[:, None] * f
    ang = np.concatenate([row, row, col, col], axis=1).astype(np.float32)
    sign = np.repeat(np.array([-1, 1, -1, 1], np.float32), 8)
    rope = np.stack([np.cos(ang), np.sin(ang) * sign], axis=1)
    rope = rope.reshape(NT, P, 2, ROPE_W).transpose(1, 0, 2, 3).reshape(P, -1).astype(np.float32)
    return {"const": const, "masks": masks, "dft": dft, "rope": rope}


def build(nc, t, out):
    at = [(nc.sbuf_base + 63) // 64 * 64]
    END = nc.sbuf_usable_end

    def fixed(name, shape, dt=F32):
        x = nc.alloc_sbuf_tensor_at(name, list(shape), dt, offset=at[0])
        at[0] += (int(np.prod(shape[1:])) * 4 + 31) // 32 * 32
        return x

    UNIT = 2048
    raw = fixed("raw", [P, 2, UNIT])
    w_hi = fixed("w_hi", [P, 2, UNIT], F32R)
    w_lo = fixed("w_lo", [P, 2, UNIT], F32R)
    xT = fixed("xT", [P, KT, S])
    h_hi = fixed("h_hi", [P, KT, S], F32R)
    h_lo = fixed("h_lo", [P, KT, S], F32R)
    const = fixed("const", [P, CONST_N])
    vecT = fixed("vecT", [P, VEC_N])
    mod = fixed("mod", [P, 48, 2])
    silu_c = fixed("silu_c", [P, KT, 2])
    bc = fixed("bc", [P, 2 * QK1 + 2 * HA])
    scl = fixed("scl", [P, 3, KT])
    one_eps = fixed("one_eps", [P, 8])
    stat = fixed("stat", [P, 2, 2, NT])
    lat_stat = fixed("lat_stat", [P, 2, 10])
    qk_stat = fixed("qk_stat", [P, 2, 3, H1])
    at_stat = fixed("at_stat", [P, 4, 4])
    o_stat = fixed("o_stat", [P, 3, 8])
    sq2 = fixed("sq2", [P, 2, S])
    acc = fixed("acc", [P, S])
    tmp2 = fixed("tmp2", [P, 2, S])
    BASE = at[0]

    class Region:

        def __init__(self, start=0):
            self.at = BASE + start

        def __call__(self, name, shape, dt=F32):
            x = nc.alloc_sbuf_tensor_at(name, list(shape), dt, offset=self.at)
            self.at += (int(np.prod(shape[1:])) * 4 + 31) // 32 * 32
            return x

        def over(self, name, shape, offset, dt=F32):
            return nc.alloc_sbuf_tensor_at(name, list(shape), dt, offset=offset)

    r = Region()
    x_in = r("x_in", [P, NT, D])
    c_in = r("c_in", [P, 2, D])
    cT = r("cT", [P, KT, C])
    c_hi = r("c_hi", [P, KT, C], F32R)
    c_lo = r("c_lo", [P, KT, C], F32R)
    vec_in = r("vec_in", [P, 2, P])
    ada_row = r("ada_row", [2, 2, 256])
    r = Region()
    qT = r("qT", [QK1, H1, S])
    kT = r("kT", [QK1, H1, S + C])
    v1 = r("v1", [P, 6, H1 * V1])
    r = Region(60 * 1024)
    lat_q = r("lat_q", [P, 2, S])
    lat_kv = r("lat_kv", [P, S + C])
    kr_T = r("kr_T", [ROPE_W, S + C])
    sq_q = r("sq_q", [P, 2, S])
    sq_kv = r("sq_kv", [P, S + C])
    kr_tok = r("kr_tok", [P, 6, ROPE_W])
    rope = r("rope", [P, NT, 2, ROPE_W])
    qk_tok = r("qk_tok", [P, 2, H1, QK1])
    w_qb = r("w_qb", [P, 2, H1 * QK1])
    w_kvb = r("w_kvb", [P, 1024])
    r = Region(60 * 1024)
    at_hi = r("at_hi", [P, 4, S], F32R)
    at_lo = r("at_lo", [P, 4, S], F32R)
    prob1 = r("prob1", [P, 2, S + C])
    probT1 = r("probT1", [P, 2, S + C])
    r = Region()
    f_T = r("f_T", [P, 4, S])
    f_c = r("f_c", [P, 4, NT, 2 * P])
    dft = r("dft", [P, NT * 2 * S + 2 * P])
    r = Region(76 * 1024)
    fm_hi = r("fm_hi", [P, 4, S], F32R)
    fm_lo = r("fm_lo", [P, 4, S], F32R)
    r = Region()
    sig1 = r("sig1", [P, 2, 4, S])
    y_part = r("y_part", [P, 2, S])
    y_hi = r("y_hi", [P, KT, S], F32R)
    y_lo = r("y_lo", [P, KT, S], F32R)
    r = Region()
    g_hi = r("g_hi", [P, KT, S], F32R)
    g_lo = r("g_lo", [P, KT, S], F32R)
    relu = r("relu", [P, 2, S])
    rsq = r("rsq", [P, 2, S])
    r = Region()
    oaT = r("oaT", [P, HA, S])
    masks = r("masks", [P, 2 * LEVELS, P], U32)
    pad_in = r("pad_in", [P, 6, S + 4])
    conv_at = r.at
    conv = r("conv", [P, 6, S])
    z_s = r("z_s", [P, 2, S])
    ab_T = r("ab_T", [16, S])
    gp = r("gp", [P, 12, NT, HA])
    k_dec = r("k_dec", [P, 2, NT, P])
    k_bg = r("k_bg", [P, 2, NT, P])
    v_b = r("v_b", [P, 2, NT, P])
    eGb = r("eGb", [P, 2, S])
    decay_at = r.at
    decay = r("decay", [P, 2, NT, P])
    q_dec = r("q_dec", [P, 2, S])
    nL_at = r.at
    nL = r("nL", [P, 2, NT, P])
    pr_at = r.at
    pr = r("pr", [P, 2, NT, P])
    nLT = r("nLT", [P, 2, NT, P])
    prT = r("prT", [P, 2, NT, P])
    u_new = r("u_new", [P, 2, P])
    state = r("state", [P, 2, P])
    inv = r.over("inv", [P, 2, NT, P], conv_at)
    invT = r.over("invT", [P, 2, NT, P], conv_at + 4 * 1024)
    prod = r.over("prod", [P, 2, NT, P], conv_at + 8 * 1024)
    u0 = r.over("u0", [P, 2, NT, P], nL_at)
    wT = r.over("wT", [P, 2, S], pr_at)
    o_tok = r.over("o_tok", [P, 2, NT, P], decay_at)
    r = Region()
    r("_oaT", [P, HA, S])
    y2 = r("y2", [P, KT, S])
    ob_at = r.at
    oa_hi = r("oa_hi", [P, HA, S], F32R)
    oa_lo = r("oa_lo", [P, HA, S], F32R)
    sig2 = r("sig2", [P, 2, 2, S])
    ob_hi = r.over("ob_hi", [P, KT, S], ob_at, F32R)
    ob_lo = r.over("ob_lo", [P, KT, S], ob_at + 16 * 1024, F32R)
    qbT = r.over("qbT", [P, 4, S], BASE)
    kbT = r.over("kbT", [P, 4, S], BASE + 8 * 1024)
    r = Region(ob_at - BASE + 32 * 1024)
    vbT = r("vbT", [P, 4, S])
    vb = r("vb", [P, NT, S])
    score_b = r("score_b", [P, 2, S])
    bias_b = r("bias_b", [P, 2, S])
    prob_b = r.over("prob_b", [P, 2, S], r.at)
    r.at += 4 * 1024
    probT_b = r("probT_b", [P, 2, S])
    r = Region()
    r("_y", [P, KT, S])
    m_q = r("m_q", [P, KT, S])
    m_kT = r("m_kT", [P, KT, C])
    m_vT = r("m_vT", [P, KT, C])
    m_v = r("m_v", [P, 2, D])
    om_hi = r("om_hi", [P, KT, S], F32R)
    om_lo = r("om_lo", [P, KT, S], F32R)
    m_in = r.over("m_in", [P, 2, D], BASE + 56 * 1024)
    m_T = r.over("m_T", [P, KT, C], BASE + 64 * 1024)
    m_hi = r.over("m_hi", [P, KT, C], BASE, F32R)
    m_lo = r.over("m_lo", [P, KT, C], BASE + 8 * 1024, F32R)
    prob_m = r.over("prob_m", [P, 2, C], BASE)
    probT_m = r.over("probT_m", [P, 2, C], BASE + 2 * 1024)
    r = Region()
    s_hi = r("s_hi", [P, 22, S], F32R)
    s_lo = r("s_lo", [P, 22, S], F32R)
    gate = r("gate", [P, 2, S])
    gu = r("gu", [P, 2, S])
    r = Region()
    yT = r("yT", [P, KT, S])
    y_out = r("y_out", [P, NT, D])

    ps = nc.alloc_psum_tensor("ps", [P, 8, 512], F32)

    def col(name, k=0):
        return vecT[:, VEC_AT[name] + k:VEC_AT[name] + k + 1]

    def con(name):
        return const[:, CONST_AT[name]:CONST_AT[name] + P]

    def over_tiles(m):
        return m.unsqueeze(1).broadcast_to([P, NT, P])

    def over_width(m, w=P):
        return m.unsqueeze(2).broadcast_to([m.shape[0], m.shape[1], w])

    class Unit:
        def __init__(self, kind, loads, tiles, split=True, n=UNIT):
            self.kind, self.loads, self.tiles, self.split, self.n = kind, loads, tiles, split, n

    units, first = [], {}

    def block(w, r0, kt, c0, cols):
        return w[r0:r0 + kt * P, c0:c0 + cols].rearrange("(k p) c -> p k c", p=P)

    def add(phase, kind, loads, tiles, split=True):
        first.setdefault(phase, len(units))
        n = max(o + k * c for (_, o, k, c) in loads)
        units.append(Unit(kind, loads, tiles, split, n))

    def wide(phase, kind, w, r0, c0, tiles=2, split=True):
        add(phase, kind, [(block(w, r0, KT, c0, 256), 0, KT, 256)], tiles, split)

    for j in range(8):
        wide("ada_a", "ada", t["ada_w"], 0, 256 * j, 0, False)
    wide("lat", "q", t["w_in"], 0, FOUR_W, 2)
    wide("lat", "kv", t["w_in"], 0, FOUR_W + Q_LORA, 4)
    for j in range(8, 24):
        wide("ada_b", "ada", t["ada_w"], 0, 256 * j, 0, False)
    for j in range(2):
        wide("f", "f", t["w_in"], 0, 256 * j)
    for j in range(4):
        wide("merge1", "gf", t["w_in"], 0, GATE1_COL + 256 * j)
        wide("merge1", "ga", t["w_in"], 0, GATE1_COL + D + 256 * j)
        add("merge1", "wfa", [(block(t["w_fourier"], 0, 4, 256 * j, 256), 0, 4, 256),
                              (block(t["w_mla_o"], 0, 4, 256 * j, 256), 1024, 4, 256)], 4)
    for j in range(4):
        wide("out1", "out", t["w_out"], 0, 256 * j)
    for c in range(4):
        for j in range(4):
            wide("mlp", "up", t["w_up"], 0, D * c + 256 * j)
        for j in range(4):
            wide("mlp", "down", t["w_down"], D * c, 256 * j)
    add("ab", "ab", [(block(t["w_in_2"], 0, KT, COL_AB, P), 0, KT, P)], 1)
    for p in range(4):
        for kind in range(4):
            wide(f"pair{p}", "qkvz"[kind], t["w_in_2"], 0, D * kind + 256 * p)
    for j in range(4):
        wide("aout", "sig", t["w_in_2"], 0, COL_GATE2 + 256 * j)
        wide("aout", "proj", t["w_a_out_2"], 0, 256 * j)
    for g in range(2):
        for kind in range(3):
            for j in range(2):
                wide(f"band{g}", "qkv"[kind], t["w_in_2"], 0, COL_BAND + D * kind + 512 * g + 256 * j)
    for j in range(4):
        wide("bout", "sig", t["w_in_2"], 0, COL_GATE2 + D + 256 * j)
        wide("bout", "proj", t["w_b_out_2"], 0, 256 * j)
    for j in range(4):
        wide("out2", "out", t["w_o_2"], 0, 256 * j)
    for j in range(4):
        wide("mq", "mq", t["w_mq_2"], 0, 256 * j)
    for j in range(8):
        wide("mkv", "mkv", t["w_mkv_2"], 0, 256 * j)
    for j in range(4):
        wide("mo", "out", t["w_mo_2"], 0, 256 * j)
    for j in range(11):
        wide("gu", "gate", t["w_gate_up_2"], 0, 256 * j)
        wide("gu", "up", t["w_gate_up_2"], 0, FF2 + 256 * j)
    for j in range(11):
        add("down2", "down2", [(block(t["w_down_2"], 256 * j, 2, 0, D), 0, 2, D)], 0)
    NU = len(units)
    split_at, tile_at, load_count, raw_used_count = [], [], [], []
    n_split = n_tile = 0
    per_slot = [0, 0]
    for u, x in enumerate(units):
        split_at.append(n_split)
        tile_at.append(n_tile)
        n_split += x.split
        n_tile += x.tiles
        per_slot[u % 2] += 16 * len(x.loads)
        load_count.append(per_slot[u % 2])
        raw_used_count.append(u // 2 + 1)
    split_at.append(n_split)
    tile_at.append(n_tile)

    def val(table, u, loop=None):
        if loop is None:
            return table[u]
        i, stride = loop
        return i * (table[u + stride] - table[u]) + table[u]

    names = """tile_done w_mm_done w_lo_done ada_mm in_done at_out dft_in masks_in at_max m_in_done y_copied y_copied2
    stored w_hi_done bias_ready act_chain n_acc n_sq n_sum n_std n_t n_hi const_done x_in_done c_in_done bc_done
    rope_done wq_done wkv_done vec_done c_silu xt_done ctx_tr ctx_t ada_tr ada_rowed one_eps_done lat_sq lat_ss
    lat_std kr_mm kr_copied qk_scaled v_scaled qk_summed qk_squared qk_turned qk_stored qk_std at_turned at_exp
    at_copied at_out_hi fm_mm fm_hi_done y_t_done y_hi_done rsq_done g_hi_done gate_dve gate_act c_pad c_conv
    o_done c_silued c_sq Gb_mm Gb_exp d_diff d_exp nL_turned nLT_done lv_m1 lv_copied uw_mm uw_copied r_su r_oc
    o_sq o_std oa_hi_done m_tr m_T_done s_hi_done x_last y_turned dve_chain n_inv n_bc n_lo vec_tr tr_done
    ada_mod lat_gained lat_inv qk_mm qk_normed scl2_done at_scores at_prob at_out_lo fc_mm fc_copied fm_lo_done
    y_lo_done g_lo_done ab_turned gate_cum c_normed kv_turned k_scaled qd_done kk_mm nL_done inv0_done lv_mm
    lv_done r_init r_ws r_u r_st o_scaled o_turned oa_lo_done vb_turned vb_copied mv_turned mv_copied s_lo_done""".split()
    sem = {n: nc.alloc_semaphore(n) for n in names}
    bias_in = [nc.alloc_semaphore(f"bias_in{i}") for i in range(2)]
    w_in_slot = [nc.alloc_semaphore(f"w_in_slot{i}") for i in range(2)]
    bank_stored = [nc.alloc_semaphore(f"bank_stored{i}") for i in range(4)]

    def tile_count(u, j, loop=None):
        return val([x + j + 1 for x in tile_at], u, loop)

    def bank_of(u, j):
        return (tile_at[u] + j) % 4

    def bank(u, j):
        return ps[:, bank_of(u, j), :]

    def stored_count(u, j, loop=None):
        return val([(x + j) // 4 + 1 for x in tile_at], u, loop)

    def slot_before(u):
        old = [x for x in range(u) if units[x].split][-2:]
        return old[0] if len(old) == 2 else None

    def w_slot(x, u):
        return x[:, split_at[u] % 2, 0:units[u].n]

    N_X, N_CTX, N_2, N_MIX = 0, 1, 2, 3
    N_XATTN, N_MEM, N_FFN, N_FINAL = 20, 21, 22, 23
    NORM_INDEX = {N_X: 0, N_CTX: 1, N_2: 2, N_MIX: 3, N_XATTN: 4, N_MEM: 5, N_FFN: 6, N_FINAL: 7}
    SUM_BANK, BC_BANK = 4, 6

    MLP_ROUNDS = [(0, None), (1, 3)]

    items = [("one", h, q) for h in range(H1) for q in range(NT)]
    items += [("band", h, q) for h in range(HB) for q in range(NT)]
    items += [("mem", h, q) for h in range(HM) for q in range(NT)]
    ITEM = {x: n for n, x in enumerate(items)}
    ATT = {"one": (0, 32), "band0": (32, 64), "band1": (64, 96), "mem": (96, 112)}

    def keys_of(n):
        kind, h, q = items[n]
        return {"one": S + C, "band": (q + 1) * P, "mem": C}[kind]

    def out_group(n):
        if n < 96:
            return n // 8, n % 8 == 7
        return 12 + (n - 96) // 4, n % 4 == 3

    def out_tiles_before(n):
        return n // 8 if n < 96 else 12 + 2 * ((n - 96) // 4)

    rot = acc[:, 0:H1 * ROPE_W].rearrange("p (h a b c) -> p h a b c", h=H1, a=2, b=2)
    last_of = {}
    for name in first:
        later = [x for x in first.values() if x > first[name]]
        last_of[name] = min(later) if later else NU

    def ada_unit(a):
        return first["ada_a"] + a if a < 8 else first["ada_b"] + a - 8

    def ada_after(m):
        return min(24, 8 + 2 * (m + 1))

    def ada_row(a):
        return tmp2[0:2, a % 2, 0:256]

    qk_sq = sq2[:, :, :].rearrange("p a c -> p (a c)")[:, 0:H1 * QK1]

    def ada_count(u):
        return u - first["ada_a"] + 1 if u < first["lat"] else 8 + u - first["ada_b"] + 1

    with nc.Block() as block:
        @block.sync
        def _(sp):
            def wait_raw_slot(u, loop=None):
                if u < 2:
                    return
                if units[u - 2].split:
                    sp.wait_ge(sem["w_lo_done"], val(split_at, u - 2, loop) + 1)
                else:
                    sp.wait_ge(sem["ada_mm"], ada_count(u - 2))

            def load(u, loop=None, src=None):
                wait_raw_slot(u, loop)
                for got, off, k, c in units[u].loads:
                    dst = raw[:, u % 2, off:off + k * c].rearrange("p (k c) -> p k c", c=c)
                    sp.dma_start(dst, got if src is None else src).then_inc(w_in_slot[u % 2], 16)

            def load_phase(name):
                for u in range(first[name], last_of[name]):
                    load(u)

            sp.dma_start(vec_in[0:VEC_SPLIT, 0, :], t["vec"][0:VEC_SPLIT, :]).then_inc(sem["in_done"], 16)
            sp.dma_start(vec_in[0:VEC_N - VEC_SPLIT, 1, :], t["vec"][VEC_SPLIT:, :]).then_inc(sem["in_done"], 16)
            for name in ("ada_a", "lat", "ada_b", "f"):
                load_phase(name)
            sp.wait_ge(sem["at_out"], 32)
            sp.dma_start(dft[:, :], t["dft"]).then_inc(sem["dft_in"], 16)
            load_phase("merge1")
            load_phase("out1")
            u0_ = first["mlp"]
            for j in range(8):
                load(u0_ + j)
            with sp.Fori(0, 3) as i:
                for j in range(4):
                    load(u0_ + 8 + j, (i, 8), t["w_up"][:, bass.ds(i * D + (D + 256 * j), 256)]
                         .rearrange("(k p) c -> p k c", p=P))
                for j in range(4):
                    load(u0_ + 12 + j, (i, 8), t["w_down"][bass.ds(i * D + D, D), 256 * j:256 * j + 256]
                         .rearrange("(k p) c -> p k c", p=P))
            load_phase("ab")
            sp.wait_ge(bank_stored[bank_of(first["mlp"] + 31, 1)], stored_count(first["mlp"] + 31, 1))
            sp.dma_start(masks[:, :, :], t["masks"].rearrange("p (m c) -> p m c", c=P)).then_inc(sem["masks_in"], 16)
            for p in range(4):
                load_phase(f"pair{p}")
            load_phase("aout")
            for g in range(2):
                for u in range(first[f"band{g}"] + 2 * g, last_of[f"band{g}"]):
                    load(u)
                for u in range(last_of[f"band{g}"], last_of[f"band{g}"] + 2):
                    load(u)
                for h in range(8 * g, 8 * g + 8):
                    if h >= 2:
                        sp.wait_ge(sem["at_max"], ITEM[("band", h - 2, NT - 1)] + 1)
                    else:
                        sp.wait_ge(bank_stored[bank_of(first["aout"] + 7, 1)], stored_count(first["aout"] + 7, 1))
                    sp.dma_start(bias_b[:, h % 2, :], t["bias_band"][h]).then_inc(bias_in[h % 2], 16)
            for u in range(first["bout"] + 2, last_of["bout"]):
                load(u)
            load_phase("out2")
            sp.wait_ge(sem["tile_done"], tile_count(first["bout"] + 7, 1))
            sp.dma_start(m_in[:, :, :], t["mem_2"].rearrange("(a p) c -> p a c", p=P)).then_inc(sem["m_in_done"], 16)
            for name in ("mq", "mkv", "mo"):
                load_phase(name)
            u0_ = first["gu"]
            for j in range(2):
                load(u0_ + j)
            with sp.Fori(0, 10) as i:
                for j in range(2):
                    load(u0_ + 2 + j, (i, 2), t["w_gate_up_2"][:, bass.ds(i * 256 + (256 + FF2 * j), 256)]
                         .rearrange("(k p) c -> p k c", p=P))
            u0_ = first["down2"]
            load(u0_)
            with sp.Fori(0, 5) as i:
                for j in range(2):
                    load(u0_ + 1 + j, (i, 2), t["w_down_2"][bass.ds(i * 512 + (256 + 256 * j), 256), :]
                         .rearrange("(k p) c -> p k c", p=P))
            for q in range(NT):
                sp.wait_ge(sem["y_copied"], q + 1)
                sp.wait_ge(sem["y_copied2"], q + 1)
                sp.dma_start(out[q * P:(q + 1) * P, :], y_out[:, q, :]).then_inc(sem["stored"], 16)
            sp.wait_ge(sem["stored"], 16 * NT)

        @block.gpsimd
        def _(pool):
            def lower(u, loop=None):
                pool.wait_ge(sem["w_hi_done"], val(split_at, u, loop) + 1)
                n = UNIT if loop else units[u].n
                nc.gpsimd.tensor_tensor(w_lo[:, split_at[u] % 2, 0:n], raw[:, u % 2, 0:n],
                                        w_hi[:, split_at[u] % 2, 0:n].bitcast(F32),
                                        ALU.subtract).then_inc(sem["w_lo_done"], 1)

            u = 0
            while u < NU:
                if u == first["mlp"] + 8:
                    with pool.Fori(0, 3) as i:
                        for j in range(8):
                            lower(u + j, (i, 8))
                    u += 24
                    continue
                if u == first["gu"] + 2:
                    with pool.Fori(0, 10) as i:
                        for j in range(2):
                            lower(u + j, (i, 2))
                    u += 20
                    continue
                if u == first["down2"] + 1:
                    with pool.Fori(0, 5) as i:
                        for j in range(2):
                            lower(u + j, (i, 2))
                    u += 10
                    continue
                if units[u].split:
                    lower(u)
                if u in (last_of["band0"] + 1, last_of["band1"] + 1):
                    g = int(u > last_of["band1"])
                    for h in range(8 * g, 8 * g + 8):
                        pool.wait_ge(bias_in[h % 2], 16 * (h // 2 + 1))
                        nc.gpsimd.memset(bias_b[0:CHUNK, h % 2, S - CHUNK:S], -1e30).then_inc(sem["bias_ready"], 1)
                u += 1

        @block.scalar
        def _(act):
            split_units = [u for u in range(NU) if units[u].split]
            turn = [0]

            def hi_of(u, loop=None):
                act.wait_ge(w_in_slot[u % 2], val(load_count, u, loop))
                old = slot_before(u)
                if old is not None and units[old].kind == "down2":
                    act.wait_ge(sem["w_mm_done"], old - first["down2"] + 1)
                elif old is not None:
                    act.wait_ge(sem["tile_done"], val(tile_at, old + 1, loop))
                n = UNIT if loop else units[u].n
                nc.scalar.activation(w_hi[:, split_at[u] % 2, 0:n], raw[:, u % 2, 0:n],
                                     ACT.Copy).then_inc(sem["w_hi_done"], 1)

            def next_hi():
                if turn[0] < len(split_units):
                    hi_of(split_units[turn[0]])
                    turn[0] += 1

            def link(ins):
                ins.then_inc(sem["act_chain"], 1)
                chain[0] += 1
                act.wait_ge(sem["act_chain"], chain[0])

            chain = [0]

            def store_tile(u, j, dst, func=ACT.Copy, rows=P, cols=S, loop=None, **kw):
                act.wait_ge(sem["tile_done"], tile_count(u, j, loop))
                p = bank(u, j)
                nc.scalar.activation(dst, p[0:rows, 0:cols], func, **kw).then_inc(bank_stored[bank_of(u, j)], 1)

            def squares(n, k, src):
                i = NORM_INDEX[n]
                before = 7 * i + (max(1, k - 2) if k >= 2 else 0)
                if before:
                    act.wait_ge(sem["n_acc"], before)
                nc.scalar.activation(sq2[:, k % 2, 0:src.shape[1]], src, ACT.Square).then_inc(sem["n_sq"], 1)

            def std_of(g, scale, nt=NT):
                act.wait_ge(sem["n_sum"], g + 1)
                nc.scalar.activation(stat[:, g % 2, 0, 0:nt], ps[:, SUM_BANK + g % 2, 0:nt * P:P], ACT.Sqrt,
                                     bias=one_eps[:, 0:1], scale=scale).then_inc(sem["n_std"], 1)

            def norm_hi(n, dst, shift):
                i = NORM_INDEX[n]
                for k in range(KT):
                    act.wait_ge(sem["n_t"], 8 * i + k + 1)
                    w = dst.shape[2]
                    if shift is None:
                        nc.scalar.activation(dst[:, k, :], tmp2[:, k % 2, 0:w], ACT.Copy).then_inc(sem["n_hi"], 1)
                    else:
                        nc.scalar.activation(dst[:, k, :], tmp2[:, k % 2, 0:w], ACT.Identity,
                                             bias=shift(k)).then_inc(sem["n_hi"], 1)

            act.dma_start(const[:, :], t["const"]).then_inc(sem["const_done"], 16)
            act.dma_start(x_in[:, :, :], t["x"].rearrange("(a p) c -> p a c", p=P)).then_inc(sem["x_in_done"], 16)
            act.dma_start(c_in[:, :, :], t["ctx"].rearrange("(a p) c -> p a c", p=P)).then_inc(sem["c_in_done"], 16)
            act.dma_start(bc[:, :], t["bc"]).then_inc(sem["bc_done"], 16)
            act.dma_start(rope[:, :, :, :].rearrange("p a b c -> p (a b c)"), t["rope"]).then_inc(sem["rope_done"], 16)
            act.dma_start(w_qb[:, :, :], t["w_qb"].rearrange("(k p) c -> p k c", p=P)).then_inc(sem["wq_done"], 16)
            act.dma_start(w_kvb[:, :], t["w_kvb"]).then_inc(sem["wkv_done"], 16)
            act.wait_ge(sem["vec_done"], 1)
            for i, name in enumerate(("c", "c_ctx")):
                nc.scalar.activation(silu_c[:, :, i], vecT[:, VEC_AT[name]:VEC_AT[name] + KT], ACT.Silu).then_inc(sem["c_silu"], 1)
            for k in range(KT):
                act.wait_ge(sem["xt_done"], k + 1)
                squares(N_X, k, xT[:, k, :])
            for k in range(KT):
                act.wait_ge(sem["ctx_tr"], k + 1)
                nc.scalar.activation(cT[:, k, :], ps[:, 4 + k % 4, 0:C], ACT.Copy).then_inc(sem["ctx_t"], 1)
            for k in range(KT):
                act.wait_ge(sem["ctx_t"], k + 1)
                squares(N_CTX, k, cT[:, k, :])

            def ada_rows(a):
                act.wait_ge(sem["ada_mm"], a + 1)
                if a >= 2:
                    act.wait_ge(sem["ada_tr"], a - 1)
                nc.scalar.activation(ada_row(a), ps[0:2, a % 2, 0:256], ACT.Copy).then_inc(sem["ada_rowed"], 1)

            for a in range(8):
                ada_rows(a)
                if a == 2:
                    act.wait_ge(sem["one_eps_done"], 1)
                    std_of(N_X, 1.0 / D)
                if a == 3:
                    std_of(N_CTX, 1.0 / D, 2)
            next_hi()
            next_hi()
            norm_hi(N_X, h_hi, lambda k: mod[:, k, 0:1])
            norm_hi(N_CTX, c_hi, lambda k: mod[:, k, 1:2])

            u = first["lat"]
            for j in range(2):
                store_tile(u, j, lat_q[:, j, :])
            store_tile(u + 1, 0, lat_kv[:, 0:S])
            store_tile(u + 1, 1, kr_T[:, 0:S], rows=ROPE_W)
            store_tile(u + 1, 2, lat_kv[:, S:S + C], cols=C)
            store_tile(u + 1, 3, kr_T[:, S:S + C], rows=ROPE_W, cols=C)
            for j in range(2):
                act.wait_ge(bank_stored[bank_of(u, j)], stored_count(u, j))
                nc.scalar.activation(sq_q[:, j, :], lat_q[:, j, :], ACT.Square).then_inc(sem["lat_sq"], 1)
            act.wait_ge(bank_stored[bank_of(u + 1, 0)], stored_count(u + 1, 0))
            act.wait_ge(bank_stored[bank_of(u + 1, 2)], stored_count(u + 1, 2))
            nc.scalar.activation(sq_kv[:, :], lat_kv[:, :], ACT.Square).then_inc(sem["lat_sq"], 1)
            act.wait_ge(sem["lat_ss"], 1)
            nc.scalar.activation(lat_stat[:, 0, 0:4], ps[:, 4, 0:4], ACT.Sqrt, bias=one_eps[:, 0:1], scale=1.0 / Q_LORA)
            nc.scalar.activation(lat_stat[:, 0, 4:10], ps[:, 4, 4:10], ACT.Sqrt, bias=one_eps[:, 0:1],
                                 scale=1.0 / KV_LORA).then_inc(sem["lat_std"], 1)
            act.wait_ge(sem["kr_mm"], 1)
            nc.scalar.activation(kr_tok[:, :, :].rearrange("p a c -> p (a c)"), ps[:, 5, 0:6 * ROPE_W],
                                 ACT.Copy).then_inc(sem["kr_copied"], 1)

            def v_and_square(m):
                if m < 6:
                    act.wait_ge(sem["qk_scaled"], m + 1)
                    kv = ps[:, 4:6, :].rearrange("p b (h c) -> p (b h) c", c=P)
                    nc.scalar.activation(v1[:, m, :].rearrange("p (h c) -> p h c", c=V1), kv[:, :, NOPE:P], ACT.Copy,
                                         scale=lat_stat[:, 1, 4 + m:5 + m]).then_inc(sem["v_scaled"], 1)
                act.wait_ge(sem["qk_scaled"], m + 1)
                if m >= 1:
                    act.wait_ge(sem["qk_summed"], m)
                nc.scalar.activation(qk_sq, qk_tok[:, m % 2, :, :].rearrange("p h c -> p (h c)"),
                                     ACT.Square).then_inc(sem["qk_squared"], 1)

            def store_qk(m):
                dst = kT[:, :, m * P:(m + 1) * P] if m < 6 else qT[:, :, (m - 6) * P:(m - 5) * P]
                act.wait_ge(sem["qk_turned"], m + 1)
                nc.scalar.activation(dst, ps[0:QK1, 6:8, :].rearrange("p b (h c) -> p (b h) c", c=P),
                                     ACT.Copy).then_inc(sem["qk_stored"], 1)

            done_ada = 8
            v_and_square(0)
            for m in range(10):
                act.wait_ge(sem["qk_summed"], m + 1)
                nc.scalar.activation(qk_stat[:, m % 2, 1, :], qk_stat[:, m % 2, 0, :], ACT.Sqrt, bias=one_eps[:, 0:1],
                                     scale=1.0 / QK1).then_inc(sem["qk_std"], 1)
                if m < 9:
                    v_and_square(m + 1)
                while done_ada < ada_after(m):
                    ada_rows(done_ada)
                    done_ada += 1
                store_qk(m)

            next_hi()
            next_hi()

            def attention(kind, prob, probT, scale, dst_hi):
                a, b = ATT[kind]

                def expo(n):
                    nk = keys_of(n)
                    src = score_b[:, n % 2, 0:nk] if items[n][0] == "band" else \
                        ps[:, 2 * (n % 2):2 * (n % 2) + 2, :].rearrange("p b c -> p (b c)")[:, 0:nk]
                    act.wait_ge(sem["at_max"], n + 1)
                    if n >= 2:
                        act.wait_ge(sem["at_turned"], n - 1)
                    nc.scalar.activation(prob[:, n % 2, 0:nk], src, ACT.Exp, bias=at_stat[:, n % 4, 1:2], scale=scale,
                                         accum_out=at_stat[:, n % 4, 2:3]).then_inc(sem["at_exp"], 1)

                def copy(n):
                    nk = keys_of(n)
                    act.wait_ge(sem["at_turned"], n + 1)
                    if n >= 2:
                        act.wait_ge(sem["at_out"], n - 1)
                    nc.scalar.activation(probT[:, n % 2, 0:nk],
                                         ps[:, 4:6, :].rearrange("p b c -> p (b c)")[:, 0:nk],
                                         ACT.Copy).then_inc(sem["at_copied"], 1)

                def out_hi(n):
                    g, last = out_group(n)
                    if last:
                        act.wait_ge(sem["at_out"], n + 1)
                        if kind == "mem":
                            for j in range(2):
                                nc.scalar.activation(dst_hi[:, 2 * (g - 12) + j, :], ps[:, 6 + j, :],
                                                     ACT.Copy).then_inc(sem["at_out_hi"], 1)
                        else:
                            nc.scalar.activation(dst_hi[:, g - (4 if kind != "one" else 0), :], ps[:, 6 + g % 2, :],
                                                 ACT.Copy).then_inc(sem["at_out_hi"], 1)

                expo(a)
                for n in range(a, b):
                    if n + 1 < b:
                        expo(n + 1)
                    copy(n)
                    if n > a:
                        out_hi(n - 1)
                out_hi(b - 1)

            attention("one", prob1, probT1, QK1 ** -0.5, at_hi)

            for j in range(2):
                for jj in range(2):
                    store_tile(first["f"] + j, jj, f_T[:, 2 * j + jj, :])
                next_hi()
            for g in range(4):
                act.wait_ge(sem["fm_mm"], g + 1)
                nc.scalar.activation(fm_hi[:, g, :], ps[:, 4 + g, :], ACT.Copy).then_inc(sem["fm_hi_done"], 1)

            for j in range(4):
                u = first["merge1"] + 3 * j
                for part in range(2):
                    for jj in range(2):
                        if j >= 2:
                            act.wait_ge(bank_stored[bank_of(u - 6 + 2, 2 * part + jj)], stored_count(u - 6 + 2, 2 * part + jj))
                        store_tile(u + part, jj, sig1[:, j % 2, 2 * part + jj, :], ACT.Sigmoid,
                                   bias=col("b_gate", 8 * part + 2 * j + jj))
                    next_hi()
                for jj in range(2):
                    act.wait_ge(sem["y_t_done"], 2 * j + jj + 1)
                    nc.scalar.activation(y_hi[:, 2 * j + jj, :], tmp2[:, jj, :], ACT.Copy).then_inc(sem["y_hi_done"], 1)
                next_hi()

            def out_phase(name, n):
                for j in range(4):
                    for jj in range(2):
                        if jj == 0:
                            act.wait_ge(sem["tile_done"], tile_count(first[name] + j, 1))
                            next_hi()
                        act.wait_ge(bank_stored[bank_of(first[name] + j, jj)], stored_count(first[name] + j, jj))
                        squares(n, 2 * j + jj, xT[:, 2 * j + jj, :])

            out_phase("out1", N_2)
            std_of(N_2, 1.0 / D)
            norm_hi(N_2, h_hi, lambda k: mod[:, 24 + k, 0:1])

            def mlp_chunk(u0_, count0, loop=None):
                for j in range(4):
                    for jj in range(2):
                        q = 2 * j + jj
                        if not (isinstance(count0, int) and count0 + q < 2):
                            act.wait_ge(sem["rsq_done"], count0 + (q - 1))
                        store_tile(u0_ + j, jj, relu[:, jj, :], ACT.Relu, loop=loop)
                    for jj in range(2):
                        q = 2 * j + jj
                        act.wait_ge(sem["rsq_done"], count0 + (q + 1))
                        nc.scalar.activation(g_hi[:, q, :], rsq[:, jj, :], ACT.Copy).then_inc(sem["g_hi_done"], 1)
                    hi_of(u0_ + j + 2, loop)
                for j in range(4):
                    act.wait_ge(sem["tile_done"], tile_count(u0_ + 4 + j, 1, loop))
                    hi_of(u0_ + 4 + j + 2, loop)

            mlp_chunk(first["mlp"], 0)
            with act.Fori(0, 3) as i:
                mlp_chunk(first["mlp"] + 8, i * 8 + 8, (i, 8))
            turn[0] = split_units.index(first["pair0"] + 1)
            for k in range(KT):
                act.wait_ge(bank_stored[bank_of(first["mlp"] + 28 + k // 2, k % 2)], stored_count(first["mlp"] + 28 + k // 2, k % 2))
                squares(N_MIX, k, xT[:, k, :])
            std_of(N_MIX, 1.0 / D)
            norm_hi(N_MIX, h_hi, None)

            store_tile(first["ab"], 0, ab_T[:, :], rows=16)
            next_hi()
            act.wait_ge(sem["gate_dve"], 1)
            nc.scalar.activation(gp[:, 6, :, :], gp[:, 9, :, :], ACT.Sigmoid)
            link(nc.scalar.activation(gp[:, 1, :, :], gp[:, 0, :, :], ACT.Abs))
            link(nc.scalar.activation(gp[:, 2, :, :], gp[:, 1, :, :], ACT.Exp, scale=-1.0))
            nc.scalar.activation(gp[:, 3, :, :], gp[:, 2, :, :], ACT.Ln, bias=one_eps[:, 1:2])
            nc.scalar.activation(gp[:, 10, 0, :], bc[:, 2 * QK1 + HA:2 * QK1 + 2 * HA], ACT.Exp).then_inc(sem["gate_act"], 1)
            act.wait_ge(sem["gate_dve"], 3)
            nc.scalar.activation(gp[:, 10, :, :], gp[:, 5, :, :], ACT.Exp)
            nc.scalar.activation(gp[:, 8, :, :], gp[:, 9, :, :], ACT.Exp).then_inc(sem["gate_act"], 1)

            for p in range(4):
                u = first[f"pair{p}"]
                for kind in range(3):
                    for a in range(2):
                        if p == 0:
                            act.wait_ge(sem["c_pad"], 1)
                        else:
                            act.wait_ge(sem["c_conv"], 6 * p)
                        store_tile(u + kind, a, pad_in[:, 2 * kind + a, 3:3 + S])
                    next_hi()
                for a in range(2):
                    if p:
                        act.wait_ge(sem["o_done"], 2 * p)
                    store_tile(u + 3, a, z_s[:, a, :], ACT.Silu)
                next_hi()
                for j in range(6):
                    act.wait_ge(sem["c_conv"], 6 * p + j + 1)
                    nc.scalar.activation(conv[:, j, :], conv[:, j, :], ACT.Silu).then_inc(sem["c_silued"], 1)
                for j in range(4):
                    g = 4 + 4 * p + j
                    act.wait_ge(sem["c_silued"], 6 * p + j + 1)
                    act.wait_ge(sem["n_sum"], g - 1)
                    nc.scalar.activation(sq2[:, j % 2, :], conv[:, j, :], ACT.Square).then_inc(sem["c_sq"], 1)
                    if j:
                        std_of(g - 1, 1.0)
                std_of(7 + 4 * p, 1.0)
                for a in range(2):
                    h = 2 * p + a
                    act.wait_ge(sem["Gb_mm"], h + 1)
                    nc.scalar.activation(eGb[:, a, :], ps[:, 4 + a, :], ACT.Exp).then_inc(sem["Gb_exp"], 1)
                    act.wait_ge(sem["d_diff"], h + 1)
                    nc.scalar.activation(decay[:, a, :, :], decay[:, a, :, :], ACT.Exp, scale=-1.0).then_inc(sem["d_exp"], 1)
                for a in range(2):
                    for i, dst in enumerate((nLT, prT)):
                        act.wait_ge(sem["nL_turned"], 4 * p + 2 * a + i + 1)
                        nc.scalar.activation(dst[:, a, :, :].rearrange("p t c -> p (t c)"), ps[:, (6 if i == 0 else 4) + a, :],
                                             ACT.Copy).then_inc(sem["nLT_done"], 1)
                for s in range(1, LEVELS):
                    for a in range(2):
                        n = (p * 5 + s - 1) * 2 + a
                        act.wait_ge(sem["lv_m1"], n + 1)
                        nc.scalar.activation(prod[:, a, :, :].rearrange("p t c -> p (t c)"), ps[:, 6 + a, :],
                                             ACT.Copy).then_inc(sem["lv_copied"], 1)
                for a in range(2):
                    for i, dst in enumerate((u0[:, a, :, :].rearrange("p t c -> p (t c)"), wT[:, a, :])):
                        act.wait_ge(sem["uw_mm"], 4 * p + 2 * a + i + 1)
                        nc.scalar.activation(dst, ps[:, 4 + 2 * i + a, :], ACT.Copy).then_inc(sem["uw_copied"], 1)
                for tt in range(NT):
                    act.wait_ge(sem["r_su"], 8 * p + 2 * tt + 2)
                    nc.scalar.activation(o_tok[:, :, tt, :], ps[:, 5 + 2 * (tt % 2), 0:2 * P].rearrange("p (a c) -> p a c", a=2),
                                         ACT.Copy).then_inc(sem["r_oc"], 1)
                act.wait_ge(sem["o_sq"], p + 1)
                nc.scalar.activation(o_stat[:, 1, :], o_stat[:, 0, :], ACT.Sqrt, bias=one_eps[:, 0:1],
                                     scale=1.0 / P).then_inc(sem["o_std"], 1)

            for k in range(HA):
                act.wait_ge(sem["o_done"], HA)
                nc.scalar.activation(oa_hi[:, k, :], oaT[:, k, :], ACT.Copy).then_inc(sem["oa_hi_done"], 1)

            def gates2(name, j):
                u = first[name] + 2 * j
                for jj in range(2):
                    if j >= 2:
                        act.wait_ge(bank_stored[bank_of(u - 4 + 1, jj)], stored_count(u - 4 + 1, jj))
                    store_tile(u, jj, sig2[:, j % 2, jj, :], ACT.Sigmoid)
                next_hi()
                act.wait_ge(sem["tile_done"], tile_count(u + 1, 1))
                next_hi()

            for j in range(4):
                gates2("aout", j)

            for g in range(2):
                for kind, dst in enumerate((qbT, kbT, vbT)):
                    for j in range(2):
                        for jj in range(2):
                            store_tile(first[f"band{g}"] + 2 * kind + j, jj, dst[:, 2 * j + jj, :])
                        next_hi()
                attention(f"band{g}", prob_b, probT_b, 1.0, ob_hi)
            for j in range(4):
                gates2("bout", j)
            for k in range(KT):
                act.wait_ge(sem["y_t_done"], 8 + k + 1)
                act.wait_ge(sem["tile_done"], tile_count(first["bout"] + 7, 1))
                nc.scalar.activation(h_hi[:, k, :], y2[:, k, :], ACT.Copy).then_inc(sem["y_hi_done"], 1)
            out_phase("out2", N_XATTN)
            std_of(N_XATTN, 1.0 / D)
            norm_hi(N_XATTN, h_hi, None)

            for j in range(4):
                for jj in range(2):
                    store_tile(first["mq"] + j, jj, m_q[:, 2 * j + jj, :])
                next_hi()
            for k in range(KT):
                act.wait_ge(sem["m_tr"], k + 1)
                nc.scalar.activation(m_T[:, k, :], ps[:, 4 + k % 4, 0:C], ACT.Copy).then_inc(sem["m_T_done"], 1)
            for k in range(KT):
                act.wait_ge(sem["m_T_done"], k + 1)
                squares(N_MEM, k, m_T[:, k, :])
            std_of(N_MEM, 1.0 / D, 2)
            norm_hi(N_MEM, m_hi, None)
            for j in range(8):
                for jj in range(2):
                    k = 2 * j + jj
                    store_tile(first["mkv"] + j, jj, m_kT[:, k, :] if k < 8 else m_vT[:, k - 8, :], cols=C)
                next_hi()
            attention("mem", prob_m, probT_m, 256 ** -0.5, om_hi)
            out_phase("mo", N_FFN)
            std_of(N_FFN, 1.0 / D)
            norm_hi(N_FFN, h_hi, None)

            def gu_round(u0_, count0, loop=None):
                for jj in range(2):
                    if loop:
                        act.wait_ge(bank_stored[bank_of(u0_ - 1, jj)], stored_count(u0_ - 1, jj, loop))
                    store_tile(u0_, jj, gate[:, jj, :], ACT.Silu, loop=loop)
                hi_of(u0_ + 2, loop)
                for jj in range(2):
                    act.wait_ge(bank_stored[bank_of(u0_ + 1, jj)], stored_count(u0_ + 1, jj, loop))
                    f = s_hi[:, :, :].rearrange("p k c -> p (k c)")
                    dst = f[:, jj * S:(jj + 1) * S] if loop is None else f[:, bass.ds(loop[0] * (2 * S) + (2 + jj) * S, S)]
                    nc.scalar.activation(dst, gu[:, jj, :], ACT.Copy).then_inc(sem["s_hi_done"], 1)
                hi_of(u0_ + 3, loop)

            gu_round(first["gu"], 0)
            with act.Fori(0, 10) as i:
                gu_round(first["gu"] + 2, i * 2 + 2, (i, 2))
            for j in range(2, 11):
                hi_of(first["down2"] + j)
            for k in range(KT):
                act.wait_ge(sem["x_last"], k + 1)
                squares(N_FINAL, k, xT[:, k, :])
            std_of(N_FINAL, 1.0 / D)
            for q in range(NT):
                act.wait_ge(sem["y_turned"], 2 * q + 1)
                nc.scalar.activation(y_out[:, q, 0:512], ps[:, (2 * q) % 4, :], ACT.Copy).then_inc(sem["y_copied"], 1)

        @block.vector
        def _(dve):
            chain = [0]

            def link(ins):
                ins.then_inc(sem["dve_chain"], 1)
                chain[0] += 1
                dve.wait_ge(sem["dve_chain"], chain[0])

            V = nc.vector

            def add_square(n, k, w=S):
                i = NORM_INDEX[n]
                if k == 0:
                    return
                dve.wait_ge(sem["n_sq"], 8 * i + k + 1)
                if k == 1:
                    if i:
                        dve.wait_ge(sem["n_sum"], n)
                    V.tensor_tensor(acc[:, 0:w], sq2[:, 0, 0:w], sq2[:, 1, 0:w], ALU.add).then_inc(sem["n_acc"], 1)
                else:
                    dve.wait_ge(sem["n_acc"], 7 * i + k - 1)
                    V.tensor_tensor(acc[:, 0:w], acc[:, 0:w], sq2[:, k % 2, 0:w], ALU.add).then_inc(sem["n_acc"], 1)

            def inverse_of(g, nt=NT):
                dve.wait_ge(sem["n_std"], g + 1)
                V.reciprocal(stat[:, g % 2, 1, 0:nt], stat[:, g % 2, 0, 0:nt]).then_inc(sem["n_inv"], 1)

            def normed(n, src, gain, lo, hi, shift, w=S):
                i = NORM_INDEX[n]
                dve.wait_ge(sem["n_bc"], n + 1)

                def scaled(k):
                    before = 8 * i + max(k - 1, 0)
                    if before:
                        dve.wait_ge(sem["n_hi"], before)
                        dve.wait_ge(sem["n_lo"], before)
                    V.scalar_tensor_tensor(tmp2[:, k % 2, 0:w], src[:, k, :], gain(k), ps[:, BC_BANK + n % 2, 0:w],
                                           ALU.mult, ALU.mult).then_inc(sem["n_t"], 1)

                def lower(k):
                    dve.wait_ge(sem["n_hi"], 8 * i + k + 1)
                    if shift is None:
                        V.tensor_tensor(lo[:, k, :], tmp2[:, k % 2, 0:w], hi[:, k, :].bitcast(F32),
                                        ALU.subtract).then_inc(sem["n_lo"], 1)
                    else:
                        V.scalar_tensor_tensor(lo[:, k, :], tmp2[:, k % 2, 0:w], shift(k), hi[:, k, :].bitcast(F32),
                                               ALU.add, ALU.subtract).then_inc(sem["n_lo"], 1)

                scaled(0)
                for k in range(KT):
                    if k + 1 < KT:
                        scaled(k + 1)
                    lower(k)

            V.memset(one_eps[:, 0:1], EPS)
            V.memset(one_eps[:, 1:2], 1.0).then_inc(sem["one_eps_done"], 1)
            dve.wait_ge(sem["vec_tr"], 1)
            V.tensor_copy(vecT[:, 0:VEC_SPLIT], ps[:, 4, 0:VEC_SPLIT])
            V.tensor_copy(vecT[:, VEC_SPLIT:VEC_N], ps[:, 4, VEC_SPLIT:VEC_N]).then_inc(sem["vec_done"], 1)

            for k in range(KT):
                dve.wait_ge(sem["tr_done"], k + 1)
                V.tensor_copy(xT[:, k, :], ps[:, 4 + k % 4, :]).then_inc(sem["xt_done"], 1)
            for k in range(KT):
                add_square(N_X, k)
            for k in range(KT):
                add_square(N_CTX, k, C)

            def ada_cols(a):
                dve.wait_ge(sem["ada_tr"], a + 1)
                if a == 0:
                    dve.wait_ge(sem["vec_done"], 1)
                bias = vecT[:, VEC_AT["ada_b"] + 2 * a:VEC_AT["ada_b"] + 2 * a + 2]
                V.tensor_tensor(mod[:, 2 * a:2 * a + 2, :], ps[:, 2 + a % 2, 0:4].rearrange("p (j i) -> p j i", i=2),
                                over_width(bias, 2), ALU.add).then_inc(sem["ada_mod"], 1)

            for a in range(8):
                ada_cols(a)
                if a == 2:
                    inverse_of(N_X)
                if a == 3:
                    inverse_of(N_CTX, 2)
            dve.wait_ge(sem["ada_mod"], 8)
            for i in range(2):
                ins = V.scalar_tensor_tensor(scl[:, i, :], mod[:, 8:16, i], 1.0,
                                             vecT[:, VEC_AT["norm1_g"]:VEC_AT["norm1_g"] + KT], ALU.add, ALU.mult)
            link(ins)
            normed(N_X, xT, lambda k: scl[:, 0, k:k + 1], h_lo, h_hi, lambda k: mod[:, k, 0:1])
            normed(N_CTX, cT, lambda k: scl[:, 1, k:k + 1], c_lo, c_hi, lambda k: mod[:, k, 1:2], C)

            for j in range(2):
                dve.wait_ge(sem["lat_sq"], j + 1)
                V.tensor_scalar(lat_q[:, j, :], lat_q[:, j, :], col("q_norm_g", j), None, ALU.mult).then_inc(sem["lat_gained"], 1)
            dve.wait_ge(sem["lat_sq"], 3)
            V.tensor_scalar(lat_kv[:, :], lat_kv[:, :], col("kv_norm_g"), None, ALU.mult).then_inc(sem["lat_gained"], 1)
            dve.wait_ge(sem["lat_std"], 1)
            V.reciprocal(lat_stat[:, 1, :], lat_stat[:, 0, :]).then_inc(sem["lat_inv"], 1)

            def scale_qk(m):
                dve.wait_ge(sem["qk_mm"], m + 1)
                if m == 0:
                    dve.wait_ge(sem["lat_inv"], 1)
                    dve.wait_ge(sem["kr_copied"], 1)
                    dve.wait_ge(sem["bc_done"], 16)
                    dve.wait_ge(sem["rope_done"], 16)
                if m >= 2:
                    dve.wait_ge(sem["qk_turned"], m - 1)
                if m < 6:
                    V.tensor_copy(qk_tok[:, m % 2, :, NOPE:QK1], kr_tok[:, m, :].unsqueeze(1).broadcast_to([P, H1, ROPE_W]))
                    kv = ps[:, 4:6, :].rearrange("p b (h c) -> p (b h) c", c=P)
                    V.tensor_scalar(qk_tok[:, m % 2, :, 0:NOPE], kv[:, :, 0:NOPE], lat_stat[:, 1, 4 + m:5 + m], None,
                                    ALU.mult).then_inc(sem["qk_scaled"], 1)
                else:
                    V.tensor_scalar(qk_tok[:, m % 2, :, :].rearrange("p (b h) c -> p b (h c)", b=2), ps[:, 4:6, 0:384],
                                    lat_stat[:, 1, m - 6:m - 5], None, ALU.mult).then_inc(sem["qk_scaled"], 1)

            def norm_qk(m):
                x = qk_tok[:, m % 2, :, :]
                dve.wait_ge(sem["qk_squared"], m + 1)
                if m >= 2:
                    dve.wait_ge(sem["qk_std"], m - 1)
                V.tensor_reduce(qk_stat[:, m % 2, 0, :], qk_sq.rearrange("p (h c) -> p h c", c=QK1), AX.X,
                                ALU.add).then_inc(sem["qk_summed"], 1)
                dve.wait_ge(sem["qk_std"], m + 1)
                link(V.reciprocal(qk_stat[:, m % 2, 2, :], qk_stat[:, m % 2, 1, :]))
                link(V.tensor_tensor(x, x, over_width(qk_stat[:, m % 2, 2, :], QK1), ALU.mult))
                gain = bc[:, QK1:2 * QK1] if m < 6 else bc[:, 0:QK1]
                ins = V.tensor_tensor(x, x, gain.unsqueeze(1).broadcast_to([P, H1, QK1]), ALU.mult)
                if m in (4, 5):
                    ins.then_inc(sem["qk_normed"], 1)
                    return
                link(ins)
                tile = m if m < 6 else m - 6
                part = x[:, :, NOPE:QK1].rearrange("p h (a b c) -> p h a b c", a=2, b=2)
                sin = rope[:, tile, 1, :].rearrange("p (a b c) -> p a b c", a=2, b=2)
                for b in range(2):
                    ins = V.tensor_tensor(rot[:, :, :, b, :], part[:, :, :, 1 - b, :],
                                          sin[:, :, b, :].unsqueeze(1).broadcast_to([P, H1, 2, 8]), ALU.mult)
                link(ins)
                rp = x[:, :, NOPE:QK1]
                link(V.tensor_tensor(rp, rp, rope[:, tile, 0, :].unsqueeze(1).broadcast_to([P, H1, ROPE_W]), ALU.mult))
                V.tensor_tensor(rp, rp, acc[:, 0:H1 * ROPE_W].rearrange("p (h c) -> p h c", c=ROPE_W),
                                ALU.add).then_inc(sem["qk_normed"], 1)

            done_ada = 8
            scale_qk(0)
            for m in range(10):
                if m < 9:
                    scale_qk(m + 1)
                norm_qk(m)
                while done_ada < ada_after(m):
                    ada_cols(done_ada)
                    done_ada += 1
            dve.wait_ge(sem["ada_mod"], 24)
            V.scalar_tensor_tensor(scl[:, 2, :], mod[:, 32:40, 0], 1.0, vecT[:, VEC_AT["norm2_g"]:VEC_AT["norm2_g"] + KT],
                                   ALU.add, ALU.mult).then_inc(sem["scl2_done"], 1)

            def attention(kind, prob, scale, dst_hi, dst_lo):
                a, b = ATT[kind]

                def maximum(n):
                    nk = keys_of(n)
                    dve.wait_ge(sem["at_scores"], n + 1)
                    src = ps[:, 2 * (n % 2):2 * (n % 2) + 2, :].rearrange("p b c -> p (b c)")[:, 0:nk]
                    if items[n][0] == "band":
                        _, h, q = items[n]
                        dve.wait_ge(sem["bias_ready"], h + 1)
                        if n >= 2:
                            dve.wait_ge(sem["at_exp"], n - 1)
                        link(V.scalar_tensor_tensor(score_b[:, n % 2, 0:nk], src, DB ** -0.5, bias_b[:, h % 2, S - nk:S],
                                                    ALU.mult, ALU.add))
                        src = score_b[:, n % 2, 0:nk]
                    link(V.reduce_max(at_stat[:, n % 4, 0:1], src, AX.X))
                    V.tensor_scalar(at_stat[:, n % 4, 1:2], at_stat[:, n % 4, 0:1], -scale, None,
                                    ALU.mult).then_inc(sem["at_max"], 1)

                def normalise(n):
                    nk = keys_of(n)
                    dve.wait_ge(sem["at_exp"], n + 1)
                    link(V.reciprocal(at_stat[:, n % 4, 3:4], at_stat[:, n % 4, 2:3]))
                    V.tensor_scalar(prob[:, n % 2, 0:nk], prob[:, n % 2, 0:nk], at_stat[:, n % 4, 3:4], None,
                                    ALU.mult).then_inc(sem["at_prob"], 1)

                def out_lo(n):
                    g, last = out_group(n)
                    if not last:
                        return
                    if kind == "mem":
                        tiles = [(2 * (g - 12) + j, 6 + j, 12 + 2 * (g - 12) + j) for j in range(2)]
                    else:
                        tiles = [(g - (4 if kind != "one" else 0), 6 + g % 2, g)]
                    for k, bank, count in tiles:
                        dve.wait_ge(sem["at_out_hi"], count + 1)
                        V.tensor_tensor(dst_lo[:, k, :], ps[:, bank, :], dst_hi[:, k, :].bitcast(F32),
                                        ALU.subtract).then_inc(sem["at_out_lo"], 1)

                maximum(a)
                for n in range(a, b):
                    if n + 1 < b:
                        maximum(n + 1)
                    normalise(n)
                    if n - 2 >= a:
                        out_lo(n - 2)
                out_lo(b - 2)
                out_lo(b - 1)

            attention("one", prob1, QK1 ** -0.5, at_hi, at_lo)

            for i in range(8):
                dve.wait_ge(sem["fc_mm"], i + 1)
                V.tensor_copy(f_c[:, i // 2, 2 * (i % 2):2 * (i % 2) + 2, :].rearrange("p t c -> p (t c)"),
                              ps[:, 4 + i % 4, :]).then_inc(sem["fc_copied"], 1)
            for g in range(4):
                dve.wait_ge(sem["fm_hi_done"], g + 1)
                V.tensor_tensor(fm_lo[:, g, :], ps[:, 4 + g, :], fm_hi[:, g, :].bitcast(F32),
                                ALU.subtract).then_inc(sem["fm_lo_done"], 1)

            for j in range(4):
                u = first["merge1"] + 3 * j
                for jj in range(2):
                    dve.wait_ge(bank_stored[bank_of(u, jj)], stored_count(u, jj))
                    dve.wait_ge(sem["tile_done"], tile_count(u + 2, jj))
                    p = bank(u + 2, jj)
                    if j:
                        dve.wait_ge(sem["y_t_done"], 2 * j - 1 + jj)
                    V.tensor_tensor(y_part[:, jj, :], p, sig1[:, j % 2, jj, :],
                                    ALU.mult).then_inc(bank_stored[bank_of(u + 2, jj)], 1)
                for jj in range(2):
                    k = 2 * j + jj
                    dve.wait_ge(bank_stored[bank_of(u + 1, jj)], stored_count(u + 1, jj))
                    dve.wait_ge(sem["tile_done"], tile_count(u + 2, 2 + jj))
                    p = bank(u + 2, 2 + jj)
                    if j:
                        dve.wait_ge(sem["y_hi_done"], k - 1)
                        dve.wait_ge(sem["y_lo_done"], k - 1)
                    else:
                        dve.wait_ge(sem["n_hi"], 8 * NORM_INDEX[N_CTX] + 8)
                        dve.wait_ge(sem["n_lo"], 8 * NORM_INDEX[N_CTX] + 8)
                    V.tensor_tensor(tmp2[:, jj, :], p, sig1[:, j % 2, 2 + jj, :],
                                    ALU.mult).then_inc(bank_stored[bank_of(u + 2, 2 + jj)], 1)
                    dve.wait_ge(bank_stored[bank_of(u + 2, 2 + jj)], stored_count(u + 2, 2 + jj))
                    dve.wait_ge(bank_stored[bank_of(u + 2, jj)], stored_count(u + 2, jj))
                    V.tensor_tensor(tmp2[:, jj, :], tmp2[:, jj, :], y_part[:, jj, :], ALU.add).then_inc(sem["y_t_done"], 1)
                for jj in range(2):
                    k = 2 * j + jj
                    dve.wait_ge(sem["y_hi_done"], k + 1)
                    V.tensor_tensor(y_lo[:, k, :], tmp2[:, jj, :], y_hi[:, k, :].bitcast(F32),
                                    ALU.subtract).then_inc(sem["y_lo_done"], 1)

            def add_to_stream(u, jj, k, gain=None, loop=None):
                dve.wait_ge(sem["tile_done"], tile_count(u, jj, loop))
                p = bank(u, jj)
                if gain is None:
                    ins = V.tensor_tensor(xT[:, k, :], p, xT[:, k, :], ALU.add)
                else:
                    ins = V.scalar_tensor_tensor(xT[:, k, :], p, gain, xT[:, k, :], ALU.mult, ALU.add)
                ins.then_inc(bank_stored[bank_of(u, jj)], 1)

            def out_phase(name, n, gain=None):
                for j in range(4):
                    for jj in range(2):
                        k = 2 * j + jj
                        add_to_stream(first[name] + j, jj, k, gain(k) if gain else None)
                        if k:
                            add_square(n, k - 1)
                add_square(n, KT - 1)

            out_phase("out1", N_2, lambda k: mod[:, 16 + k, 0:1])
            inverse_of(N_2)
            dve.wait_ge(sem["scl2_done"], 1)
            normed(N_2, xT, lambda k: scl[:, 2, k:k + 1], h_lo, h_hi, lambda k: mod[:, 24 + k, 0:1])

            def mlp_chunk(u0_, count0, loop=None):
                for j in range(4):
                    for jj in range(2):
                        q = 2 * j + jj
                        dve.wait_ge(bank_stored[bank_of(u0_ + j, jj)], stored_count(u0_ + j, jj, loop))
                        if not (isinstance(count0, int) and count0 + q < 2):
                            dve.wait_ge(sem["g_hi_done"], count0 + (q - 1))
                            dve.wait_ge(sem["g_lo_done"], count0 + (q - 1))
                        V.tensor_tensor(rsq[:, jj, :], relu[:, jj, :], relu[:, jj, :], ALU.mult).then_inc(sem["rsq_done"], 1)
                    for jj in range(2):
                        q = 2 * j + jj
                        dve.wait_ge(sem["g_hi_done"], count0 + (q + 1))
                        V.tensor_tensor(g_lo[:, q, :], rsq[:, jj, :], g_hi[:, q, :].bitcast(F32),
                                        ALU.subtract).then_inc(sem["g_lo_done"], 1)
                for j in range(4):
                    for jj in range(2):
                        k = 2 * j + jj
                        add_to_stream(u0_ + 4 + j, jj, k, mod[:, 40 + k, 0:1], loop)

            mlp_chunk(first["mlp"], 0)
            with dve.Fori(0, 3) as i:
                mlp_chunk(first["mlp"] + 8, i * 8 + 8, (i, 8))
            for k in range(KT):
                add_square(N_MIX, k)
            inverse_of(N_MIX)
            normed(N_MIX, xT, lambda k: col("norm_mix_2", k), h_lo, h_hi, None)

            ab = ps[:, 4, 0:NT * 16].rearrange("p (t c) -> p t c", c=16)
            dve.wait_ge(sem["ab_turned"], 1)
            V.memset(pad_in[:, :, 0:3], 0.0).then_inc(sem["c_pad"], 1)
            V.tensor_tensor(gp[:, 0, :, :], ab[:, :, 0:HA], bc[:, 2 * QK1:2 * QK1 + HA].unsqueeze(1).broadcast_to([P, NT, HA]),
                            ALU.add)
            V.tensor_copy(gp[:, 9, :, :], ab[:, :, HA:16]).then_inc(sem["gate_dve"], 1)
            dve.wait_ge(sem["gate_dve"], 1)
            dve.wait_ge(sem["gate_act"], 1)
            link(V.tensor_scalar(gp[:, 1, :, :], gp[:, 0, :, :], 0.0, None, ALU.max))
            link(V.tensor_tensor(gp[:, 3, :, :], gp[:, 3, :, :], gp[:, 1, :, :], ALU.add))
            V.scalar_tensor_tensor(gp[:, 4, :, :], gp[:, 3, :, :], -1.0, gp[:, 10, 0, :].unsqueeze(1).broadcast_to([P, NT, HA]),
                                   ALU.mult, ALU.mult)
            V.tensor_scalar(gp[:, 11, :, :], gp[:, 6, :, :], -1.0, None, ALU.mult).then_inc(sem["gate_dve"], 1)
            dve.wait_ge(sem["gate_cum"], 1)
            cum = ps[:, 5, 0:64].rearrange("p (i t c) -> p i t c", i=2, c=HA)
            link(V.tensor_copy(gp[:, 5, :, :], cum[:, 0]))
            V.tensor_tensor(gp[:, 9, :, :], cum[:, 1], gp[:, 5, :, :], ALU.subtract).then_inc(sem["gate_dve"], 1)
            dve.wait_ge(sem["gate_act"], 2)
            V.tensor_tensor(gp[:, 7, :, :], gp[:, 10, :, :], gp[:, 6, :, :], ALU.mult).then_inc(sem["gate_dve"], 1)

            def taps(j, h):
                at_ = (j // 2) * HA + h
                return [col("conv_w_2", 24 * i + at_) for i in range(4)]

            for p in range(4):
                u = first[f"pair{p}"]
                for j in range(6):
                    dve.wait_ge(bank_stored[bank_of(u + j // 2, j % 2)], stored_count(u + j // 2, j % 2))
                    w = taps(j, 2 * p + j % 2)
                    if j == 0 and p == 0:
                        dve.wait_ge(sem["c_pad"], 1)
                    x = pad_in[:, j, :]
                    link(V.tensor_scalar(conv[:, j, :], x[:, 3:3 + S], w[3], None, ALU.mult))
                    for i in (2, 1, 0):
                        ins = V.scalar_tensor_tensor(conv[:, j, :], x[:, i:i + S], w[i], conv[:, j, :], ALU.mult, ALU.add)
                        if i:
                            link(ins)
                    ins.then_inc(sem["c_conv"], 1)
                for j in range(4):
                    g = 4 + 4 * p + j
                    if j == 0:
                        inverse_of(g)
                    if j < 3:
                        inverse_of(g + 1)
                    dve.wait_ge(sem["n_bc"], g + 1)
                    V.scalar_tensor_tensor(conv[:, j, :], conv[:, j, :], P ** -0.5 if j < 2 else 1.0,
                                           ps[:, BC_BANK + g % 2, :], ALU.mult, ALU.mult).then_inc(sem["c_normed"], 1)
                dve.wait_ge(sem["gate_act"], 2)
                dve.wait_ge(sem["gate_dve"], 4)

                def tiled(x):
                    return x.rearrange("p (t c) -> p t c", c=P)

                for a in range(2):
                    h = 2 * p + a
                    dve.wait_ge(sem["kv_turned"], 2 * h + 1)
                    k_tok = tiled(ps[:, 4 + a, :])
                    V.tensor_tensor(k_dec[:, a, :, :], k_tok, over_width(gp[:, 8, :, h]), ALU.mult)
                    V.tensor_tensor(k_bg[:, a, :, :], k_tok, over_width(gp[:, 7, :, h]), ALU.mult).then_inc(sem["k_scaled"], 1)
                    dve.wait_ge(sem["kv_turned"], 2 * h + 2)
                    V.tensor_tensor(v_b[:, a, :, :], tiled(ps[:, 6 + a, :]), over_width(gp[:, 6, :, h]),
                                    ALU.mult).then_inc(sem["k_scaled"], 1)
                for a in range(2):
                    h = 2 * p + a
                    dve.wait_ge(sem["Gb_exp"], h + 1)
                    for tt in range(NT):
                        ins = V.tensor_scalar(decay[:, a, tt, :], ps[:, 4 + a, tt * P:(tt + 1) * P], gp[:, 5, tt, h:h + 1],
                                              0.0, ALU.subtract, ALU.max)
                    ins.then_inc(sem["d_diff"], 1)
                for a in range(2):
                    h = 2 * p + a
                    dve.wait_ge(sem["d_exp"], h + 1)
                    link(V.tensor_tensor(decay[:, a, :, :], decay[:, a, :, :], over_tiles(con("incl")), ALU.mult))
                    dve.wait_ge(sem["Gb_exp"], h + 1)
                    V.tensor_tensor(q_dec[:, a, :], conv[:, a, :], eGb[:, a, :], ALU.mult).then_inc(sem["qd_done"], 1)
                for a in range(2):
                    h = 2 * p + a
                    dve.wait_ge(sem["kk_mm"], 2 * h + 1)
                    link(V.tensor_tensor(nL[:, a, :, :], tiled(ps[:, 6 + a, :]), decay[:, a, :, :], ALU.mult))
                    V.tensor_tensor(nL[:, a, :, :], nL[:, a, :, :], over_width(gp[:, 11, :, h]), ALU.mult).then_inc(sem["nL_done"], 1)
                    dve.wait_ge(sem["kk_mm"], 2 * h + 2)
                    V.tensor_tensor(pr[:, a, :, :], tiled(ps[:, 4 + a, :]), decay[:, a, :, :], ALU.mult).then_inc(sem["nL_done"], 1)
                if p == 0:
                    dve.wait_ge(sem["masks_in"], 16)
                for a in range(2):
                    h = 2 * p + a
                    dve.wait_ge(sem["qd_done"], h + 1)
                    dve.wait_ge(sem["nL_done"], 2 * h + 2)
                    link(V.tensor_copy(inv[:, a, :, :], over_tiles(con("ident"))))
                    V.copy_predicated(inv[:, a, :, :], over_tiles(masks[:, 0, :]), nL[:, a, :, :])
                    link(V.tensor_copy(invT[:, a, :, :], over_tiles(con("ident"))))
                    dve.wait_ge(sem["nLT_done"], 2 * h + 1)
                    V.copy_predicated(invT[:, a, :, :], over_tiles(masks[:, 1, :]), nLT[:, a, :, :]).then_inc(sem["inv0_done"], 1)
                dve.wait_ge(sem["inv0_done"], 2 * p + 2)
                for s in range(1, LEVELS):
                    for a in range(2):
                        n = (p * 5 + s - 1) * 2 + a
                        dve.wait_ge(sem["lv_mm"], n + 1)
                        if s < LEVELS - 1:
                            V.copy_predicated(inv[:, a, :, :], over_tiles(masks[:, 2 * s, :]), tiled(ps[:, 4 + a, :]))
                        V.copy_predicated(invT[:, a, :, :], over_tiles(masks[:, 2 * s + 1, :]),
                                          tiled(ps[:, 6 + a, :])).then_inc(sem["lv_done"], 1)
                V.memset(state[:, :, :], 0.0).then_inc(sem["r_init"], 1)
                dve.wait_ge(sem["uw_copied"], 4 * p + 4)
                for n in range(N_CHUNKS):
                    R, tt, row = 8 * p + n, n // 2, slice((n % 2) * CHUNK, (n % 2 + 1) * CHUNK)
                    dve.wait_ge(sem["r_ws"], R + 1)
                    V.tensor_tensor(u_new[row, :, :], u0[row, :, tt, :], ps[row, 4, 0:2 * P].rearrange("p (a c) -> p a c", a=2),
                                    ALU.subtract).then_inc(sem["r_u"], 1)
                    dve.wait_ge(sem["r_su"], R + 1)
                    if n == 0:
                        dve.wait_ge(sem["r_init"], p + 1)
                    for a in range(2):
                        e = n * CHUNK + CHUNK - 1
                        ins = V.scalar_tensor_tensor(state[:, a, :], state[:, a, :], eGb[:, a, e:e + 1],
                                                     ps[:, 6, a * P:(a + 1) * P], ALU.mult, ALU.add)
                    ins.then_inc(sem["r_st"], 1)
                dve.wait_ge(sem["r_oc"], 4 * p + 4)
                flat = o_tok[:, :, :, :].rearrange("p a t c -> p (a t) c")
                sq = tmp2[:, :, :].rearrange("p a (t c) -> p (a t) c", c=P)
                link(V.tensor_tensor(sq, flat, flat, ALU.mult))
                V.tensor_reduce(o_stat[:, 0, :], sq, AX.X, ALU.add).then_inc(sem["o_sq"], 1)
                dve.wait_ge(sem["o_std"], p + 1)
                link(V.reciprocal(o_stat[:, 2, :], o_stat[:, 1, :]))
                V.tensor_tensor(flat, flat, over_width(o_stat[:, 2, :]), ALU.mult).then_inc(sem["o_scaled"], 1)
                for a in range(2):
                    dve.wait_ge(sem["o_turned"], 2 * p + a + 1)
                    dve.wait_ge(bank_stored[bank_of(u + 3, a)], stored_count(u + 3, a))
                    V.scalar_tensor_tensor(oaT[:, 2 * p + a, :], ps[:, 4 + a, :], col("head_norm_2"), z_s[:, a, :],
                                           ALU.mult, ALU.mult).then_inc(sem["o_done"], 1)

            for k in range(HA):
                dve.wait_ge(sem["oa_hi_done"], k + 1)
                dve.wait_ge(sem["o_done"], HA)
                V.tensor_tensor(oa_lo[:, k, :], oaT[:, k, :], oa_hi[:, k, :].bitcast(F32),
                                ALU.subtract).then_inc(sem["oa_lo_done"], 1)
            for j in range(4):
                u = first["aout"] + 2 * j
                for jj in range(2):
                    dve.wait_ge(bank_stored[bank_of(u, jj)], stored_count(u, jj))
                    dve.wait_ge(sem["tile_done"], tile_count(u + 1, jj))
                    p = bank(u + 1, jj)
                    V.tensor_tensor(y2[:, 2 * j + jj, :], p, sig2[:, j % 2, jj, :],
                                    ALU.mult).then_inc(bank_stored[bank_of(u + 1, jj)], 1)

            for g in range(2):
                for tt in range(NT):
                    dve.wait_ge(sem["vb_turned"], 4 * g + tt + 1)
                    V.tensor_copy(vb[:, tt, :], ps[:, 4 + tt, :]).then_inc(sem["vb_copied"], 1)
                attention(f"band{g}", prob_b, 1.0, ob_hi, ob_lo)
            for j in range(4):
                u = first["bout"] + 2 * j
                for jj in range(2):
                    k = 2 * j + jj
                    dve.wait_ge(bank_stored[bank_of(u, jj)], stored_count(u, jj))
                    dve.wait_ge(sem["tile_done"], tile_count(u + 1, jj))
                    p = bank(u + 1, jj)
                    if j:
                        dve.wait_ge(sem["y_t_done"], 8 + k - 1)
                    V.tensor_tensor(tmp2[:, jj, :], p, sig2[:, j % 2, jj, :],
                                    ALU.mult).then_inc(bank_stored[bank_of(u + 1, jj)], 1)
                    dve.wait_ge(bank_stored[bank_of(u + 1, jj)], stored_count(u + 1, jj))
                    V.tensor_tensor(y2[:, k, :], tmp2[:, jj, :], y2[:, k, :], ALU.add).then_inc(sem["y_t_done"], 1)
            for k in range(KT):
                dve.wait_ge(sem["y_hi_done"], 8 + k + 1)
                V.tensor_tensor(h_lo[:, k, :], y2[:, k, :], h_hi[:, k, :].bitcast(F32), ALU.subtract).then_inc(sem["y_lo_done"], 1)
            out_phase("out2", N_XATTN)
            inverse_of(N_XATTN)
            normed(N_XATTN, xT, lambda k: col("norm_xattn_2", k), h_lo, h_hi, None)

            for k in range(KT):
                add_square(N_MEM, k, C)
            inverse_of(N_MEM, 2)
            normed(N_MEM, m_T, lambda k: col("norm_mem_2", k), m_lo, m_hi, None, C)
            for i in range(2):
                dve.wait_ge(sem["mv_turned"], i + 1)
                V.tensor_copy(m_v[:, i, :], ps[:, 4 + 2 * i:6 + 2 * i, :].rearrange("p b c -> p (b c)")).then_inc(sem["mv_copied"], 1)
            attention("mem", prob_m, 256 ** -0.5, om_hi, om_lo)
            out_phase("mo", N_FFN)
            inverse_of(N_FFN)
            normed(N_FFN, xT, lambda k: col("norm_ffn_2", k), h_lo, h_hi, None)

            def gu_round(u0_, count0, loop=None):
                def tile(x, jj):
                    f = x[:, :, :].rearrange("p k c -> p (k c)")
                    return f[:, jj * S:(jj + 1) * S] if loop is None else f[:, bass.ds(loop[0] * (2 * S) + (2 + jj) * S, S)]

                for jj in range(2):
                    dve.wait_ge(bank_stored[bank_of(u0_, jj)], stored_count(u0_, jj, loop))
                    dve.wait_ge(sem["tile_done"], tile_count(u0_ + 1, jj, loop))
                    p = bank(u0_ + 1, jj)
                    if loop:
                        dve.wait_ge(sem["s_hi_done"], count0 + (jj - 1))
                        dve.wait_ge(sem["s_lo_done"], count0 + (jj - 1))
                    V.tensor_tensor(gu[:, jj, :], p, gate[:, jj, :], ALU.mult).then_inc(bank_stored[bank_of(u0_ + 1, jj)], 1)
                for jj in range(2):
                    dve.wait_ge(sem["s_hi_done"], count0 + (jj + 1))
                    V.tensor_tensor(tile(s_lo, jj), gu[:, jj, :], tile(s_hi, jj).bitcast(F32),
                                    ALU.subtract).then_inc(sem["s_lo_done"], 1)

            gu_round(first["gu"], 0)
            with dve.Fori(0, 10) as i:
                gu_round(first["gu"] + 2, i * 2 + 2, (i, 2))
            dve.wait_ge(sem["w_mm_done"], 11)
            for k in range(KT):
                V.tensor_tensor(xT[:, k, :], ps[:, k, :], xT[:, k, :], ALU.add).then_inc(sem["x_last"], 1)
                if k:
                    add_square(N_FINAL, k - 1)
            add_square(N_FINAL, KT - 1)
            inverse_of(N_FINAL)
            dve.wait_ge(sem["n_bc"], N_FINAL + 1)
            for k in range(KT):
                V.scalar_tensor_tensor(yT[:, k, :], xT[:, k, :], col("norm_final_2", k), ps[:, BC_BANK + N_FINAL % 2, :],
                                       ALU.mult, ALU.mult).then_inc(sem["n_t"], 1)
            for q in range(NT):
                dve.wait_ge(sem["y_turned"], 2 * q + 2)
                V.tensor_copy(y_out[:, q, 512:1024], ps[:, (2 * q + 1) % 4, :]).then_inc(sem["y_copied2"], 1)

        @block.tensor
        def _(pe):
            T = nc.tensor

            def mm3(out_, w0, w, s, hi, lo, start, stop):
                wh, wl = w_hi[:, s, w0:w0 + w], w_lo[:, s, w0:w0 + w]
                T.matmul(out_, wh, hi, start=start, stop=False, skip_group_check=True)
                T.matmul(out_, wh, lo, start=False, stop=False, skip_group_check=True)
                return T.matmul(out_, wl, hi, start=False, stop=stop, skip_group_check=True)

            def gemm(u, tiles, loop=None, ready=None):
                s = split_at[u] % 2
                pe.wait_ge(sem["w_lo_done"], val(split_at, u, loop) + 1)
                for pair in range(0, len(tiles), 2):
                    some = list(enumerate(tiles))[pair:pair + 2]
                    n = len(some[0][1][0])
                    for j, _ in some:
                        if tile_at[u] + j >= 4:
                            pe.wait_ge(bank_stored[bank_of(u, j)], stored_count(u, j, loop) - 1)
                    cut = n - 2 if n > 4 else n
                    for ks in (range(0, cut), range(cut, n)):
                        for j, (terms, w) in some:
                            for k in ks:
                                if ready and pair == 0 and j == 0:
                                    ready(k)
                                w0, hi, lo = terms[k]
                                ins = mm3(ps[:, bank_of(u, j), 0:w], w0, P, s, hi, lo, k == 0, k == n - 1)
                            if len(ks) and ks[-1] == n - 1:
                                ins.then_inc(sem["tile_done"], 1)

            def wide_gemm(u, hi, lo, loop=None, ready=None, cols=S):
                gemm(u, [([(k * 256 + jj * P, hi[:, k, 0:cols], lo[:, k, 0:cols]) for k in range(KT)], cols)
                         for jj in range(2)], loop, ready)

            def after(done, base):
                def ready(k):
                    pe.wait_ge(done, base + k + 1)
                return ready

            def sum_of(g, src, nt=NT):
                if g >= 2:
                    pe.wait_ge(sem["n_std"], g - 1)
                for tt in range(nt):
                    ins = T.matmul(ps[:, SUM_BANK + g % 2, tt * P:(tt + 1) * P], src[:, tt * P:(tt + 1) * P], con("ones"),
                                   start=True, stop=True)
                ins.then_inc(sem["n_sum"], 1)

            def norm_sum(n, nt=NT):
                pe.wait_ge(sem["n_acc"], 7 * NORM_INDEX[n] + 7)
                sum_of(n, acc, nt)

            def spread(g, nt=NT):
                pe.wait_ge(sem["n_inv"], g + 1)
                for tt in range(nt):
                    ins = T.matmul(ps[:, BC_BANK + g % 2, tt * P:(tt + 1) * P],
                                   stat[:, g % 2, 1, tt:tt + 1].broadcast_to([P, P]), con("ident"), start=True, stop=True)
                ins.then_inc(sem["n_bc"], 1)

            def turn(out_, src):
                rows = src.shape[0]
                return T.transpose(out_, src, const[0:rows, CONST_AT["ident"]:CONST_AT["ident"] + rows])

            pe.wait_ge(sem["const_done"], 16)
            pe.wait_ge(sem["in_done"], 32)
            turn(ps[:, 4, 0:VEC_SPLIT], vec_in[0:VEC_SPLIT, 0, :])
            turn(ps[:, 4, VEC_SPLIT:VEC_N], vec_in[0:VEC_N - VEC_SPLIT, 1, :]).then_inc(sem["vec_tr"], 1)
            pe.wait_ge(sem["vec_done"], 1)
            pe.wait_ge(sem["x_in_done"], 16)
            for k in range(KT):
                if k >= 4:
                    pe.wait_ge(sem["xt_done"], k - 3)
                for tt in range(NT):
                    ins = turn(ps[:, 4 + k % 4, tt * P:(tt + 1) * P], x_in[:, tt, k * P:(k + 1) * P])
                ins.then_inc(sem["tr_done"], 1)
            pe.wait_ge(sem["c_in_done"], 16)
            for k in range(KT):
                if k < 4:
                    pe.wait_ge(sem["xt_done"], 5 + k)
                else:
                    pe.wait_ge(sem["ctx_t"], k - 3)
                for tt in range(2):
                    ins = turn(ps[:, 4 + k % 4, tt * P:(tt + 1) * P], c_in[:, tt, k * P:(k + 1) * P])
                ins.then_inc(sem["ctx_tr"], 1)

            def ada_mm(a):
                u = ada_unit(a)
                if a == 0:
                    pe.wait_ge(sem["c_silu"], 2)
                if a >= 2:
                    pe.wait_ge(sem["ada_rowed"], a - 1)
                pe.wait_ge(w_in_slot[u % 2], load_count[u])
                for k in range(KT):
                    ins = T.matmul(ps[0:2, a % 2, 0:256], silu_c[:, k, :], raw[:, u % 2, k * 256:(k + 1) * 256],
                                   start=k == 0, stop=k == KT - 1)
                ins.then_inc(sem["ada_mm"], 1)

            def ada_turn(a):
                pe.wait_ge(sem["ada_rowed"], a + 1)
                if a >= 2:
                    pe.wait_ge(sem["ada_mod"], a - 1)
                for j in range(2):
                    ins = T.matmul(ps[:, 2 + a % 2, 2 * j:2 * j + 2], ada_row(a)[:, j * P:(j + 1) * P],
                                   const[0:2, CONST_AT["ident"]:CONST_AT["ident"] + 2], start=True, stop=True)
                ins.then_inc(sem["ada_tr"], 1)

            for a in range(8):
                ada_mm(a)
                if a == 1:
                    pe.wait_ge(sem["ctx_t"], KT)
                    norm_sum(N_X)
                if a == 2:
                    norm_sum(N_CTX, 2)
                if a >= 1:
                    ada_turn(a - 1)
                if a == 4:
                    spread(N_X)
                if a == 5:
                    spread(N_CTX, 2)
            ada_turn(7)
            pe.wait_ge(sem["ada_mod"], 8)

            u = first["lat"]
            wide_gemm(u, h_hi, h_lo, ready=after(sem["n_lo"], 0))
            pe.wait_ge(sem["n_lo"], 16)
            gemm(u + 1, [([(k * 256 + jj * P, x[0][:, k, :], x[1][:, k, :]) for k in range(KT)], w)
                         for x, w in (((h_hi, h_lo), S), ((c_hi, c_lo), C)) for jj in range(2)])

            pe.wait_ge(sem["lat_sq"], 3)
            pe.wait_ge(sem["n_lo"], 16)
            one = const[:, CONST_AT["ones"]:CONST_AT["ones"] + 1]
            for i in range(4):
                for k in range(2):
                    T.matmul(ps[:, 4, i:i + 1], sq_q[:, k, i * P:(i + 1) * P], one, start=k == 0, stop=k == 1)
            for i in range(6):
                ins = T.matmul(ps[:, 4, 4 + i:5 + i], sq_kv[:, i * P:(i + 1) * P], one, start=True, stop=True)
            ins.then_inc(sem["lat_ss"], 1)
            pe.wait_ge(bank_stored[bank_of(u + 1, 1)], stored_count(u + 1, 1))
            pe.wait_ge(bank_stored[bank_of(u + 1, 3)], stored_count(u + 1, 3))
            for i in range(6):
                ins = turn(ps[:, 5, i * ROPE_W:(i + 1) * ROPE_W], kr_T[:, i * P:(i + 1) * P])
            ins.then_inc(sem["kr_mm"], 1)

            def qk_mm(m):
                if m == 0:
                    pe.wait_ge(sem["lat_std"], 1)
                    pe.wait_ge(sem["kr_copied"], 1)
                    pe.wait_ge(sem["lat_gained"], 3)
                    pe.wait_ge(sem["wq_done"], 16)
                    pe.wait_ge(sem["wkv_done"], 16)
                else:
                    pe.wait_ge(sem["qk_scaled"], m)
                    pe.wait_ge(sem["v_scaled"], min(m, 6))
                for b in range(2):
                    if m < 6:
                        ins = T.matmul(ps[:, 4 + b, :], lat_kv[:, m * P:(m + 1) * P], w_kvb[:, b * 512:(b + 1) * 512],
                                       start=True, stop=True)
                    else:
                        for k in range(2):
                            ins = T.matmul(ps[:, 4 + b, 0:384], lat_q[:, k, (m - 6) * P:(m - 5) * P],
                                           w_qb[:, k, b * 384:(b + 1) * 384], start=k == 0, stop=k == 1)
                ins.then_inc(sem["qk_mm"], 1)

            def qk_turn(m):
                pe.wait_ge(sem["qk_normed"], m + 1)
                if m:
                    pe.wait_ge(sem["qk_stored"], m)
                for h in range(H1):
                    ins = turn(ps[0:QK1, 6 + h // 4, (h % 4) * P:(h % 4 + 1) * P], qk_tok[:, m % 2, h, :])
                ins.then_inc(sem["qk_turned"], 1)

            done_ada = 8
            for j in range(4):
                pe.wait_ge(bank_stored[bank_of(u + 1, j)], stored_count(u + 1, j))
            qk_mm(0)
            for m in range(10):
                if m < 9:
                    qk_mm(m + 1)
                while done_ada < ada_after(m):
                    ada_mm(done_ada)
                    done_ada += 1
                    ada_turn(done_ada - 1)
                qk_turn(m)

            def attention(kind):
                a, b = ATT[kind]

                def scores(n):
                    what, h, q = items[n]
                    nk = keys_of(n)
                    if n - 2 >= a:
                        pe.wait_ge(sem["at_exp"], n - 1)
                    tok = slice(q * P, (q + 1) * P)
                    bank = 2 * (n % 2)
                    if what == "one":
                        T.matmul(ps[:, bank, :], qT[:, h, tok], kT[:, h, 0:S], start=True, stop=True)
                        ins = T.matmul(ps[:, bank + 1, 0:C], qT[:, h, tok], kT[:, h, S:S + C], start=True, stop=True)
                    elif what == "band":
                        row, tile = slice((h % 2) * DB, (h % 2 + 1) * DB), (h % 8) // 2
                        ins = T.matmul(ps[:, bank, 0:nk], qbT[row, tile, tok], kbT[row, tile, 0:nk], start=True, stop=True)
                    else:
                        for k in range(2):
                            ins = T.matmul(ps[:, bank, 0:nk], m_q[:, 2 * h + k, tok], m_kT[:, 2 * h + k, :],
                                           start=k == 0, stop=k == 1)
                    ins.then_inc(sem["at_scores"], 1)

                def turned(n):
                    prob = {"one": prob1, "band": prob_b, "mem": prob_m}[items[n][0]]
                    pe.wait_ge(sem["at_prob"], n + 1)
                    if n:
                        pe.wait_ge(sem["at_copied"], n)
                    for kt in range(keys_of(n) // P):
                        ins = turn(ps[:, 4 + kt // 4, (kt % 4) * P:(kt % 4 + 1) * P], prob[:, n % 2, kt * P:(kt + 1) * P])
                    ins.then_inc(sem["at_turned"], 1)

                def values(n):
                    what, h, q = items[n]
                    g, _ = out_group(n)
                    tok = slice(q * P, (q + 1) * P)
                    pe.wait_ge(sem["at_copied"], n + 1)
                    if what == "mem":
                        pe.wait_ge(sem["at_out_lo"], 12 + 2 * (g - 12))
                        for j in range(2):
                            for kt in range(2):
                                ins = T.matmul(ps[:, 6 + j, tok], m_v[:, kt, h * 256 + j * P:h * 256 + (j + 1) * P],
                                               probT_m[:, n % 2, kt * P:(kt + 1) * P], start=kt == 0, stop=kt == 1)
                    else:
                        if g >= 2:
                            pe.wait_ge(sem["at_out_lo"], g - 1)
                        v, pT = (v1, probT1) if what == "one" else (vb, probT_b)
                        nk = keys_of(n) // P
                        for kt in range(nk):
                            ins = T.matmul(ps[(h % 2) * 64:(h % 2 + 1) * 64, 6 + g % 2, tok],
                                           v[:, kt, (h % 8) * 64:(h % 8 + 1) * 64], pT[:, n % 2, kt * P:(kt + 1) * P],
                                           start=kt == 0, stop=kt == nk - 1)
                    ins.then_inc(sem["at_out"], 1)

                scores(a)
                for n in range(a, b):
                    if n + 1 < b:
                        scores(n + 1)
                    if n > a:
                        values(n - 1)
                    turned(n)
                values(b - 1)

            pe.wait_ge(sem["ada_mod"], 24)
            pe.wait_ge(sem["qk_stored"], 10)
            attention("one")

            pe.wait_ge(sem["at_exp"], 32)
            for j in range(2):
                wide_gemm(first["f"] + j, h_hi, h_lo)
            pe.wait_ge(sem["dft_in"], 16)
            pe.wait_ge(sem["at_out_lo"], 4)
            dft_c = dft[:, NT * 2 * S:]
            dft_n = dft[:, 0:NT * 2 * S].rearrange("p (t i c) -> p t i c", i=2, c=S)
            for i in range(8):
                g = i // 2
                pe.wait_ge(bank_stored[bank_of(first["f"] + g // 2, g % 2)], stored_count(first["f"] + g // 2, g % 2))
                if i >= 4:
                    pe.wait_ge(sem["fc_copied"], i - 3)
                for tt in range(2):
                    tok = slice((2 * (i % 2) + tt) * P, (2 * (i % 2) + tt + 1) * P)
                    ins = T.matmul(ps[:, 4 + i % 4, tt * 256:(tt + 1) * 256], f_T[:, g, tok], dft_c, start=True, stop=True)
                ins.then_inc(sem["fc_mm"], 1)
            for g in range(4):
                pe.wait_ge(sem["fc_copied"], g + 5)
                for tt in range(NT):
                    for i in range(2):
                        ins = T.matmul(ps[:, 4 + g, :], f_c[:, g, tt, i * P:(i + 1) * P], dft_n[:, tt, i, :],
                                       start=tt == 0 and i == 0, stop=tt == NT - 1 and i == 1)
                ins.then_inc(sem["fm_mm"], 1)

            for j in range(4):
                u = first["merge1"] + 3 * j
                wide_gemm(u, h_hi, h_lo)
                wide_gemm(u + 1, h_hi, h_lo)
                if j == 0:
                    pe.wait_ge(sem["fm_lo_done"], 4)
                gemm(u + 2, [([(1024 * i + k * 256 + jj * P, hi[:, k, :], lo[:, k, :]) for k in range(4)], S)
                             for i, (hi, lo) in enumerate(((fm_hi, fm_lo), (at_hi, at_lo))) for jj in range(2)])

            def out_phase(name, hi, lo, ready, n):
                for j in range(4):
                    wide_gemm(first[name] + j, hi, lo, ready=ready if j == 0 else None)
                norm_sum(n)
                spread(n)

            out_phase("out1", y_hi, y_lo, after(sem["y_lo_done"], 0), N_2)

            def mlp_chunk(u0_, count0, loop=None):
                for j in range(4):
                    wide_gemm(u0_ + j, h_hi, h_lo, loop, after(sem["n_lo"], 16) if loop is None and j == 0 else None)
                for j in range(4):
                    wide_gemm(u0_ + 4 + j, g_hi, g_lo, loop, after(sem["g_lo_done"], count0) if j == 0 else None)

            mlp_chunk(first["mlp"], 0)
            with pe.Fori(0, 3) as i:
                mlp_chunk(first["mlp"] + 8, i * 8 + 8, (i, 8))
            norm_sum(N_MIX)
            spread(N_MIX)

            u = first["ab"]
            gemm(u, [([(k * P, h_hi[:, k, :], h_lo[:, k, :]) for k in range(KT)], S)], ready=after(sem["n_lo"], 24))
            pe.wait_ge(bank_stored[bank_of(u, 0)], stored_count(u, 0))
            for tt in range(NT):
                ins = turn(ps[:, 4, tt * 16:(tt + 1) * 16], ab_T[:, tt * P:(tt + 1) * P])
            ins.then_inc(sem["ab_turned"], 1)
            pe.wait_ge(sem["gate_dve"], 2)
            rhs = gp[:, 4, :, :].rearrange("p t c -> p (t c)")
            T.matmul(ps[:, 5, 0:32], con("tri"), rhs, start=True, stop=True)
            T.matmul(ps[:, 5, 32:64], con("same"), rhs, start=True, stop=True).then_inc(sem["gate_cum"], 1)
            pe.wait_ge(sem["gate_dve"], 3)

            def tok(tt):
                return slice(tt * P, (tt + 1) * P)

            for p in range(4):
                u = first[f"pair{p}"]
                for kind in range(4):
                    wide_gemm(u + kind, h_hi, h_lo)
                for j in range(4):
                    g = 4 + 4 * p + j
                    pe.wait_ge(sem["c_sq"], 4 * p + j + 1)
                    sum_of(g, sq2[:, j % 2, :])
                    if j:
                        if g - 1 >= 6:
                            pe.wait_ge(sem["c_normed"], g - 6)
                        spread(g - 1)
                pe.wait_ge(sem["c_normed"], 4 * p + 2)
                spread(7 + 4 * p)
                pe.wait_ge(sem["c_normed"], 4 * p + 4)
                pe.wait_ge(sem["c_silued"], 6 * p + 6)
                for a in range(2):
                    for tt in range(NT):
                        ins = turn(ps[:, 4 + a, tok(tt)], conv[:, 2 + a, tok(tt)])
                    ins.then_inc(sem["kv_turned"], 1)
                    for tt in range(NT):
                        ins = turn(ps[:, 6 + a, tok(tt)], conv[:, 4 + a, tok(tt)])
                    ins.then_inc(sem["kv_turned"], 1)
                for a in range(2):
                    h = 2 * p + a
                    pe.wait_ge(sem["k_scaled"], 2 * h + 1)
                    for tt in range(NT):
                        ins = T.matmul(ps[:, 4 + a, tok(tt)], gp[:, 4, tt, h:h + 1].broadcast_to([P, P]), con("tri"),
                                       start=True, stop=True)
                    ins.then_inc(sem["Gb_mm"], 1)
                for a in range(2):
                    h = 2 * p + a
                    pe.wait_ge(sem["k_scaled"], 2 * h + 2)
                    for tt in range(NT):
                        ins = T.matmul(ps[:, 6 + a, tok(tt)], conv[:, 2 + a, tok(tt)], conv[:, 2 + a, tok(tt)], start=True, stop=True)
                    ins.then_inc(sem["kk_mm"], 1)
                    pe.wait_ge(sem["Gb_exp"], h + 1)
                    pe.wait_ge(sem["d_diff"], h + 1)
                    for tt in range(NT):
                        ins = T.matmul(ps[:, 4 + a, tok(tt)], conv[:, a, tok(tt)], conv[:, 2 + a, tok(tt)], start=True, stop=True)
                    ins.then_inc(sem["kk_mm"], 1)
                for a in range(2):
                    for i, src in enumerate((nL, pr)):
                        pe.wait_ge(sem["nL_done"], 4 * p + 2 * a + i + 1)
                        for tt in range(NT):
                            ins = turn(ps[:, (6 if i == 0 else 4) + a, tok(tt)], src[:, a, tt, :])
                        ins.then_inc(sem["nL_turned"], 1)
                pe.wait_ge(sem["nLT_done"], 4 * p + 4)
                for s in range(1, LEVELS):
                    for a in range(2):
                        n = (p * 5 + s - 1) * 2 + a
                        if s == 1:
                            pe.wait_ge(sem["inv0_done"], 2 * p + a + 1)
                        else:
                            pe.wait_ge(sem["lv_done"], n - 1)
                        for tt in range(NT):
                            ins = T.matmul(ps[:, 6 + a, tok(tt)], nLT[:, a, tt, :], inv[:, a, tt, :], start=True, stop=True)
                        ins.then_inc(sem["lv_m1"], 1)
                    for a in range(2):
                        n = (p * 5 + s - 1) * 2 + a
                        pe.wait_ge(sem["lv_copied"], n + 1)
                        if s < LEVELS - 1:
                            for tt in range(NT):
                                T.matmul(ps[:, 4 + a, tok(tt)], invT[:, a, tt, :], prod[:, a, tt, :], start=True, stop=True)
                        for tt in range(NT):
                            ins = T.matmul(ps[:, 6 + a, tok(tt)], prod[:, a, tt, :], invT[:, a, tt, :], start=True, stop=True)
                        ins.then_inc(sem["lv_mm"], 1)
                for a in range(2):
                    pe.wait_ge(sem["lv_done"], (p * 5 + 4) * 2 + a + 1)
                    for tt in range(NT):
                        ins = T.matmul(ps[:, 4 + a, tok(tt)], invT[:, a, tt, :], v_b[:, a, tt, :], start=True, stop=True)
                    ins.then_inc(sem["uw_mm"], 1)
                    for tt in range(NT):
                        ins = T.matmul(ps[:, 6 + a, tok(tt)], k_bg[:, a, tt, :], invT[:, a, tt, :], start=True, stop=True)
                    ins.then_inc(sem["uw_mm"], 1)
                pe.wait_ge(sem["uw_copied"], 4 * p + 4)
                pe.wait_ge(sem["r_init"], p + 1)
                for n in range(N_CHUNKS):
                    R, tt, r0_ = 8 * p + n, n // 2, (n % 2) * CHUNK
                    row, ch = slice(r0_, r0_ + CHUNK), slice(n * CHUNK, (n + 1) * CHUNK)
                    ob = 5 + 2 * (tt % 2)
                    if n:
                        pe.wait_ge(sem["r_st"], R)
                    for a in range(2):
                        ins = T.matmul(ps[row, 4, a * P:(a + 1) * P], wT[:, a, ch], state[:, a, :], start=True, stop=True)
                    ins.then_inc(sem["r_ws"], 1)
                    if tt >= 2:
                        pe.wait_ge(sem["r_oc"], 4 * p + tt - 1)
                    for a in range(2):
                        T.matmul(ps[row, ob, a * P:(a + 1) * P], q_dec[:, a, ch], state[:, a, :], start=a == 0, stop=False,
                                 skip_group_check=True)
                    pe.wait_ge(sem["r_u"], R + 1)
                    for a in range(2):
                        T.matmul(ps[row, ob, a * P:(a + 1) * P], prT[row, a, tt, ch.start - tt * P:ch.stop - tt * P], u_new[row, a, :],
                                 start=False, stop=True, skip_group_check=True)
                    for a in range(2):
                        ins = T.matmul(ps[:, 6, a * P:(a + 1) * P], k_dec[row, a, tt, :], u_new[row, a, :], start=True, stop=True)
                    ins.then_inc(sem["r_su"], 1)
                pe.wait_ge(sem["o_scaled"], p + 1)
                for a in range(2):
                    for tt in range(NT):
                        ins = turn(ps[:, 4 + a, tok(tt)], o_tok[:, a, tt, :])
                    ins.then_inc(sem["o_turned"], 1)

            for j in range(4):
                wide_gemm(first["aout"] + 2 * j, h_hi, h_lo)
                wide_gemm(first["aout"] + 2 * j + 1, oa_hi, oa_lo, ready=after(sem["oa_lo_done"], 0) if j == 0 else None)

            for g in range(2):
                u = first[f"band{g}"]
                for j in range(6):
                    wide_gemm(u + j, h_hi, h_lo)
                for j in range(6):
                    pe.wait_ge(bank_stored[bank_of(u + j, 0)], stored_count(u + j, 0))
                    pe.wait_ge(bank_stored[bank_of(u + j, 1)], stored_count(u + j, 1))
                pe.wait_ge(sem["o_done"], 8)
                for tt in range(NT):
                    for i in range(4):
                        ins = turn(ps[:, 4 + tt, i * P:(i + 1) * P], vbT[:, i, tok(tt)])
                    ins.then_inc(sem["vb_turned"], 1)
                pe.wait_ge(sem["vb_copied"], 4 * g + 4)
                attention(f"band{g}")
                pe.wait_ge(sem["at_out_lo"], 8 + 4 * g)
            for j in range(4):
                wide_gemm(first["bout"] + 2 * j, h_hi, h_lo)
                wide_gemm(first["bout"] + 2 * j + 1, ob_hi, ob_lo)
            out_phase("out2", h_hi, h_lo, after(sem["y_lo_done"], 8), N_XATTN)

            for j in range(4):
                wide_gemm(first["mq"] + j, h_hi, h_lo, ready=after(sem["n_lo"], 32) if j == 0 else None)
            pe.wait_ge(sem["m_in_done"], 16)
            pe.wait_ge(sem["n_t"], 8 * NORM_INDEX[N_XATTN] + 8)
            for k in range(KT):
                if k >= 4:
                    pe.wait_ge(sem["m_T_done"], k - 3)
                for tt in range(2):
                    ins = turn(ps[:, 4 + k % 4, tok(tt)], m_in[:, tt, k * P:(k + 1) * P])
                ins.then_inc(sem["m_tr"], 1)
            pe.wait_ge(sem["m_T_done"], KT)
            norm_sum(N_MEM, 2)
            spread(N_MEM, 2)
            for j in range(8):
                wide_gemm(first["mkv"] + j, m_hi, m_lo, ready=after(sem["n_lo"], 40) if j == 0 else None, cols=C)
            for j in range(8):
                pe.wait_ge(bank_stored[bank_of(first["mkv"] + j, 0)], stored_count(first["mkv"] + j, 0))
                pe.wait_ge(bank_stored[bank_of(first["mkv"] + j, 1)], stored_count(first["mkv"] + j, 1))
            for i in range(2):
                for k in range(KT):
                    ins = turn(ps[:, 4 + 2 * i + k // 4, (k % 4) * P:(k % 4 + 1) * P], m_vT[:, k, tok(i)])
                ins.then_inc(sem["mv_turned"], 1)
            pe.wait_ge(sem["mv_copied"], 2)
            attention("mem")
            out_phase("mo", om_hi, om_lo, after(sem["at_out_lo"], 12), N_FFN)

            def gu_round(u0_, loop=None):
                for j in range(2):
                    wide_gemm(u0_ + j, h_hi, h_lo, loop, after(sem["n_lo"], 48) if loop is None and j == 0 else None)

            gu_round(first["gu"])
            with pe.Fori(0, 10) as i:
                gu_round(first["gu"] + 2, (i, 2))

            def down(j, loop=None):
                u = first["down2"] + j
                pe.wait_ge(sem["w_lo_done"], val(split_at, u, loop) + 1)
                pe.wait_ge(sem["s_lo_done"], (2 * j if loop is None else i_ * 4 + 2 * j) + 2)
                s = split_at[u] % 2
                for o in range(8):
                    for k in range(2):
                        if loop is None:
                            hi, lo = s_hi[:, 2 * j + k, :], s_lo[:, 2 * j + k, :]
                        else:
                            at_ = bass.ds(i_ * (4 * S) + (2 * j + k) * S, S)
                            hi, lo = (x[:, :, :].rearrange("p k c -> p (k c)")[:, at_] for x in (s_hi, s_lo))
                        ins = mm3(ps[:, o, :], k * D + o * P, P, s, hi, lo, j == 0 and k == 0, j == 10 and k == 1)
                ins.then_inc(sem["w_mm_done"], 1)

            for j in range(2):
                pe.wait_ge(bank_stored[bank_of(first["gu"] + 20, j)], stored_count(first["gu"] + 20, j))
                pe.wait_ge(bank_stored[bank_of(first["gu"] + 21, j)], stored_count(first["gu"] + 21, j))
            pe.wait_ge(sem["n_t"], 8 * NORM_INDEX[N_FFN] + 8)
            down(0)
            with pe.Fori(0, 4) as i_:
                for j in range(2):
                    down(1 + j, (i_, 2))
            down(9)
            down(10)
            pe.wait_ge(sem["x_last"], KT)
            norm_sum(N_FINAL)
            spread(N_FINAL)
            pe.wait_ge(sem["n_t"], 8 * NORM_INDEX[N_FINAL] + 8)
            for q in range(NT):
                for half in range(2):
                    n = 2 * q + half
                    if n >= 4:
                        pe.wait_ge(sem["y_copied"] if half == 0 else sem["y_copied2"], q - 1)
                    for k in range(4):
                        ins = turn(ps[:, n % 4, k * P:(k + 1) * P], yT[:, 4 * half + k, tok(q)])
                    ins.then_inc(sem["y_turned"], 1)


_TWO_D = ["ada_w", "w_in", "w_fourier", "w_qb", "w_kvb", "w_mla_o", "w_out", "w_up", "w_down", "w_in_2", "w_a_out_2",
          "w_b_out_2", "w_o_2", "w_mq_2", "w_mkv_2", "w_mo_2", "w_gate_up_2", "w_down_2", "x", "ctx", "mem_2"]


def kernel(**inputs):
    import concourse.bacc as bacc
    from concourse.bass_utils import run_bass_kernel_spmd

    arrays = {}
    for name in _TWO_D:
        a = np.asarray(inputs[name])
        arrays[name] = np.ascontiguousarray(a.reshape(a.shape[-2:]))
    rows = [np.asarray(inputs[name]).reshape(-1, P) for name, _ in VEC_ROWS]
    arrays["vec"] = np.ascontiguousarray(np.concatenate(rows, axis=0))
    wide = [np.asarray(inputs[n]).reshape(1, -1) for n in ("q_gain", "k_gain", "dt_bias_2", "a_log_2")]
    arrays["bc"] = np.ascontiguousarray(np.broadcast_to(np.concatenate(wide, axis=1), (P, 2 * QK1 + 2 * HA)))
    dist = 384 + np.arange(P)[:, None] - np.arange(S)[None, :]
    arrays["bias_band"] = np.ascontiguousarray(
        np.asarray(inputs["rel_bias_2"])[:, np.clip(dist, -(CHUNK - 1), MAX_REL) + (CHUNK - 1)])
    arrays.update(shape_constants())

    nc = bacc.Bacc("TRN2", target_bir_lowering=False, num_devices=1)
    t = {n: nc.dram_tensor(n, a.shape, mybir.dt.from_np(a.dtype), kind="ExternalInput").ap() for n, a in arrays.items()}
    out = nc.dram_tensor("out", (S, D), F32, kind="ExternalOutput").ap()
    build(nc, t, out)
    got = run_bass_kernel_spmd(nc, [arrays], core_ids=[0])
    return got.results[0]["out"].reshape(1, S, D)
```

```python
import math

import numpy as np

import concourse.bass as bass
from concourse import mybir

F32 = mybir.dt.float32
F32R = mybir.dt.float32r
U32 = mybir.dt.uint32
ACT = mybir.ActivationFunctionType
ALU = mybir.AluOpType
AX = mybir.AxisListType

P = 128
D = 1024
KT = D // P
S = 512
NT = S // P
C = 256
EPS = 1e-6
FOUR_W, Q_LORA, KV_LORA, ROPE_W = 512, 256, 128, 32
GATE1_COL = FOUR_W + Q_LORA + KV_LORA + ROPE_W
H1, NOPE, QK1, V1 = 8, 64, 96, 64
D_FF = 4 * D
CHUNK, N_CHUNKS = 64, 8
HA = 8
HB, DB = 16, 64
HM = 4
FF2 = 2816
MAX_REL = 256
COL_AB = 4 * D
COL_BAND = 4 * D + 16
COL_GATE2 = COL_BAND + 3 * D

VEC_ROWS = [("norm1_g", 8), ("norm2_g", 8), ("ada_b", 48), ("b_gate", 16), ("q_norm_g", 2), ("kv_norm_g", 1),
            ("norm_mix_2", 8), ("head_norm_2", 1), ("norm_xattn_2", 8), ("norm_mem_2", 8), ("norm_ffn_2", 8),
            ("norm_final_2", 8), ("c", 8), ("c_ctx", 8), ("conv_w_2", 96)]
VEC_SPLIT = 124
VEC_AT, _n = {}, 0
for _name, _rows in VEC_ROWS:
    VEC_AT[_name] = _n
    _n += _rows
VEC_N = _n

CONST_AT, CONST_N = {}, 0
for _name, _cols in [("ident", P), ("ones", P), ("tri", P), ("same", P), ("incl", P)]:
    CONST_AT[_name] = CONST_N
    CONST_N += _cols
LEVELS = 6


def shape_constants():
    i = np.arange(P)
    same = (i[:, None] // CHUNK) == (i[None, :] // CHUNK)
    cols = {"ident": np.eye(P), "ones": np.ones((P, P)), "tri": same & (i[:, None] <= i[None, :]), "same": same,
            "incl": same & (i[:, None] >= i[None, :])}
    const = np.concatenate([np.asarray(cols[n], np.float32) for n in CONST_AT], axis=1)
    masks = []
    for s in range(LEVELS):
        b = i >> s
        low = (b[:, None] % 2 == 1) & (b[None, :] == b[:, None] - 1)
        masks += [low, low.T]
    masks = np.stack(masks, axis=1).astype(np.uint32).reshape(P, 2 * LEVELS * P)
    n, c = np.arange(S), np.arange(P)
    norm = 1.0 / math.sqrt(S * P)
    an, ac = 2 * np.pi * ((n[:, None] * n[None, :]) % S) / S, 2 * np.pi * ((c[:, None] * c[None, :]) % P) / P
    dft_n = np.stack([np.cos(an), -np.sin(an)], axis=0).reshape(2, NT, P, S).transpose(2, 1, 0, 3)
    dft_c = np.concatenate([np.cos(ac), np.sin(ac)], axis=1) * norm
    dft = np.concatenate([dft_n.reshape(P, -1), dft_c], axis=1).astype(np.float32)
    f = np.float32(10000.0) ** (-np.arange(8, dtype=np.float32) / np.float32(8))
    t = np.arange(S)
    row, col = (t // 64).astype(np.float32)[:, None] * f, (t % 64).astype(np.float32)[:, None] * f
    ang = np.concatenate([row, row, col, col], axis=1).astype(np.float32)
    sign = np.repeat(np.array([-1, 1, -1, 1], np.float32), 8)
    rope = np.stack([np.cos(ang), np.sin(ang) * sign], axis=1)
    rope = rope.reshape(NT, P, 2, ROPE_W).transpose(1, 0, 2, 3).reshape(P, -1).astype(np.float32)
    return {"const": const, "masks": masks, "dft": dft, "rope": rope}


def build(nc, t, out):
    at = [(nc.sbuf_base + 63) // 64 * 64]
    END = nc.sbuf_usable_end

    def fixed(name, shape, dt=F32):
        x = nc.alloc_sbuf_tensor_at(name, list(shape), dt, offset=at[0])
        at[0] += (int(np.prod(shape[1:])) * 4 + 31) // 32 * 32
        return x

    UNIT = 2048
    raw = fixed("raw", [P, 2, UNIT])
    w_hi = fixed("w_hi", [P, 2, UNIT], F32R)
    w_lo = fixed("w_lo", [P, 2, UNIT], F32R)
    xT = fixed("xT", [P, KT, S])
    h_hi = fixed("h_hi", [P, KT, S], F32R)
    h_lo = fixed("h_lo", [P, KT, S], F32R)
    const = fixed("const", [P, CONST_N])
    vecT = fixed("vecT", [P, VEC_N])
    mod = fixed("mod", [P, 48, 2])
    silu_c = fixed("silu_c", [P, KT, 2])
    bc = fixed("bc", [P, 2 * QK1 + 2 * HA])
    scl = fixed("scl", [P, 3, KT])
    one_eps = fixed("one_eps", [P, 8])
    stat = fixed("stat", [P, 2, 2, NT])
    lat_stat = fixed("lat_stat", [P, 2, 10])
    qk_stat = fixed("qk_stat", [P, 2, 3, H1])
    at_stat = fixed("at_stat", [P, 4, 4])
    o_stat = fixed("o_stat", [P, 3, 8])
    sq2 = fixed("sq2", [P, 2, S])
    acc = fixed("acc", [P, S])
    tmp2 = fixed("tmp2", [P, 2, S])
    BASE = at[0]

    class Region:

        def __init__(self, start=0):
            self.at = BASE + start

        def __call__(self, name, shape, dt=F32):
            x = nc.alloc_sbuf_tensor_at(name, list(shape), dt, offset=self.at)
            self.at += (int(np.prod(shape[1:])) * 4 + 31) // 32 * 32
            return x

        def over(self, name, shape, offset, dt=F32):
            return nc.alloc_sbuf_tensor_at(name, list(shape), dt, offset=offset)

    r = Region()
    x_in = r("x_in", [P, NT, D])
    c_in = r("c_in", [P, 2, D])
    cT = r("cT", [P, KT, C])
    c_hi = r("c_hi", [P, KT, C], F32R)
    c_lo = r("c_lo", [P, KT, C], F32R)
    vec_in = r("vec_in", [P, 2, P])
    ada_row = r("ada_row", [2, 2, 256])
    r = Region()
    qT = r("qT", [QK1, H1, S])
    kT = r("kT", [QK1, H1, S + C])
    v1 = r("v1", [P, 6, H1 * V1])
    ada_sum = r("ada_sum", [P, 8, 256])
    r = Region(60 * 1024)
    lat_q = r("lat_q", [P, 2, S])
    lat_kv = r("lat_kv", [P, S + C])
    kr_T = r("kr_T", [ROPE_W, S + C])
    sq_q = r("sq_q", [P, 2, S])
    sq_kv = r("sq_kv", [P, S + C])
    kr_tok = r("kr_tok", [P, 6, ROPE_W])
    rope = r("rope", [P, NT, 2, ROPE_W])
    qk_tok = r("qk_tok", [P, 2, H1, QK1])
    w_qb = r("w_qb", [P, 2, H1 * QK1])
    w_kvb = r("w_kvb", [P, 1024])
    r = Region(60 * 1024)
    at_hi = r("at_hi", [P, 4, S], F32R)
    at_lo = r("at_lo", [P, 4, S], F32R)
    prob1 = r("prob1", [P, 2, S + C])
    probT1 = r("probT1", [P, 2, S + C])
    r = Region()
    f_T = r("f_T", [P, 4, S])
    f_c = r("f_c", [P, 4, NT, 2 * P])
    dft = r("dft", [P, NT * 2 * S + 2 * P])
    r = Region(76 * 1024)
    fm_hi = r("fm_hi", [P, 4, S], F32R)
    fm_lo = r("fm_lo", [P, 4, S], F32R)
    r = Region()
    sig1 = r("sig1", [P, 2, 4, S])
    y_part = r("y_part", [P, 2, S])
    y_hi = r("y_hi", [P, KT, S], F32R)
    y_lo = r("y_lo", [P, KT, S], F32R)
    r = Region()
    g_hi = r("g_hi", [P, KT, S], F32R)
    g_lo = r("g_lo", [P, KT, S], F32R)
    relu = r("relu", [P, 2, S])
    rsq = r("rsq", [P, 2, S])
    r = Region()
    oaT = r("oaT", [P, HA, S])
    masks = r("masks", [P, 2 * LEVELS, P], U32)
    pad_in = r("pad_in", [P, 6, S + 4])
    conv_at = r.at
    conv = r("conv", [P, 6, S])
    z_s = r("z_s", [P, 2, S])
    ab_T = r("ab_T", [16, S])
    gp = r("gp", [P, 12, NT, HA])
    k_dec = r("k_dec", [P, 2, NT, P])
    k_bg = r("k_bg", [P, 2, NT, P])
    v_b = r("v_b", [P, 2, NT, P])
    eGb = r("eGb", [P, 2, S])
    decay_at = r.at
    decay = r("decay", [P, 2, NT, P])
    q_dec = r("q_dec", [P, 2, S])
    nL_at = r.at
    nL = r("nL", [P, 2, NT, P])
    pr_at = r.at
    pr = r("pr", [P, 2, NT, P])
    nLT = r("nLT", [P, 2, NT, P])
    prT = r("prT", [P, 2, NT, P])
    u_new = r("u_new", [P, 2, P])
    state = r("state", [P, 2, P])
    inv = r.over("inv", [P, 2, NT, P], conv_at)
    invT = r.over("invT", [P, 2, NT, P], conv_at + 4 * 1024)
    prod = r.over("prod", [P, 2, NT, P], conv_at + 8 * 1024)
    u0 = r.over("u0", [P, 2, NT, P], nL_at)
    wT = r.over("wT", [P, 2, S], pr_at)
    o_tok = r.over("o_tok", [P, 2, NT, P], decay_at)
    r = Region(16 * 1024)
    y2 = r("y2", [P, KT, S])
    ob_at = r.at
    oa_hi = r("oa_hi", [P, HA, S], F32R)
    oa_lo = r("oa_lo", [P, HA, S], F32R)
    sig2 = r("sig2", [P, 2, 2, S])
    ob_hi = r.over("ob_hi", [P, KT, S], ob_at, F32R)
    ob_lo = r.over("ob_lo", [P, KT, S], ob_at + 16 * 1024, F32R)
    qbT = r.over("qbT", [P, 4, S], BASE)
    kbT = r.over("kbT", [P, 4, S], BASE + 8 * 1024)
    r = Region(ob_at - BASE + 32 * 1024)
    vbT = r("vbT", [P, 4, S])
    vb = r("vb", [P, NT, S])
    score_b = r("score_b", [P, 2, S])
    bias_b = r("bias_b", [P, 2, S])
    prob_b = r.over("prob_b", [P, 2, S], r.at)
    r.at += 4 * 1024
    probT_b = r("probT_b", [P, 2, S])
    r = Region(16 * 1024)
    m_q = r("m_q", [P, KT, S])
    m_kT = r("m_kT", [P, KT, C])
    m_vT = r("m_vT", [P, KT, C])
    m_v = r("m_v", [P, 2, D])
    om_hi = r("om_hi", [P, KT, S], F32R)
    om_lo = r("om_lo", [P, KT, S], F32R)
    m_in = r.over("m_in", [P, 2, D], BASE + 56 * 1024)
    m_T = r.over("m_T", [P, KT, C], BASE + 64 * 1024)
    m_hi = r.over("m_hi", [P, KT, C], BASE, F32R)
    m_lo = r.over("m_lo", [P, KT, C], BASE + 8 * 1024, F32R)
    prob_m = r.over("prob_m", [P, 2, C], BASE)
    probT_m = r.over("probT_m", [P, 2, C], BASE + 2 * 1024)
    r = Region()
    s_hi = r("s_hi", [P, 22, S], F32R)
    s_lo = r("s_lo", [P, 22, S], F32R)
    gate = r("gate", [P, 2, S])
    gu = r("gu", [P, 2, S])
    r = Region()
    yT = r("yT", [P, KT, S])
    y_out = r("y_out", [P, NT, D])

    ps = nc.alloc_psum_tensor("ps", [P, 8, 512], F32)

    def col(name, k=0):
        return vecT[:, VEC_AT[name] + k:VEC_AT[name] + k + 1]

    def con(name):
        return const[:, CONST_AT[name]:CONST_AT[name] + P]

    def over_tiles(m):
        return m.unsqueeze(1).broadcast_to([P, NT, P])

    def over_width(m, w=P):
        return m.unsqueeze(2).broadcast_to([m.shape[0], m.shape[1], w])

    class Unit:
        def __init__(self, kind, loads, tiles, split=True, n=UNIT):
            self.kind, self.loads, self.tiles, self.split, self.n = kind, loads, tiles, split, n

    units, first = [], {}
    GATED = [("sig", 0), ("sig", 1), ("proj", 0), ("sig", 2), ("proj", 1), ("sig", 3), ("proj", 2), ("proj", 3)]

    def block(w, r0, kt, c0, cols):
        return w[r0:r0 + kt * P, c0:c0 + cols].rearrange("(k p) c -> p k c", p=P)

    def add(phase, kind, loads, tiles, split=True):
        first.setdefault(phase, len(units))
        n = max(o + k * c for (_, o, k, c) in loads)
        units.append(Unit(kind, loads, tiles, split, n))

    def wide(phase, kind, w, r0, c0, tiles=2, split=True):
        add(phase, kind, [(block(w, r0, KT, c0, 256), 0, KT, 256)], tiles, split)

    ADA_BLOCK = [4, 5, 6, 7, 0, 1, 2, 3]
    for i, j in enumerate(ADA_BLOCK):
        if i == 5:
            wide("lat_q", "q", t["w_in"], 0, FOUR_W, 2)
        wide("ada_a", "ada", t["ada_w"], 0, 256 * j, 0, False)
    wide("lat_kv", "kv", t["w_in"], 0, FOUR_W + Q_LORA, 4)
    for j in range(8, 24):
        wide("ada_b", "ada", t["ada_w"], 0, 256 * j, 0, False)
    for j in range(2):
        wide("f", "f", t["w_in"], 0, 256 * j)
    for j in range(4):
        wide("merge1", "gf", t["w_in"], 0, GATE1_COL + 256 * j)
        wide("merge1", "ga", t["w_in"], 0, GATE1_COL + D + 256 * j)
        add("merge1", "wfa", [(block(t["w_fourier"], 0, 4, 256 * j, 256), 0, 4, 256),
                              (block(t["w_mla_o"], 0, 4, 256 * j, 256), 1024, 4, 256)], 4)
    for j in range(4):
        wide("out1", "out", t["w_out"], 0, 256 * j)
    for c in range(4):
        for j in range(4):
            wide("mlp", "up", t["w_up"], 0, D * c + 256 * j)
        for j in range(4):
            wide("mlp", "down", t["w_down"], D * c, 256 * j)
    add("ab", "ab", [(block(t["w_in_2"], 0, KT, COL_AB, P), 0, KT, P)], 1)
    for p in range(4):
        for kind in range(4):
            wide(f"pair{p}", "qkvz"[kind], t["w_in_2"], 0, D * kind + 256 * p)
    for kind, j in GATED:
        if kind == "sig":
            wide("aout", "sig", t["w_in_2"], 0, COL_GATE2 + 256 * j)
        else:
            wide("aout", "proj", t["w_a_out_2"], 0, 256 * j)
    for g in range(2):
        for kind in range(3):
            for j in range(2):
                wide(f"band{g}", "qkv"[kind], t["w_in_2"], 0, COL_BAND + D * kind + 512 * g + 256 * j)
    for kind, j in GATED:
        if kind == "sig":
            wide("bout", "sig", t["w_in_2"], 0, COL_GATE2 + D + 256 * j)
        else:
            wide("bout", "proj", t["w_b_out_2"], 0, 256 * j)
    for j in range(4):
        wide("out2", "out", t["w_o_2"], 0, 256 * j)
    for j in range(4):
        wide("mq", "mq", t["w_mq_2"], 0, 256 * j)
    for j in range(8):
        wide("mkv", "mkv", t["w_mkv_2"], 0, 256 * j)
    for j in range(4):
        wide("mo", "out", t["w_mo_2"], 0, 256 * j)
    for j in range(11):
        wide("gu", "gate", t["w_gate_up_2"], 0, 256 * j)
        wide("gu", "up", t["w_gate_up_2"], 0, FF2 + 256 * j)
    for j in range(11):
        add("down2", "down2", [(block(t["w_down_2"], 256 * j, 2, 0, D), 0, 2, D)], 0)
    NU = len(units)
    ada_units = [u for u in range(NU) if units[u].kind == "ada"]
    split_at, tile_at, load_count, raw_used_count = [], [], [], []
    n_split = n_tile = 0
    per_slot = [0, 0]
    for u, x in enumerate(units):
        split_at.append(n_split)
        tile_at.append(n_tile)
        n_split += x.split
        n_tile += x.tiles
        per_slot[u % 2] += 16 * len(x.loads)
        load_count.append(per_slot[u % 2])
        raw_used_count.append(u // 2 + 1)
    split_at.append(n_split)
    tile_at.append(n_tile)

    def val(table, u, loop=None):
        if loop is None:
            return table[u]
        i, stride = loop
        return i * (table[u + stride] - table[u]) + table[u]

    names = """tile_done w_mm_done last_mm w_lo_half w_lo_done ada_mm ada_summed ada_batch pool_chain in_done at_out dft_in masks_in at_max m_in_done y_copied y_copied2
    stored w_hi_done bias_ready act_chain n_acc n_sq n_sum n_std n_t n_hi const_done x_in_done c_in_done bc_done
    rope_done wq_done wkv_done vec_done c_silu xt_done ctx_tr ctx_t ada_tr ada_rowed one_eps_done lat_sq lat_ss
    lat_std kr_mm kr_copied kr_put qk_scaled v_scaled qk_summed qk_squared qk_turned qk_stored qk_std at_turned at_exp
    at_copied at_out_hi fm_mm fm_hi_done y_t_done y_hi_done rsq_done g_hi_done gate_dve gate_act c_pad c_conv
    o_done c_silued c_sq Gb_mm Gb_exp d_diff d_exp nL_turned nLT_done lv_m1 lv_copied uw_mm uw_copied r_su r_oc
    o_sq o_std oa_hi_done m_tr m_T_done s_hi_done x_last y_turned dve_chain n_inv n_bc n_lo vec_tr tr_done
    ada_mod lat_gained lat_inv qk_mm qk_normed scl2_done at_scores at_prob at_out_lo fc_mm fc_copied fm_lo_done
    y_lo_done g_lo_done ab_turned gate_cum c_normed kv_turned k_scaled qd_done kk_mm nL_done inv0_done lv_mm
    lv_done r_init r_ws r_u r_st o_scaled o_turned oa_lo_done vb_turned vb_copied mv_turned mv_copied s_lo_done""".split()
    sem = {n: nc.alloc_semaphore(n) for n in names}
    bias_in = [nc.alloc_semaphore(f"bias_in{i}") for i in range(2)]
    w_in_slot = [nc.alloc_semaphore(f"w_in_slot{i}") for i in range(2)]
    bank_stored = [nc.alloc_semaphore(f"bank_stored{i}") for i in range(4)]

    def tile_count(u, j, loop=None):
        return val([x + j + 1 for x in tile_at], u, loop)

    def bank_of(u, j):
        return (tile_at[u] + j) % 4

    def bank(u, j):
        return ps[:, bank_of(u, j), :]

    def stored_count(u, j, loop=None):
        return val([(x + j) // 4 + 1 for x in tile_at], u, loop)

    def slot_before(u):
        old = [x for x in range(u) if units[x].split][-2:]
        return old[0] if len(old) == 2 else None

    shared_lo = list(range(first["mkv"] + 2, first["mkv"] + 8))

    def lo_half_count(u):
        return shared_lo.index(u) + 1

    def gated(name, kind, j):
        return first[name] + GATED.index((kind, j))

    N_X, N_CTX, N_2, N_MIX = 0, 1, 2, 3
    N_XATTN, N_MEM, N_FFN, N_FINAL = 20, 21, 22, 23
    NORM_INDEX = {N_X: 0, N_CTX: 1, N_2: 2, N_MIX: 3, N_XATTN: 4, N_MEM: 5, N_FFN: 6, N_FINAL: 7}
    SUM_BANK, BC_BANK = 4, 6

    items = [("one", h, q) for h in range(H1) for q in range(NT)]
    items += [("band", h, q) for h in range(HB) for q in range(NT)]
    items += [("mem", h, q) for h in range(HM) for q in range(NT)]
    ITEM = {x: n for n, x in enumerate(items)}
    ATT = {"one": (0, 32), "band0": (32, 64), "band1": (64, 96), "mem": (96, 112)}

    def keys_of(n):
        kind, h, q = items[n]
        return {"one": S + C, "band": (q + 1) * P, "mem": C}[kind]

    def out_group(n):
        if n < 96:
            return n // 8, n % 8 == 7
        return 12 + (n - 96) // 4, n % 4 == 3

    def out_tiles_before(n):
        return n // 8 if n < 96 else 12 + 2 * ((n - 96) // 4)

    rot = acc[:, 0:H1 * ROPE_W].rearrange("p (h a b c) -> p h a b c", h=H1, a=2, b=2)
    last_of = {}
    for name in first:
        later = [x for x in first.values() if x > first[name]]
        last_of[name] = min(later) if later else NU

    def score_bank(n):
        return 4 + n % 2 if items[n][0] == "band" else 2 * (n % 2)

    def turned_bank(n):
        return 7 if items[n][0] == "band" else 4

    def out_bank(n, j=0):
        kind, g = items[n][0], out_group(n)[0]
        return {"one": 6 + g % 2, "band": 6, "mem": 6 + j if g % 2 else 1 + 2 * j}[kind]

    def qk_bank(m):
        return 4 if m % 2 == 0 else 0

    qk_sq = sq2[:, :, :].rearrange("p a c -> p (a c)")[:, 0:H1 * QK1]

    with nc.Block() as block:
        @block.sync
        def _(sp):
            def wait_raw_slot(u, loop=None):
                if u < 2:
                    return
                if units[u - 2].split:
                    sp.wait_ge(sem["w_lo_done"], val(split_at, u - 2, loop) + 1)
                    if u - 2 in shared_lo:
                        sp.wait_ge(sem["w_lo_half"], lo_half_count(u - 2))
                elif u - 2 < first["ada_b"]:
                    sp.wait_ge(sem["ada_mm"], ada_units.index(u - 2) + 1)
                else:
                    sp.wait_ge(sem["ada_summed"], ada_units.index(u - 2) - 7)

            def load(u, loop=None, src=None):
                wait_raw_slot(u, loop)
                for got, off, k, c in units[u].loads:
                    dst = raw[:, u % 2, off:off + k * c].rearrange("p (k c) -> p k c", c=c)
                    sp.dma_start(dst, got if src is None else src).then_inc(w_in_slot[u % 2], 16)

            def load_phase(name):
                for u in range(first[name], last_of[name]):
                    load(u)

            sp.dma_start(vec_in[0:VEC_SPLIT, 0, :], t["vec"][0:VEC_SPLIT, :]).then_inc(sem["in_done"], 16)
            sp.dma_start(vec_in[0:VEC_N - VEC_SPLIT, 1, :], t["vec"][VEC_SPLIT:, :]).then_inc(sem["in_done"], 16)
            for u in range(first["merge1"]):
                load(u)
            sp.wait_ge(sem["at_out"], 32)
            sp.dma_start(dft[:, :], t["dft"]).then_inc(sem["dft_in"], 16)
            load_phase("merge1")
            load_phase("out1")
            u0_ = first["mlp"]
            for j in range(8):
                load(u0_ + j)
            with sp.Fori(0, 3) as i:
                for j in range(4):
                    load(u0_ + 8 + j, (i, 8), t["w_up"][:, bass.ds(i * D + (D + 256 * j), 256)]
                         .rearrange("(k p) c -> p k c", p=P))
                for j in range(4):
                    load(u0_ + 12 + j, (i, 8), t["w_down"][bass.ds(i * D + D, D), 256 * j:256 * j + 256]
                         .rearrange("(k p) c -> p k c", p=P))
            load_phase("ab")
            for u in range(first["pair0"], first["pair0"] + 2):
                load(u)
            sp.wait_ge(bank_stored[bank_of(first["mlp"] + 31, 1)], stored_count(first["mlp"] + 31, 1))
            sp.dma_start(masks[:, :, :], t["masks"].rearrange("p (m c) -> p m c", c=P)).then_inc(sem["masks_in"], 16)
            for u in range(first["pair0"] + 2, first["aout"]):
                load(u)
            load_phase("aout")
            for g in range(2):
                for u in range(first[f"band{g}"] + 4 * g, last_of[f"band{g}"] + 2):
                    load(u)
                for h in range(8 * g, 8 * g + 8):
                    if h == 8 * g + 2:
                        for u in range(last_of[f"band{g}"] + 2, last_of[f"band{g}"] + 4):
                            load(u)
                    if h >= 2:
                        sp.wait_ge(sem["at_max"], ITEM[("band", h - 2, NT - 1)] + 1)
                    else:
                        sp.wait_ge(bank_stored[bank_of(first["aout"] + 7, 1)], stored_count(first["aout"] + 7, 1))
                    sp.dma_start(bias_b[:, h % 2, :], t["bias_band"][h]).then_inc(bias_in[h % 2], 16)
            for u in range(first["bout"] + 4, last_of["bout"]):
                load(u)
            load_phase("out2")
            sp.wait_ge(sem["tile_done"], tile_count(first["bout"] + 7, 1))
            sp.dma_start(m_in[:, :, :], t["mem_2"].rearrange("(a p) c -> p a c", p=P)).then_inc(sem["m_in_done"], 16)
            for name in ("mq", "mkv", "mo"):
                load_phase(name)
            u0_ = first["gu"]
            for j in range(2):
                load(u0_ + j)
            with sp.Fori(0, 10) as i:
                for j in range(2):
                    load(u0_ + 2 + j, (i, 2), t["w_gate_up_2"][:, bass.ds(i * 256 + (256 + FF2 * j), 256)]
                         .rearrange("(k p) c -> p k c", p=P))
            u0_ = first["down2"]
            load(u0_)
            with sp.Fori(0, 5) as i:
                for j in range(2):
                    load(u0_ + 1 + j, (i, 2), t["w_down_2"][bass.ds(i * 512 + (256 + 256 * j), 256), :]
                         .rearrange("(k p) c -> p k c", p=P))
            for q in range(NT):
                sp.wait_ge(sem["y_copied"], q + 1)
                sp.dma_start(out[q * P:(q + 1) * P, 0:512], y_out[:, q, 0:512]).then_inc(sem["stored"], 16)
            for q in range(NT):
                if q < 2:
                    sp.wait_ge(sem["y_copied2"], q + 1)
                else:
                    sp.wait_ge(sem["y_copied"], NT + q - 1)
                sp.dma_start(out[q * P:(q + 1) * P, 512:1024], y_out[:, q, 512:1024]).then_inc(sem["stored"], 16)
            sp.wait_ge(sem["stored"], 16 * 2 * NT)

        @block.gpsimd
        def _(pool):
            def lower(u, loop=None):
                pool.wait_ge(sem["w_hi_done"], val(split_at, u, loop) + 1)
                n = UNIT if loop else units[u].n // 2 if u in shared_lo else units[u].n
                nc.gpsimd.tensor_tensor(w_lo[:, split_at[u] % 2, 0:n], raw[:, u % 2, 0:n],
                                        w_hi[:, split_at[u] % 2, 0:n].bitcast(F32),
                                        ALU.subtract).then_inc(sem["w_lo_done"], 1)

            def modulate(a):
                u, slot = first["ada_b"] + a, a % 8
                pool.wait_ge(w_in_slot[u % 2], load_count[u])
                pool.wait_ge(sem["c_silu"], 2)
                x = raw[:, u % 2, :].rearrange("p (k c) -> p k c", k=KT)
                chain = 3 * a

                def half(k, dst):
                    pool.wait_ge(sem["pool_chain"], chain + {4: 1, 2: 2, 1: 3}[k])
                    return nc.gpsimd.tensor_tensor(dst, x[:, 0:k, :], x[:, k:2 * k, :], ALU.add)

                nc.gpsimd.tensor_tensor(x, x, over_width(silu_c[:, :, 0], 256), ALU.mult).then_inc(sem["pool_chain"], 1)
                half(4, x[:, 0:4, :]).then_inc(sem["pool_chain"], 1)
                half(2, x[:, 0:2, :]).then_inc(sem["pool_chain"], 1)
                if a >= 8:
                    pool.wait_ge(sem["ada_batch"], 1)
                half(1, ada_sum[:, slot:slot + 1, :]).then_inc(sem["ada_summed"], 1)

            u = 0
            while u < NU:
                if u == first["ada_b"]:
                    for a in range(16):
                        modulate(a)
                    u += 16
                    continue
                if u == first["mlp"] + 8:
                    with pool.Fori(0, 3) as i:
                        for j in range(8):
                            lower(u + j, (i, 8))
                    u += 24
                    continue
                if u == first["gu"] + 2:
                    with pool.Fori(0, 10) as i:
                        for j in range(2):
                            lower(u + j, (i, 2))
                    u += 20
                    continue
                if u == first["down2"] + 1:
                    with pool.Fori(0, 5) as i:
                        for j in range(2):
                            lower(u + j, (i, 2))
                    u += 10
                    continue
                if units[u].split:
                    lower(u)
                if u in (last_of["band0"] + 1, last_of["band1"] + 1):
                    g = int(u > last_of["band1"])
                    for h in range(8 * g, 8 * g + 8):
                        pool.wait_ge(bias_in[h % 2], 16 * (h // 2 + 1))
                        nc.gpsimd.memset(bias_b[0:CHUNK, h % 2, S - CHUNK:S], -1e30).then_inc(sem["bias_ready"], 1)
                u += 1

        @block.scalar
        def _(act):
            split_units = [u for u in range(NU) if units[u].split]
            turn = [0]

            def hi_of(u, loop=None):
                act.wait_ge(w_in_slot[u % 2], val(load_count, u, loop))
                old = slot_before(u)
                if old is not None and units[old].kind == "down2":
                    act.wait_ge(sem["w_mm_done"], old - first["down2"] + 1)
                elif old is not None:
                    act.wait_ge(sem["tile_done"], val(tile_at, old + 1, loop))
                n = UNIT if loop else units[u].n
                nc.scalar.activation(w_hi[:, split_at[u] % 2, 0:n], raw[:, u % 2, 0:n],
                                     ACT.Copy).then_inc(sem["w_hi_done"], 1)

            def next_hi():
                if turn[0] < len(split_units):
                    hi_of(split_units[turn[0]])
                    turn[0] += 1

            def link(ins):
                ins.then_inc(sem["act_chain"], 1)
                chain[0] += 1
                act.wait_ge(sem["act_chain"], chain[0])

            chain = [0]

            def store_tile(u, j, dst, func=ACT.Copy, rows=P, cols=S, loop=None, **kw):
                act.wait_ge(sem["tile_done"], tile_count(u, j, loop))
                p = bank(u, j)
                nc.scalar.activation(dst, p[0:rows, 0:cols], func, **kw).then_inc(bank_stored[bank_of(u, j)], 1)

            def squares(n, k, src):
                i = NORM_INDEX[n]
                before = 7 * i + (max(1, k - 2) if k >= 2 else 0)
                if before:
                    act.wait_ge(sem["n_acc"], before)
                nc.scalar.activation(sq2[:, k % 2, 0:src.shape[1]], src, ACT.Square).then_inc(sem["n_sq"], 1)

            def std_of(g, scale, nt=NT):
                act.wait_ge(sem["n_sum"], g + 1)
                nc.scalar.activation(stat[:, g % 2, 0, 0:nt], ps[:, SUM_BANK + g % 2, 0:nt * P:P], ACT.Sqrt,
                                     bias=one_eps[:, 0:1], scale=scale).then_inc(sem["n_std"], 1)

            def norm_hi(n, dst, shift, tiles=range(KT)):
                i = NORM_INDEX[n]
                for k in tiles:
                    act.wait_ge(sem["n_t"], 8 * i + k + 1)
                    w = dst.shape[2]
                    if shift is None:
                        nc.scalar.activation(dst[:, k, :], tmp2[:, k % 2, 0:w], ACT.Copy).then_inc(sem["n_hi"], 1)
                    else:
                        nc.scalar.activation(dst[:, k, :], tmp2[:, k % 2, 0:w], ACT.Identity,
                                             bias=shift(k)).then_inc(sem["n_hi"], 1)

            act.dma_start(const[:, :], t["const"]).then_inc(sem["const_done"], 16)
            act.dma_start(x_in[:, :, :], t["x"].rearrange("(a p) c -> p a c", p=P)).then_inc(sem["x_in_done"], 16)
            act.dma_start(c_in[:, :, :], t["ctx"].rearrange("(a p) c -> p a c", p=P)).then_inc(sem["c_in_done"], 16)
            act.dma_start(bc[:, :], t["bc"]).then_inc(sem["bc_done"], 16)
            act.dma_start(rope[:, :, :, :].rearrange("p a b c -> p (a b c)"), t["rope"]).then_inc(sem["rope_done"], 16)
            act.dma_start(w_qb[:, :, :], t["w_qb"].rearrange("(k p) c -> p k c", p=P)).then_inc(sem["wq_done"], 16)
            act.dma_start(w_kvb[:, :], t["w_kvb"]).then_inc(sem["wkv_done"], 16)
            act.wait_ge(sem["vec_done"], 1)
            for i, name in enumerate(("c", "c_ctx")):
                nc.scalar.activation(silu_c[:, :, i], vecT[:, VEC_AT[name]:VEC_AT[name] + KT], ACT.Silu).then_inc(sem["c_silu"], 1)
            for k in range(KT):
                act.wait_ge(sem["xt_done"], k + 1)
                squares(N_X, k, xT[:, k, :])
            for k in range(KT):
                act.wait_ge(sem["ctx_tr"], k + 1)
                nc.scalar.activation(cT[:, k, :], ps[:, 4 + k % 4, 0:C], ACT.Copy).then_inc(sem["ctx_t"], 1)

            def ada_rows(a):
                act.wait_ge(sem["ada_mm"], a + 1)
                if a >= 2:
                    act.wait_ge(sem["ada_tr"], a - 1)
                nc.scalar.activation(ada_row[:, a % 2, :], ps[0:2, a % 2, 0:256], ACT.Copy).then_inc(sem["ada_rowed"], 1)

            for a in range(8):
                ada_rows(a)
                if a == 1:
                    for k in range(KT):
                        act.wait_ge(sem["ctx_t"], k + 1)
                        squares(N_CTX, k, cT[:, k, :])
                if a == 2:
                    act.wait_ge(sem["one_eps_done"], 1)
                    std_of(N_X, 1.0 / D)
                if a == 3:
                    std_of(N_CTX, 1.0 / D, 2)
                if a == 4:
                    next_hi()
                if a >= 5:
                    act.wait_ge(sem["ada_mod"], a)
                    norm_hi(N_X, h_hi, lambda k: mod[:, k, 0:1], range(2 * (a - 5), 2 * (a - 4)))
            act.wait_ge(sem["ada_mod"], 8)
            norm_hi(N_X, h_hi, lambda k: mod[:, k, 0:1], range(6, KT))
            next_hi()
            norm_hi(N_CTX, c_hi, lambda k: mod[:, k, 1:2])

            u, v = first["lat_q"], first["lat_kv"]
            for j in range(2):
                store_tile(u, j, lat_q[:, j, :])
            store_tile(v, 0, lat_kv[:, 0:S])
            store_tile(v, 1, kr_T[:, 0:S], rows=ROPE_W)
            store_tile(v, 2, lat_kv[:, S:S + C], cols=C)
            store_tile(v, 3, kr_T[:, S:S + C], rows=ROPE_W, cols=C)
            for j in range(2):
                act.wait_ge(bank_stored[bank_of(u, j)], stored_count(u, j))
                nc.scalar.activation(sq_q[:, j, :], lat_q[:, j, :], ACT.Square).then_inc(sem["lat_sq"], 1)
            act.wait_ge(bank_stored[bank_of(v, 0)], stored_count(v, 0))
            act.wait_ge(bank_stored[bank_of(v, 2)], stored_count(v, 2))
            nc.scalar.activation(sq_kv[:, :], lat_kv[:, :], ACT.Square).then_inc(sem["lat_sq"], 1)
            act.wait_ge(sem["lat_ss"], 1)
            nc.scalar.activation(lat_stat[:, 0, 0:4], ps[:, 4, 0:4], ACT.Sqrt, bias=one_eps[:, 0:1], scale=1.0 / Q_LORA)
            nc.scalar.activation(lat_stat[:, 0, 4:10], ps[:, 4, 4:10], ACT.Sqrt, bias=one_eps[:, 0:1],
                                 scale=1.0 / KV_LORA).then_inc(sem["lat_std"], 1)
            act.wait_ge(sem["kr_mm"], 1)
            nc.scalar.activation(kr_tok[:, :, :].rearrange("p a c -> p (a c)"), ps[:, 5, 0:6 * ROPE_W],
                                 ACT.Copy).then_inc(sem["kr_copied"], 1)

            def v_and_square(m):
                banks = ps[:, qk_bank(m):qk_bank(m) + 2, :]
                act.wait_ge(sem["qk_mm"], m + 1)
                if m == 0:
                    act.wait_ge(sem["lat_inv"], 1)
                if m >= 2:
                    act.wait_ge(sem["qk_turned"], m - 1)
                if m < 6:
                    kv = banks.rearrange("p b (h c) -> p (b h) c", c=P)
                    nc.scalar.activation(qk_tok[:, m % 2, :, 0:NOPE], kv[:, :, 0:NOPE], ACT.Copy,
                                         scale=lat_stat[:, 1, 4 + m:5 + m]).then_inc(sem["qk_scaled"], 1)
                    nc.scalar.activation(v1[:, m, :].rearrange("p (h c) -> p h c", c=V1), kv[:, :, NOPE:P], ACT.Copy,
                                         scale=lat_stat[:, 1, 4 + m:5 + m]).then_inc(sem["v_scaled"], 1)
                    act.wait_ge(sem["kr_put"], m + 1)
                else:
                    nc.scalar.activation(qk_tok[:, m % 2, :, :].rearrange("p (b h) c -> p b (h c)", b=2),
                                         banks[:, :, 0:384], ACT.Copy,
                                         scale=lat_stat[:, 1, m - 6:m - 5]).then_inc(sem["qk_scaled"], 1)
                act.wait_ge(sem["qk_scaled"], m + 1)
                if m >= 1:
                    act.wait_ge(sem["qk_summed"], m)
                nc.scalar.activation(qk_sq, qk_tok[:, m % 2, :, :].rearrange("p h c -> p (h c)"),
                                     ACT.Square).then_inc(sem["qk_squared"], 1)

            def store_qk(m):
                dst = kT[:, :, m * P:(m + 1) * P] if m < 6 else qT[:, :, (m - 6) * P:(m - 5) * P]
                act.wait_ge(sem["qk_turned"], m + 1)
                nc.scalar.activation(dst, ps[0:QK1, 6:8, :].rearrange("p b (h c) -> p (b h) c", c=P),
                                     ACT.Copy).then_inc(sem["qk_stored"], 1)

            v_and_square(0)
            for m in range(10):
                act.wait_ge(sem["qk_summed"], m + 1)
                nc.scalar.activation(qk_stat[:, m % 2, 1, :], qk_stat[:, m % 2, 0, :], ACT.Sqrt, bias=one_eps[:, 0:1],
                                     scale=1.0 / QK1).then_inc(sem["qk_std"], 1)
                if m < 9:
                    v_and_square(m + 1)
                store_qk(m)

            def attention(kind, prob, probT, scale, dst_hi, hi_at=()):
                a, b = ATT[kind]

                def expo(n):
                    nk = keys_of(n)
                    src = score_b[:, n % 2, 0:nk] if items[n][0] == "band" else \
                        ps[:, score_bank(n):score_bank(n) + 2, :].rearrange("p b c -> p (b c)")[:, 0:nk]
                    act.wait_ge(sem["at_max"], n + 1)
                    if n >= 2:
                        act.wait_ge(sem["at_turned"], n - 1)
                    nc.scalar.activation(prob[:, n % 2, 0:nk], src, ACT.Exp, bias=at_stat[:, n % 4, 1:2], scale=scale,
                                         accum_out=at_stat[:, n % 4, 2:3]).then_inc(sem["at_exp"], 1)

                def copy(n):
                    nk = keys_of(n)
                    act.wait_ge(sem["at_turned"], n + 1)
                    if n >= 2:
                        act.wait_ge(sem["at_out"], n - 1)
                    at_ = turned_bank(n) * 512
                    nc.scalar.activation(probT[:, n % 2, 0:nk],
                                         ps[:, :, :].rearrange("p b c -> p (b c)")[:, at_:at_ + nk],
                                         ACT.Copy).then_inc(sem["at_copied"], 1)

                def out_hi(n):
                    g, last = out_group(n)
                    if last:
                        act.wait_ge(sem["at_out"], n + 1)
                        if kind == "mem":
                            for j in range(2):
                                nc.scalar.activation(dst_hi[:, 2 * (g - 12) + j, :], ps[:, out_bank(n, j), :],
                                                     ACT.Copy).then_inc(sem["at_out_hi"], 1)
                        else:
                            nc.scalar.activation(dst_hi[:, g - (4 if kind != "one" else 0), :], ps[:, out_bank(n), :],
                                                 ACT.Copy).then_inc(sem["at_out_hi"], 1)

                expo(a)
                expo(a + 1)
                for n in range(a, b):
                    copy(n)
                    if n + 2 < b:
                        expo(n + 2)
                    if n > a:
                        out_hi(n - 1)
                    if n - a in hi_at:
                        next_hi()
                out_hi(b - 1)

            attention("one", prob1, probT1, QK1 ** -0.5, at_hi, (20, 25))

            for j in range(2):
                for jj in range(2):
                    store_tile(first["f"] + j, jj, f_T[:, 2 * j + jj, :])
                next_hi()
            for g in range(4):
                act.wait_ge(sem["fm_mm"], g + 1)
                nc.scalar.activation(fm_hi[:, g, :], ps[:, 4 + g, :], ACT.Copy).then_inc(sem["fm_hi_done"], 1)

            for j in range(4):
                u = first["merge1"] + 3 * j
                for part in range(2):
                    for jj in range(2):
                        if j >= 2:
                            act.wait_ge(bank_stored[bank_of(u - 6 + 2, 2 * part + jj)], stored_count(u - 6 + 2, 2 * part + jj))
                        store_tile(u + part, jj, sig1[:, j % 2, 2 * part + jj, :], ACT.Sigmoid,
                                   bias=col("b_gate", 8 * part + 2 * j + jj))
                    next_hi()
                for jj in range(2):
                    act.wait_ge(sem["y_t_done"], 2 * j + jj + 1)
                    nc.scalar.activation(y_hi[:, 2 * j + jj, :], tmp2[:, jj, :], ACT.Copy).then_inc(sem["y_hi_done"], 1)
                next_hi()

            def out_phase(name, n):
                for j in range(4):
                    for jj in range(2):
                        if jj == 0:
                            act.wait_ge(sem["tile_done"], tile_count(first[name] + j, 1))
                            next_hi()
                        act.wait_ge(bank_stored[bank_of(first[name] + j, jj)], stored_count(first[name] + j, jj))
                        squares(n, 2 * j + jj, xT[:, 2 * j + jj, :])

            out_phase("out1", N_2)
            std_of(N_2, 1.0 / D)
            norm_hi(N_2, h_hi, lambda k: mod[:, 24 + k, 0:1])

            def mlp_chunk(u0_, count0, loop=None, last=False):
                for j in range(4):
                    for jj in range(2):
                        q = 2 * j + jj
                        if not (isinstance(count0, int) and count0 + q < 2):
                            act.wait_ge(sem["rsq_done"], count0 + (q - 1))
                        store_tile(u0_ + j, jj, relu[:, jj, :], ACT.Relu, loop=loop)
                    for jj in range(2):
                        q = 2 * j + jj
                        act.wait_ge(sem["rsq_done"], count0 + (q + 1))
                        nc.scalar.activation(g_hi[:, q, :], rsq[:, jj, :], ACT.Copy).then_inc(sem["g_hi_done"], 1)
                    hi_of(u0_ + j + 2, loop)
                for j in range(4):
                    act.wait_ge(sem["tile_done"], tile_count(u0_ + 4 + j, 1, loop))
                    hi_of(u0_ + 4 + j + 2, loop)
                    for jj in range(2 if last else 0):
                        act.wait_ge(bank_stored[bank_of(u0_ + 4 + j, jj)], stored_count(u0_ + 4 + j, jj))
                        squares(N_MIX, 2 * j + jj, xT[:, 2 * j + jj, :])

            mlp_chunk(first["mlp"], 0)
            with act.Fori(0, 2) as i:
                mlp_chunk(first["mlp"] + 8, i * 8 + 8, (i, 8))
            mlp_chunk(first["mlp"] + 24, 24, last=True)
            turn[0] = split_units.index(first["pair0"] + 1)
            std_of(N_MIX, 1.0 / D)
            norm_hi(N_MIX, h_hi, None)

            store_tile(first["ab"], 0, ab_T[:, :], rows=16)
            next_hi()
            act.wait_ge(sem["gate_dve"], 1)
            nc.scalar.activation(gp[:, 6, :, :], gp[:, 9, :, :], ACT.Sigmoid)
            link(nc.scalar.activation(gp[:, 1, :, :], gp[:, 0, :, :], ACT.Abs))
            link(nc.scalar.activation(gp[:, 2, :, :], gp[:, 1, :, :], ACT.Exp, scale=-1.0))
            nc.scalar.activation(gp[:, 3, :, :], gp[:, 2, :, :], ACT.Ln, bias=one_eps[:, 1:2])
            nc.scalar.activation(gp[:, 10, 0, :], bc[:, 2 * QK1 + HA:2 * QK1 + 2 * HA], ACT.Exp).then_inc(sem["gate_act"], 1)

            def pair_qkv(p, kind):
                for a in range(2):
                    if p:
                        act.wait_ge(sem["c_conv"], 6 * p)
                    store_tile(first[f"pair{p}"] + kind, a, pad_in[:, 2 * kind + a, 3:3 + S])
                next_hi()

            for p in range(4):
                u = first[f"pair{p}"]
                if p == 0:
                    act.wait_ge(sem["c_pad"], 1)
                    pair_qkv(p, 0)
                    act.wait_ge(sem["gate_dve"], 3)
                    nc.scalar.activation(gp[:, 10, :, :], gp[:, 5, :, :], ACT.Exp)
                    nc.scalar.activation(gp[:, 8, :, :], gp[:, 9, :, :], ACT.Exp).then_inc(sem["gate_act"], 1)
                    pair_qkv(p, 1)
                    pair_qkv(p, 2)

                def silu(j):
                    act.wait_ge(sem["c_conv"], 6 * p + j + 1)
                    nc.scalar.activation(conv[:, j, :], conv[:, j, :], ACT.Silu).then_inc(sem["c_silued"], 1)

                def square(j):
                    act.wait_ge(sem["c_silued"], 6 * p + j + 1)
                    act.wait_ge(sem["n_sum"], 4 + 4 * p + j - 1)
                    nc.scalar.activation(sq2[:, j % 2, :], conv[:, j, :], ACT.Square).then_inc(sem["c_sq"], 1)

                for j in range(4):
                    silu(j)
                square(0)
                square(1)
                silu(4)
                silu(5)
                std_of(4 + 4 * p, 1.0)
                square(2)
                std_of(5 + 4 * p, 1.0)
                square(3)
                std_of(6 + 4 * p, 1.0)
                std_of(7 + 4 * p, 1.0)
                for a in range(2):
                    if p:
                        act.wait_ge(sem["o_done"], 2 * p)
                    store_tile(u + 3, a, z_s[:, a, :], ACT.Silu)
                next_hi()
                for a in range(2):
                    h = 2 * p + a
                    act.wait_ge(sem["Gb_mm"], h + 1)
                    nc.scalar.activation(eGb[:, a, :], ps[:, 4 + a, :], ACT.Exp).then_inc(sem["Gb_exp"], 1)
                    act.wait_ge(sem["d_diff"], h + 1)
                    nc.scalar.activation(decay[:, a, :, :], decay[:, a, :, :], ACT.Exp, scale=-1.0).then_inc(sem["d_exp"], 1)
                for a in range(2):
                    for i, dst in enumerate((nLT, prT)):
                        act.wait_ge(sem["nL_turned"], 4 * p + 2 * a + i + 1)
                        nc.scalar.activation(dst[:, a, :, :].rearrange("p t c -> p (t c)"), ps[:, (6 if i == 0 else 4) + a, :],
                                             ACT.Copy).then_inc(sem["nLT_done"], 1)
                for s in range(1, LEVELS):
                    for a in range(2):
                        n = (p * 5 + s - 1) * 2 + a
                        act.wait_ge(sem["lv_m1"], n + 1)
                        nc.scalar.activation(prod[:, a, :, :].rearrange("p t c -> p (t c)"), ps[:, 6 + a, :],
                                             ACT.Copy).then_inc(sem["lv_copied"], 1)
                for a in range(2):
                    for i, dst in enumerate((u0[:, a, :, :].rearrange("p t c -> p (t c)"), wT[:, a, :])):
                        act.wait_ge(sem["uw_mm"], 4 * p + 2 * a + i + 1)
                        nc.scalar.activation(dst, ps[:, 4 + 2 * i + a, :], ACT.Copy).then_inc(sem["uw_copied"], 1)
                if p < 3:
                    pair_qkv(p + 1, 0)
                else:
                    next_hi()
                for tt in range(NT):
                    act.wait_ge(sem["r_su"], 8 * p + 2 * tt + 2)
                    nc.scalar.activation(o_tok[:, :, tt, :], ps[:, 5 + 2 * (tt % 2), 0:2 * P].rearrange("p (a c) -> p a c", a=2),
                                         ACT.Copy).then_inc(sem["r_oc"], 1)
                    if tt == 1 and p < 3:
                        pair_qkv(p + 1, 1)
                    elif tt == 2 and p == 3:
                        next_hi()
                    elif p == 3 and tt in (0, 1):
                        act.wait_ge(sem["o_done"], 6)
                        for k in range(3 * tt, 3 * tt + 3):
                            nc.scalar.activation(oa_hi[:, k, :], oaT[:, k, :], ACT.Copy).then_inc(sem["oa_hi_done"], 1)
                if p < 3:
                    pair_qkv(p + 1, 2)
                act.wait_ge(sem["o_sq"], p + 1)
                nc.scalar.activation(o_stat[:, 1, :], o_stat[:, 0, :], ACT.Sqrt, bias=one_eps[:, 0:1],
                                     scale=1.0 / P).then_inc(sem["o_std"], 1)

            for k in range(6, HA):
                act.wait_ge(sem["o_done"], k + 1)
                nc.scalar.activation(oa_hi[:, k, :], oaT[:, k, :], ACT.Copy).then_inc(sem["oa_hi_done"], 1)

            def gated_out(name):
                for n, (kind, j) in enumerate(GATED):
                    for jj in range(2):
                        if kind == "sig":
                            if j >= 2:
                                old = gated(name, "proj", j - 2)
                                act.wait_ge(bank_stored[bank_of(old, jj)], stored_count(old, jj))
                            store_tile(first[name] + n, jj, sig2[:, j % 2, jj, :], ACT.Sigmoid)
                    if n >= 2:
                        act.wait_ge(sem["tile_done"], tile_count(first[name] + n, 1))
                        next_hi()

            gated_out("aout")

            for g in range(2):
                for kind, dst in enumerate((qbT, kbT, vbT)):
                    for j in range(2):
                        for jj in range(2):
                            store_tile(first[f"band{g}"] + 2 * kind + j, jj, dst[:, 2 * j + jj, :])
                        if g == 0 or kind:
                            next_hi()
                attention(f"band{g}", prob_b, probT_b, 1.0, ob_hi, (14, 29))
            gated_out("bout")
            for k in range(KT):
                act.wait_ge(sem["y_t_done"], 8 + k + 1)
                act.wait_ge(sem["tile_done"], tile_count(first["bout"] + 7, 1))
                nc.scalar.activation(h_hi[:, k, :], y2[:, k, :], ACT.Copy).then_inc(sem["y_hi_done"], 1)
            out_phase("out2", N_XATTN)
            std_of(N_XATTN, 1.0 / D)
            norm_hi(N_XATTN, h_hi, None)

            for j in range(4):
                if j == 3:
                    for k in range(KT):
                        act.wait_ge(sem["m_T_done"], k + 1)
                        squares(N_MEM, k, m_T[:, k, :])
                    std_of(N_MEM, 1.0 / D, 2)
                for jj in range(2):
                    store_tile(first["mq"] + j, jj, m_q[:, 2 * j + jj, :])
                next_hi()
                for k in {1: range(4), 2: range(4, KT)}.get(j, ()):
                    act.wait_ge(sem["m_tr"], k + 1)
                    nc.scalar.activation(m_T[:, k, :], ps[:, 4 + k % 4, 0:C], ACT.Copy).then_inc(sem["m_T_done"], 1)
            norm_hi(N_MEM, m_hi, None)
            for j in range(8):
                for jj in range(2):
                    k = 2 * j + jj
                    store_tile(first["mkv"] + j, jj, m_kT[:, k, :] if k < 8 else m_vT[:, k - 8, :], cols=C)
                next_hi()
            attention("mem", prob_m, probT_m, 256 ** -0.5, om_hi)
            out_phase("mo", N_FFN)
            std_of(N_FFN, 1.0 / D)
            norm_hi(N_FFN, h_hi, None)

            def gu_round(u0_, count0, loop=None):
                for jj in range(2):
                    if loop:
                        act.wait_ge(bank_stored[bank_of(u0_ - 1, jj)], stored_count(u0_ - 1, jj, loop))
                    store_tile(u0_, jj, gate[:, jj, :], ACT.Silu, loop=loop)
                hi_of(u0_ + 2, loop)
                for jj in range(2):
                    act.wait_ge(bank_stored[bank_of(u0_ + 1, jj)], stored_count(u0_ + 1, jj, loop))
                    f = s_hi[:, :, :].rearrange("p k c -> p (k c)")
                    dst = f[:, jj * S:(jj + 1) * S] if loop is None else f[:, bass.ds(loop[0] * (2 * S) + (2 + jj) * S, S)]
                    nc.scalar.activation(dst, gu[:, jj, :], ACT.Copy).then_inc(sem["s_hi_done"], 1)
                hi_of(u0_ + 3, loop)

            gu_round(first["gu"], 0)
            with act.Fori(0, 10) as i:
                gu_round(first["gu"] + 2, i * 2 + 2, (i, 2))
            for j in range(2, 11):
                hi_of(first["down2"] + j)
            for k in range(KT):
                act.wait_ge(sem["x_last"], k + 1)
                squares(N_FINAL, k, xT[:, k, :])
            std_of(N_FINAL, 1.0 / D)
            for q in range(NT):
                act.wait_ge(sem["y_turned"], q + 1)
                nc.scalar.activation(y_out[:, q, 0:512], ps[:, q, :], ACT.Copy).then_inc(sem["y_copied"], 1)
            for q in range(2, NT):
                act.wait_ge(sem["y_turned"], NT + q + 1)
                nc.scalar.activation(y_out[:, q, 512:1024], ps[:, q, :], ACT.Copy).then_inc(sem["y_copied"], 1)

        @block.vector
        def _(dve):
            chain = [0]

            def link(ins):
                ins.then_inc(sem["dve_chain"], 1)
                chain[0] += 1
                dve.wait_ge(sem["dve_chain"], chain[0])

            V = nc.vector

            def add_square(n, k, w=S):
                i = NORM_INDEX[n]
                if k == 0:
                    return
                dve.wait_ge(sem["n_sq"], 8 * i + k + 1)
                if k == 1:
                    if i:
                        dve.wait_ge(sem["n_sum"], n)
                    V.tensor_tensor(acc[:, 0:w], sq2[:, 0, 0:w], sq2[:, 1, 0:w], ALU.add).then_inc(sem["n_acc"], 1)
                else:
                    dve.wait_ge(sem["n_acc"], 7 * i + k - 1)
                    V.tensor_tensor(acc[:, 0:w], acc[:, 0:w], sq2[:, k % 2, 0:w], ALU.add).then_inc(sem["n_acc"], 1)

            def inverse_of(g, nt=NT):
                dve.wait_ge(sem["n_std"], g + 1)
                V.reciprocal(stat[:, g % 2, 1, 0:nt], stat[:, g % 2, 0, 0:nt]).then_inc(sem["n_inv"], 1)

            def normed(n, src, gain, lo, hi, shift, w=S, before_lower=None):
                i = NORM_INDEX[n]
                dve.wait_ge(sem["n_bc"], n + 1)

                def scaled(k):
                    before = 8 * i + max(k - 1, 0)
                    if before:
                        dve.wait_ge(sem["n_hi"], before)
                        dve.wait_ge(sem["n_lo"], before)
                    V.scalar_tensor_tensor(tmp2[:, k % 2, 0:w], src[:, k, :], gain(k), ps[:, BC_BANK + n % 2, 0:w],
                                           ALU.mult, ALU.mult).then_inc(sem["n_t"], 1)

                def lower(k):
                    if before_lower:
                        before_lower(k)
                    dve.wait_ge(sem["n_hi"], 8 * i + k + 1)
                    if shift is None:
                        V.tensor_tensor(lo[:, k, :], tmp2[:, k % 2, 0:w], hi[:, k, :].bitcast(F32),
                                        ALU.subtract).then_inc(sem["n_lo"], 1)
                    else:
                        V.scalar_tensor_tensor(lo[:, k, :], tmp2[:, k % 2, 0:w], shift(k), hi[:, k, :].bitcast(F32),
                                               ALU.add, ALU.subtract).then_inc(sem["n_lo"], 1)

                scaled(0)
                for k in range(KT):
                    if k + 1 < KT:
                        scaled(k + 1)
                    lower(k)

            V.memset(one_eps[:, 0:1], EPS)
            V.memset(one_eps[:, 1:2], 1.0).then_inc(sem["one_eps_done"], 1)
            dve.wait_ge(sem["vec_tr"], 1)
            V.tensor_copy(vecT[:, 0:VEC_SPLIT], ps[:, 4, 0:VEC_SPLIT])
            V.tensor_copy(vecT[:, VEC_SPLIT:VEC_N], ps[:, 4, VEC_SPLIT:VEC_N]).then_inc(sem["vec_done"], 1)

            for k in range(KT):
                dve.wait_ge(sem["tr_done"], k + 1)
                V.tensor_copy(xT[:, k, :], ps[:, 4 + k % 4, :]).then_inc(sem["xt_done"], 1)
            for k in range(KT):
                add_square(N_X, k)
            for k in range(KT):
                add_square(N_CTX, k, C)

            def ada_cols(a):
                b = ADA_BLOCK[a]
                dve.wait_ge(sem["ada_tr"], a + 1)
                if a == 0:
                    dve.wait_ge(sem["vec_done"], 1)
                bias = vecT[:, VEC_AT["ada_b"] + 2 * b:VEC_AT["ada_b"] + 2 * b + 2]
                V.tensor_tensor(mod[:, 2 * b:2 * b + 2, :], ps[:, 2 + a % 2, 0:4].rearrange("p (j i) -> p j i", i=2),
                                over_width(bias, 2), ALU.add).then_inc(sem["ada_mod"], 1)

            def shifts_of(k):
                if k % 2 == 0:
                    ada_cols(4 + k // 2)
                    dve.wait_ge(sem["ada_mod"], 5 + k // 2)

            for a in range(4):
                ada_cols(a)
                if a == 2:
                    inverse_of(N_X)
            inverse_of(N_CTX, 2)
            dve.wait_ge(sem["ada_mod"], 4)
            for i in range(2):
                ins = V.scalar_tensor_tensor(scl[:, i, :], mod[:, 8:16, i], 1.0,
                                             vecT[:, VEC_AT["norm1_g"]:VEC_AT["norm1_g"] + KT], ALU.add, ALU.mult)
            link(ins)
            normed(N_X, xT, lambda k: scl[:, 0, k:k + 1], h_lo, h_hi, lambda k: mod[:, k, 0:1], before_lower=shifts_of)
            normed(N_CTX, cT, lambda k: scl[:, 1, k:k + 1], c_lo, c_hi, lambda k: mod[:, k, 1:2], C)

            for j in range(2):
                dve.wait_ge(sem["lat_sq"], j + 1)
                V.tensor_scalar(lat_q[:, j, :], lat_q[:, j, :], col("q_norm_g", j), None, ALU.mult).then_inc(sem["lat_gained"], 1)
            dve.wait_ge(sem["lat_sq"], 3)
            V.tensor_scalar(lat_kv[:, :], lat_kv[:, :], col("kv_norm_g"), None, ALU.mult).then_inc(sem["lat_gained"], 1)
            dve.wait_ge(sem["lat_std"], 1)
            V.reciprocal(lat_stat[:, 1, :], lat_stat[:, 0, :]).then_inc(sem["lat_inv"], 1)

            def put_kr(m):
                if m == 0:
                    dve.wait_ge(sem["kr_copied"], 1)
                    dve.wait_ge(sem["bc_done"], 16)
                    dve.wait_ge(sem["rope_done"], 16)
                if m >= 2:
                    dve.wait_ge(sem["qk_turned"], m - 1)
                V.tensor_copy(qk_tok[:, m % 2, :, NOPE:QK1],
                              kr_tok[:, m, :].unsqueeze(1).broadcast_to([P, H1, ROPE_W])).then_inc(sem["kr_put"], 1)

            def norm_qk(m):
                x = qk_tok[:, m % 2, :, :]
                dve.wait_ge(sem["qk_squared"], m + 1)
                if m >= 2:
                    dve.wait_ge(sem["qk_std"], m - 1)
                V.tensor_reduce(qk_stat[:, m % 2, 0, :], qk_sq.rearrange("p (h c) -> p h c", c=QK1), AX.X,
                                ALU.add).then_inc(sem["qk_summed"], 1)
                if m < 5:
                    put_kr(m + 1)
                dve.wait_ge(sem["qk_std"], m + 1)
                link(V.reciprocal(qk_stat[:, m % 2, 2, :], qk_stat[:, m % 2, 1, :]))
                link(V.tensor_tensor(x, x, over_width(qk_stat[:, m % 2, 2, :], QK1), ALU.mult))
                gain = bc[:, QK1:2 * QK1] if m < 6 else bc[:, 0:QK1]
                ins = V.tensor_tensor(x, x, gain.unsqueeze(1).broadcast_to([P, H1, QK1]), ALU.mult)
                if m in (4, 5):
                    ins.then_inc(sem["qk_normed"], 1)
                    return
                link(ins)
                tile = m if m < 6 else m - 6
                part = x[:, :, NOPE:QK1].rearrange("p h (a b c) -> p h a b c", a=2, b=2)
                sin = rope[:, tile, 1, :].rearrange("p (a b c) -> p a b c", a=2, b=2)
                for b in range(2):
                    ins = V.tensor_tensor(rot[:, :, :, b, :], part[:, :, :, 1 - b, :],
                                          sin[:, :, b, :].unsqueeze(1).broadcast_to([P, H1, 2, 8]), ALU.mult)
                link(ins)
                rp = x[:, :, NOPE:QK1]
                link(V.tensor_tensor(rp, rp, rope[:, tile, 0, :].unsqueeze(1).broadcast_to([P, H1, ROPE_W]), ALU.mult))
                V.tensor_tensor(rp, rp, acc[:, 0:H1 * ROPE_W].rearrange("p (h c) -> p h c", c=ROPE_W),
                                ALU.add).then_inc(sem["qk_normed"], 1)

            put_kr(0)
            for m in range(10):
                norm_qk(m)

            def modulation(b):
                at_ = 16 + 16 * b
                dve.wait_ge(sem["ada_batch"], b + 1)
                V.tensor_tensor(mod[:, at_:at_ + 16, 0], ps[:, 2 + 2 * b, 0:16],
                                vecT[:, VEC_AT["ada_b"] + at_:VEC_AT["ada_b"] + at_ + 16],
                                ALU.add).then_inc(sem["ada_mod"], 1)

            modulation(0)

            def attention(kind, prob, scale, dst_hi, dst_lo):
                a, b = ATT[kind]

                def maximum(n):
                    nk = keys_of(n)
                    dve.wait_ge(sem["at_scores"], n + 1)
                    src = ps[:, :, :].rearrange("p b c -> p (b c)")[:, score_bank(n) * 512:score_bank(n) * 512 + nk]
                    if items[n][0] == "band":
                        _, h, q = items[n]
                        dve.wait_ge(sem["bias_ready"], h + 1)
                        if n >= 2:
                            dve.wait_ge(sem["at_exp"], n - 1)
                        link(V.scalar_tensor_tensor(score_b[:, n % 2, 0:nk], src, DB ** -0.5, bias_b[:, h % 2, S - nk:S],
                                                    ALU.mult, ALU.add))
                        src = score_b[:, n % 2, 0:nk]
                    link(V.reduce_max(at_stat[:, n % 4, 0:1], src, AX.X))
                    V.tensor_scalar(at_stat[:, n % 4, 1:2], at_stat[:, n % 4, 0:1], -scale, None,
                                    ALU.mult).then_inc(sem["at_max"], 1)

                def normalise(n):
                    nk = keys_of(n)
                    dve.wait_ge(sem["at_exp"], n + 1)
                    link(V.reciprocal(at_stat[:, n % 4, 3:4], at_stat[:, n % 4, 2:3]))
                    V.tensor_scalar(prob[:, n % 2, 0:nk], prob[:, n % 2, 0:nk], at_stat[:, n % 4, 3:4], None,
                                    ALU.mult).then_inc(sem["at_prob"], 1)

                def out_lo(n):
                    g, last = out_group(n)
                    if not last:
                        return
                    if kind == "mem":
                        tiles = [(2 * (g - 12) + j, out_bank(n, j), 12 + 2 * (g - 12) + j) for j in range(2)]
                    else:
                        tiles = [(g - (4 if kind != "one" else 0), out_bank(n), g)]
                    for k, bank, count in tiles:
                        dve.wait_ge(sem["at_out_hi"], count + 1)
                        V.tensor_tensor(dst_lo[:, k, :], ps[:, bank, :], dst_hi[:, k, :].bitcast(F32),
                                        ALU.subtract).then_inc(sem["at_out_lo"], 1)

                maximum(a)
                maximum(a + 1)
                for n in range(a, b):
                    normalise(n)
                    if n + 2 < b:
                        maximum(n + 2)
                    if n - 2 >= a:
                        out_lo(n - 2)
                out_lo(b - 2)
                out_lo(b - 1)

            attention("one", prob1, QK1 ** -0.5, at_hi, at_lo)
            modulation(1)
            dve.wait_ge(sem["ada_mod"], 10)
            V.scalar_tensor_tensor(scl[:, 2, :], mod[:, 32:40, 0], 1.0, vecT[:, VEC_AT["norm2_g"]:VEC_AT["norm2_g"] + KT],
                                   ALU.add, ALU.mult).then_inc(sem["scl2_done"], 1)

            for i in range(8):
                dve.wait_ge(sem["fc_mm"], i + 1)
                V.tensor_copy(f_c[:, i // 2, 2 * (i % 2):2 * (i % 2) + 2, :].rearrange("p t c -> p (t c)"),
                              ps[:, 4 + i % 4, :]).then_inc(sem["fc_copied"], 1)
            for g in range(4):
                dve.wait_ge(sem["fm_hi_done"], g + 1)
                V.tensor_tensor(fm_lo[:, g, :], ps[:, 4 + g, :], fm_hi[:, g, :].bitcast(F32),
                                ALU.subtract).then_inc(sem["fm_lo_done"], 1)

            for j in range(4):
                u = first["merge1"] + 3 * j
                for jj in range(2):
                    dve.wait_ge(bank_stored[bank_of(u, jj)], stored_count(u, jj))
                    dve.wait_ge(sem["tile_done"], tile_count(u + 2, jj))
                    p = bank(u + 2, jj)
                    if j:
                        dve.wait_ge(sem["y_t_done"], 2 * j - 1 + jj)
                    V.tensor_tensor(y_part[:, jj, :], p, sig1[:, j % 2, jj, :],
                                    ALU.mult).then_inc(bank_stored[bank_of(u + 2, jj)], 1)
                for jj in range(2):
                    k = 2 * j + jj
                    dve.wait_ge(bank_stored[bank_of(u + 1, jj)], stored_count(u + 1, jj))
                    dve.wait_ge(sem["tile_done"], tile_count(u + 2, 2 + jj))
                    p = bank(u + 2, 2 + jj)
                    if j:
                        dve.wait_ge(sem["y_hi_done"], k - 1)
                        dve.wait_ge(sem["y_lo_done"], k - 1)
                    else:
                        dve.wait_ge(sem["n_hi"], 8 * NORM_INDEX[N_CTX] + 8)
                        dve.wait_ge(sem["n_lo"], 8 * NORM_INDEX[N_CTX] + 8)
                    V.tensor_tensor(tmp2[:, jj, :], p, sig1[:, j % 2, 2 + jj, :],
                                    ALU.mult).then_inc(bank_stored[bank_of(u + 2, 2 + jj)], 1)
                    dve.wait_ge(bank_stored[bank_of(u + 2, 2 + jj)], stored_count(u + 2, 2 + jj))
                    dve.wait_ge(bank_stored[bank_of(u + 2, jj)], stored_count(u + 2, jj))
                    V.tensor_tensor(tmp2[:, jj, :], tmp2[:, jj, :], y_part[:, jj, :], ALU.add).then_inc(sem["y_t_done"], 1)
                for jj in range(2):
                    k = 2 * j + jj
                    dve.wait_ge(sem["y_hi_done"], k + 1)
                    V.tensor_tensor(y_lo[:, k, :], tmp2[:, jj, :], y_hi[:, k, :].bitcast(F32),
                                    ALU.subtract).then_inc(sem["y_lo_done"], 1)

            def add_to_stream(u, jj, k, gain=None, loop=None):
                dve.wait_ge(sem["tile_done"], tile_count(u, jj, loop))
                p = bank(u, jj)
                if gain is None:
                    ins = V.tensor_tensor(xT[:, k, :], p, xT[:, k, :], ALU.add)
                else:
                    ins = V.scalar_tensor_tensor(xT[:, k, :], p, gain, xT[:, k, :], ALU.mult, ALU.add)
                ins.then_inc(bank_stored[bank_of(u, jj)], 1)

            def out_phase(name, n, gain=None):
                for j in range(4):
                    for jj in range(2):
                        k = 2 * j + jj
                        add_to_stream(first[name] + j, jj, k, gain(k) if gain else None)
                        if k:
                            add_square(n, k - 1)
                add_square(n, KT - 1)

            out_phase("out1", N_2, lambda k: mod[:, 16 + k, 0:1])
            inverse_of(N_2)
            dve.wait_ge(sem["scl2_done"], 1)
            normed(N_2, xT, lambda k: scl[:, 2, k:k + 1], h_lo, h_hi, lambda k: mod[:, 24 + k, 0:1])

            def mlp_chunk(u0_, count0, loop=None, last=False):
                for j in range(4):
                    for jj in range(2):
                        q = 2 * j + jj
                        dve.wait_ge(bank_stored[bank_of(u0_ + j, jj)], stored_count(u0_ + j, jj, loop))
                        if not (isinstance(count0, int) and count0 + q < 2):
                            dve.wait_ge(sem["g_hi_done"], count0 + (q - 1))
                            dve.wait_ge(sem["g_lo_done"], count0 + (q - 1))
                        V.tensor_tensor(rsq[:, jj, :], relu[:, jj, :], relu[:, jj, :], ALU.mult).then_inc(sem["rsq_done"], 1)
                    for jj in range(2):
                        q = 2 * j + jj
                        dve.wait_ge(sem["g_hi_done"], count0 + (q + 1))
                        V.tensor_tensor(g_lo[:, q, :], rsq[:, jj, :], g_hi[:, q, :].bitcast(F32),
                                        ALU.subtract).then_inc(sem["g_lo_done"], 1)
                for j in range(4):
                    for jj in range(2):
                        k = 2 * j + jj
                        add_to_stream(u0_ + 4 + j, jj, k, mod[:, 40 + k, 0:1], loop)
                        if last and k:
                            add_square(N_MIX, k - 1)

            mlp_chunk(first["mlp"], 0)
            with dve.Fori(0, 2) as i:
                mlp_chunk(first["mlp"] + 8, i * 8 + 8, (i, 8))
            mlp_chunk(first["mlp"] + 24, 24, last=True)
            add_square(N_MIX, KT - 1)
            inverse_of(N_MIX)
            normed(N_MIX, xT, lambda k: col("norm_mix_2", k), h_lo, h_hi, None)

            ab = ps[:, 4, 0:NT * 16].rearrange("p (t c) -> p t c", c=16)
            dve.wait_ge(sem["ab_turned"], 1)
            V.memset(pad_in[:, :, 0:3], 0.0).then_inc(sem["c_pad"], 1)
            V.tensor_tensor(gp[:, 0, :, :], ab[:, :, 0:HA], bc[:, 2 * QK1:2 * QK1 + HA].unsqueeze(1).broadcast_to([P, NT, HA]),
                            ALU.add)
            V.tensor_copy(gp[:, 9, :, :], ab[:, :, HA:16]).then_inc(sem["gate_dve"], 1)
            dve.wait_ge(sem["gate_dve"], 1)
            dve.wait_ge(sem["gate_act"], 1)
            link(V.tensor_scalar(gp[:, 1, :, :], gp[:, 0, :, :], 0.0, None, ALU.max))
            link(V.tensor_tensor(gp[:, 3, :, :], gp[:, 3, :, :], gp[:, 1, :, :], ALU.add))
            V.scalar_tensor_tensor(gp[:, 4, :, :], gp[:, 3, :, :], -1.0, gp[:, 10, 0, :].unsqueeze(1).broadcast_to([P, NT, HA]),
                                   ALU.mult, ALU.mult)
            V.tensor_scalar(gp[:, 11, :, :], gp[:, 6, :, :], -1.0, None, ALU.mult).then_inc(sem["gate_dve"], 1)
            dve.wait_ge(sem["gate_cum"], 1)
            cum = ps[:, 5, 0:64].rearrange("p (i t c) -> p i t c", i=2, c=HA)
            link(V.tensor_copy(gp[:, 5, :, :], cum[:, 0]))
            V.tensor_tensor(gp[:, 9, :, :], cum[:, 1], gp[:, 5, :, :], ALU.subtract).then_inc(sem["gate_dve"], 1)
            dve.wait_ge(sem["gate_act"], 2)
            V.tensor_tensor(gp[:, 7, :, :], gp[:, 10, :, :], gp[:, 6, :, :], ALU.mult).then_inc(sem["gate_dve"], 1)

            def taps(j, h):
                at_ = (j // 2) * HA + h
                return [col("conv_w_2", 24 * i + at_) for i in range(4)]

            def convolve_a(p, j):
                v = first[f"pair{p}"] + j // 2
                dve.wait_ge(bank_stored[bank_of(v, j % 2)], stored_count(v, j % 2))
                w, x = taps(j, 2 * p + j % 2), pad_in[:, j, :]
                link(V.tensor_scalar(conv[:, j, :], x[:, 3:3 + S], w[3], None, ALU.mult))
                link(V.scalar_tensor_tensor(conv[:, j, :], x[:, 2:2 + S], w[2], conv[:, j, :], ALU.mult, ALU.add))

            def convolve_b(p, j):
                w, x = taps(j, 2 * p + j % 2), pad_in[:, j, :]
                link(V.scalar_tensor_tensor(conv[:, j, :], x[:, 1:1 + S], w[1], conv[:, j, :], ALU.mult, ALU.add))
                V.scalar_tensor_tensor(conv[:, j, :], x[:, 0:S], w[0], conv[:, j, :],
                                       ALU.mult, ALU.add).then_inc(sem["c_conv"], 1)

            def convolve(p, j):
                convolve_a(p, j)
                convolve_b(p, j)

            for p in range(4):
                u = first[f"pair{p}"]
                if p == 0:
                    dve.wait_ge(sem["c_pad"], 1)
                    for j in range(6):
                        convolve(p, j)
                for j in range(4):
                    g = 4 + 4 * p + j
                    if j == 0:
                        inverse_of(g)
                    if j < 3:
                        inverse_of(g + 1)
                    dve.wait_ge(sem["n_bc"], g + 1)
                    V.scalar_tensor_tensor(conv[:, j, :], conv[:, j, :], P ** -0.5 if j < 2 else 1.0,
                                           ps[:, BC_BANK + g % 2, :], ALU.mult, ALU.mult).then_inc(sem["c_normed"], 1)
                dve.wait_ge(sem["gate_act"], 2)
                dve.wait_ge(sem["gate_dve"], 4)

                def tiled(x):
                    return x.rearrange("p (t c) -> p t c", c=P)

                for a in range(2):
                    h = 2 * p + a
                    dve.wait_ge(sem["kv_turned"], 2 * h + 1)
                    k_tok = tiled(ps[:, 4 + a, :])
                    V.tensor_tensor(k_dec[:, a, :, :], k_tok, over_width(gp[:, 8, :, h]), ALU.mult)
                    V.tensor_tensor(k_bg[:, a, :, :], k_tok, over_width(gp[:, 7, :, h]), ALU.mult).then_inc(sem["k_scaled"], 1)
                    dve.wait_ge(sem["kv_turned"], 2 * h + 2)
                    V.tensor_tensor(v_b[:, a, :, :], tiled(ps[:, 6 + a, :]), over_width(gp[:, 6, :, h]),
                                    ALU.mult).then_inc(sem["k_scaled"], 1)
                for a in range(2):
                    h = 2 * p + a
                    dve.wait_ge(sem["Gb_exp"], h + 1)
                    for tt in range(NT):
                        ins = V.tensor_scalar(decay[:, a, tt, :], ps[:, 4 + a, tt * P:(tt + 1) * P], gp[:, 5, tt, h:h + 1],
                                              0.0, ALU.subtract, ALU.max)
                    ins.then_inc(sem["d_diff"], 1)
                for a in range(2):
                    h = 2 * p + a
                    dve.wait_ge(sem["d_exp"], h + 1)
                    link(V.tensor_tensor(decay[:, a, :, :], decay[:, a, :, :], over_tiles(con("incl")), ALU.mult))
                    dve.wait_ge(sem["Gb_exp"], h + 1)
                    V.tensor_tensor(q_dec[:, a, :], conv[:, a, :], eGb[:, a, :], ALU.mult).then_inc(sem["qd_done"], 1)
                for a in range(2):
                    h = 2 * p + a
                    dve.wait_ge(sem["kk_mm"], 2 * h + 1)
                    link(V.tensor_tensor(nL[:, a, :, :], tiled(ps[:, 6 + a, :]), decay[:, a, :, :], ALU.mult))
                    V.tensor_tensor(nL[:, a, :, :], nL[:, a, :, :], over_width(gp[:, 11, :, h]), ALU.mult).then_inc(sem["nL_done"], 1)
                    dve.wait_ge(sem["kk_mm"], 2 * h + 2)
                    V.tensor_tensor(pr[:, a, :, :], tiled(ps[:, 4 + a, :]), decay[:, a, :, :], ALU.mult).then_inc(sem["nL_done"], 1)
                if p == 0:
                    dve.wait_ge(sem["masks_in"], 16)
                for a in range(2):
                    h = 2 * p + a
                    dve.wait_ge(sem["qd_done"], h + 1)
                    dve.wait_ge(sem["nL_done"], 2 * h + 2)
                    link(V.tensor_copy(inv[:, a, :, :], over_tiles(con("ident"))))
                    V.copy_predicated(inv[:, a, :, :], over_tiles(masks[:, 0, :]), nL[:, a, :, :])
                    link(V.tensor_copy(invT[:, a, :, :], over_tiles(con("ident"))))
                    dve.wait_ge(sem["nLT_done"], 2 * h + 1)
                    V.copy_predicated(invT[:, a, :, :], over_tiles(masks[:, 1, :]), nLT[:, a, :, :]).then_inc(sem["inv0_done"], 1)
                dve.wait_ge(sem["inv0_done"], 2 * p + 2)
                for s in range(1, LEVELS):
                    for a in range(2):
                        n = (p * 5 + s - 1) * 2 + a
                        dve.wait_ge(sem["lv_mm"], n + 1)
                        if s < LEVELS - 1:
                            V.copy_predicated(inv[:, a, :, :], over_tiles(masks[:, 2 * s, :]), tiled(ps[:, 4 + a, :]))
                        V.copy_predicated(invT[:, a, :, :], over_tiles(masks[:, 2 * s + 1, :]),
                                          tiled(ps[:, 6 + a, :])).then_inc(sem["lv_done"], 1)
                V.memset(state[:, :, :], 0.0).then_inc(sem["r_init"], 1)
                dve.wait_ge(sem["uw_copied"], 4 * p + 4)
                for n in range(N_CHUNKS):
                    R, tt, row = 8 * p + n, n // 2, slice((n % 2) * CHUNK, (n % 2 + 1) * CHUNK)
                    dve.wait_ge(sem["r_ws"], R + 1)
                    V.tensor_tensor(u_new[row, :, :], u0[row, :, tt, :], ps[row, 4, 0:2 * P].rearrange("p (a c) -> p a c", a=2),
                                    ALU.subtract).then_inc(sem["r_u"], 1)
                    j = {0: 0, 1: 1, 5: 2, 6: 3}.get(n) if p < 3 else None
                    if j is not None:
                        convolve_a(p + 1, j)
                    dve.wait_ge(sem["r_su"], R + 1)
                    if n == 0:
                        dve.wait_ge(sem["r_init"], p + 1)
                    for a in range(2):
                        e = n * CHUNK + CHUNK - 1
                        ins = V.scalar_tensor_tensor(state[:, a, :], state[:, a, :], eGb[:, a, e:e + 1],
                                                     ps[:, 6, a * P:(a + 1) * P], ALU.mult, ALU.add)
                    ins.then_inc(sem["r_st"], 1)
                    if j is not None:
                        convolve_b(p + 1, j)
                dve.wait_ge(sem["r_oc"], 4 * p + 4)
                flat = o_tok[:, :, :, :].rearrange("p a t c -> p (a t) c")
                sq = tmp2[:, :, :].rearrange("p a (t c) -> p (a t) c", c=P)
                link(V.tensor_tensor(sq, flat, flat, ALU.mult))
                V.tensor_reduce(o_stat[:, 0, :], sq, AX.X, ALU.add).then_inc(sem["o_sq"], 1)
                dve.wait_ge(sem["o_std"], p + 1)
                link(V.reciprocal(o_stat[:, 2, :], o_stat[:, 1, :]))
                V.tensor_tensor(flat, flat, over_width(o_stat[:, 2, :]), ALU.mult).then_inc(sem["o_scaled"], 1)
                if p < 3:
                    convolve(p + 1, 4)
                for a in range(2):
                    dve.wait_ge(sem["o_turned"], 2 * p + a + 1)
                    dve.wait_ge(bank_stored[bank_of(u + 3, a)], stored_count(u + 3, a))
                    V.scalar_tensor_tensor(oaT[:, 2 * p + a, :], ps[:, 4 + a, :], col("head_norm_2"), z_s[:, a, :],
                                           ALU.mult, ALU.mult).then_inc(sem["o_done"], 1)
                if p < 3:
                    convolve(p + 1, 5)

            for k in range(HA):
                dve.wait_ge(sem["oa_hi_done"], k + 1)
                dve.wait_ge(sem["o_done"], HA)
                V.tensor_tensor(oa_lo[:, k, :], oaT[:, k, :], oa_hi[:, k, :].bitcast(F32),
                                ALU.subtract).then_inc(sem["oa_lo_done"], 1)
            for j in range(4):
                u, v = gated("aout", "sig", j), gated("aout", "proj", j)
                for jj in range(2):
                    dve.wait_ge(bank_stored[bank_of(u, jj)], stored_count(u, jj))
                    dve.wait_ge(sem["tile_done"], tile_count(v, jj))
                    p = bank(v, jj)
                    V.tensor_tensor(y2[:, 2 * j + jj, :], p, sig2[:, j % 2, jj, :],
                                    ALU.mult).then_inc(bank_stored[bank_of(v, jj)], 1)

            for g in range(2):
                for tt in range(NT):
                    dve.wait_ge(sem["vb_turned"], 4 * g + tt + 1)
                    V.tensor_copy(vb[:, tt, :], ps[:, 4 + tt, :]).then_inc(sem["vb_copied"], 1)
                attention(f"band{g}", prob_b, 1.0, ob_hi, ob_lo)
            for j in range(4):
                u, v = gated("bout", "sig", j), gated("bout", "proj", j)
                for jj in range(2):
                    k = 2 * j + jj
                    dve.wait_ge(bank_stored[bank_of(u, jj)], stored_count(u, jj))
                    dve.wait_ge(sem["tile_done"], tile_count(v, jj))
                    p = bank(v, jj)
                    if j:
                        dve.wait_ge(sem["y_t_done"], 8 + k - 1)
                    V.tensor_tensor(tmp2[:, jj, :], p, sig2[:, j % 2, jj, :],
                                    ALU.mult).then_inc(bank_stored[bank_of(v, jj)], 1)
                    dve.wait_ge(bank_stored[bank_of(v, jj)], stored_count(v, jj))
                    V.tensor_tensor(y2[:, k, :], tmp2[:, jj, :], y2[:, k, :], ALU.add).then_inc(sem["y_t_done"], 1)
            for k in range(KT):
                dve.wait_ge(sem["y_hi_done"], 8 + k + 1)
                V.tensor_tensor(h_lo[:, k, :], y2[:, k, :], h_hi[:, k, :].bitcast(F32), ALU.subtract).then_inc(sem["y_lo_done"], 1)
            out_phase("out2", N_XATTN)
            inverse_of(N_XATTN)
            normed(N_XATTN, xT, lambda k: col("norm_xattn_2", k), h_lo, h_hi, None)

            for k in range(KT):
                add_square(N_MEM, k, C)
            inverse_of(N_MEM, 2)
            normed(N_MEM, m_T, lambda k: col("norm_mem_2", k), m_lo, m_hi, None, C)
            for u in shared_lo:
                dve.wait_ge(sem["w_hi_done"], split_at[u] + 1)
                s, half = split_at[u] % 2, slice(UNIT // 2, UNIT)
                V.tensor_tensor(w_lo[:, s, half], raw[:, u % 2, half], w_hi[:, s, half].bitcast(F32),
                                ALU.subtract).then_inc(sem["w_lo_half"], 1)
            for i in range(2):
                dve.wait_ge(sem["mv_turned"], i + 1)
                V.tensor_copy(m_v[:, i, :], ps[:, 4 + 2 * i:6 + 2 * i, :].rearrange("p b c -> p (b c)")).then_inc(sem["mv_copied"], 1)
            attention("mem", prob_m, 256 ** -0.5, om_hi, om_lo)
            out_phase("mo", N_FFN)
            inverse_of(N_FFN)
            normed(N_FFN, xT, lambda k: col("norm_ffn_2", k), h_lo, h_hi, None)

            def gu_round(u0_, count0, loop=None):
                def tile(x, jj):
                    f = x[:, :, :].rearrange("p k c -> p (k c)")
                    return f[:, jj * S:(jj + 1) * S] if loop is None else f[:, bass.ds(loop[0] * (2 * S) + (2 + jj) * S, S)]

                for jj in range(2):
                    dve.wait_ge(bank_stored[bank_of(u0_, jj)], stored_count(u0_, jj, loop))
                    dve.wait_ge(sem["tile_done"], tile_count(u0_ + 1, jj, loop))
                    p = bank(u0_ + 1, jj)
                    if loop:
                        dve.wait_ge(sem["s_hi_done"], count0 + (jj - 1))
                        dve.wait_ge(sem["s_lo_done"], count0 + (jj - 1))
                    V.tensor_tensor(gu[:, jj, :], p, gate[:, jj, :], ALU.mult).then_inc(bank_stored[bank_of(u0_ + 1, jj)], 1)
                for jj in range(2):
                    dve.wait_ge(sem["s_hi_done"], count0 + (jj + 1))
                    V.tensor_tensor(tile(s_lo, jj), gu[:, jj, :], tile(s_hi, jj).bitcast(F32),
                                    ALU.subtract).then_inc(sem["s_lo_done"], 1)

            gu_round(first["gu"], 0)
            with dve.Fori(0, 10) as i:
                gu_round(first["gu"] + 2, i * 2 + 2, (i, 2))
            for k in range(KT):
                dve.wait_ge(sem["last_mm"], k + 1)
                V.tensor_tensor(xT[:, k, :], ps[:, k, :], xT[:, k, :], ALU.add).then_inc(sem["x_last"], 1)
                if k:
                    add_square(N_FINAL, k - 1)
            add_square(N_FINAL, KT - 1)
            inverse_of(N_FINAL)
            dve.wait_ge(sem["n_bc"], N_FINAL + 1)
            for k in range(KT):
                V.scalar_tensor_tensor(yT[:, k, :], xT[:, k, :], col("norm_final_2", k), ps[:, BC_BANK + N_FINAL % 2, :],
                                       ALU.mult, ALU.mult).then_inc(sem["n_t"], 1)
            for q in range(2):
                dve.wait_ge(sem["y_turned"], NT + q + 1)
                V.tensor_copy(y_out[:, q, 512:1024], ps[:, q, :]).then_inc(sem["y_copied2"], 1)

        @block.tensor
        def _(pe):
            T = nc.tensor

            def mm3(out_, w0, w, s, hi, lo, start, stop):
                wh, wl = w_hi[:, s, w0:w0 + w], w_lo[:, s, w0:w0 + w]
                T.matmul(out_, wh, hi, start=start, stop=False, skip_group_check=True)
                T.matmul(out_, wh, lo, start=False, stop=False, skip_group_check=True)
                return T.matmul(out_, wl, hi, start=False, stop=stop, skip_group_check=True)

            def gemm(u, tiles, loop=None, ready=None, late=None):
                s = split_at[u] % 2
                pe.wait_ge(sem["w_lo_done"], val(split_at, u, loop) + 1)
                if u in shared_lo:
                    pe.wait_ge(sem["w_lo_half"], lo_half_count(u))
                for pair in range(0, len(tiles), 2):
                    if pair and late:
                        late()
                    some = list(enumerate(tiles))[pair:pair + 2]
                    n = len(some[0][1][0])
                    for j, _ in some:
                        if tile_at[u] + j >= 4:
                            pe.wait_ge(bank_stored[bank_of(u, j)], stored_count(u, j, loop) - 1)
                    cut = n - 2 if n > 4 else n
                    for ks in (range(0, cut), range(cut, n)):
                        for j, (terms, w) in some:
                            for k in ks:
                                if ready and pair == 0 and j == 0:
                                    ready(k)
                                w0, hi, lo = terms[k]
                                ins = mm3(ps[:, bank_of(u, j), 0:w], w0, P, s, hi, lo, k == 0, k == n - 1)
                            if len(ks) and ks[-1] == n - 1:
                                ins.then_inc(sem["tile_done"], 1)

            def wide_gemm(u, hi, lo, loop=None, ready=None, cols=S):
                gemm(u, [([(k * 256 + jj * P, hi[:, k, 0:cols], lo[:, k, 0:cols]) for k in range(KT)], cols)
                         for jj in range(2)], loop, ready)

            def piece(u, k):
                s = split_at[u] % 2
                if k == 0:
                    pe.wait_ge(sem["w_lo_done"], split_at[u] + 1)
                for j in range(2):
                    if k == 0:
                        pe.wait_ge(bank_stored[bank_of(u, j)], stored_count(u, j) - 1)
                    ins = mm3(ps[:, bank_of(u, j), :], k * 256 + j * P, P, s, h_hi[:, k, :], h_lo[:, k, :],
                              k == 0, k == KT - 1)
                    if k == KT - 1:
                        ins.then_inc(sem["tile_done"], 1)

            def after(done, base):
                def ready(k):
                    pe.wait_ge(done, base + k + 1)
                return ready

            def sum_of(g, src, nt=NT):
                if g >= 2:
                    pe.wait_ge(sem["n_std"], g - 1)
                for tt in range(nt):
                    ins = T.matmul(ps[:, SUM_BANK + g % 2, tt * P:tt * P + 1], src[:, tt * P:(tt + 1) * P],
                                   con("ones")[:, 0:1], start=True, stop=True)
                ins.then_inc(sem["n_sum"], 1)

            def norm_sum(n, nt=NT):
                pe.wait_ge(sem["n_acc"], 7 * NORM_INDEX[n] + 7)
                sum_of(n, acc, nt)

            def spread(g, nt=NT):
                pe.wait_ge(sem["n_inv"], g + 1)
                for tt in range(nt):
                    ins = T.matmul(ps[:, BC_BANK + g % 2, tt * P:(tt + 1) * P],
                                   stat[:, g % 2, 1, tt:tt + 1].broadcast_to([P, P]), con("ident"), start=True, stop=True)
                ins.then_inc(sem["n_bc"], 1)

            def turn(out_, src):
                rows = src.shape[0]
                return T.transpose(out_, src, const[0:rows, CONST_AT["ident"]:CONST_AT["ident"] + rows])

            def ada_mm(a):
                u = ada_units[a]
                if a == 0:
                    pe.wait_ge(sem["c_silu"], 2)
                if a >= 2:
                    pe.wait_ge(sem["ada_rowed"], a - 1)
                pe.wait_ge(w_in_slot[u % 2], load_count[u])
                for k in range(KT):
                    ins = T.matmul(ps[0:2, a % 2, 0:256], silu_c[:, k, :], raw[:, u % 2, k * 256:(k + 1) * 256],
                                   start=k == 0, stop=k == KT - 1)
                ins.then_inc(sem["ada_mm"], 1)

            pe.wait_ge(sem["const_done"], 16)
            pe.wait_ge(sem["in_done"], 32)
            turn(ps[:, 4, 0:VEC_SPLIT], vec_in[0:VEC_SPLIT, 0, :])
            turn(ps[:, 4, VEC_SPLIT:VEC_N], vec_in[0:VEC_N - VEC_SPLIT, 1, :]).then_inc(sem["vec_tr"], 1)
            pe.wait_ge(sem["vec_done"], 1)
            pe.wait_ge(sem["x_in_done"], 16)
            for k in range(KT):
                if k >= 4:
                    pe.wait_ge(sem["xt_done"], k - 3)
                for tt in range(NT):
                    ins = turn(ps[:, 4 + k % 4, tt * P:(tt + 1) * P], x_in[:, tt, k * P:(k + 1) * P])
                ins.then_inc(sem["tr_done"], 1)
            ada_mm(0)
            ada_mm(1)
            pe.wait_ge(sem["c_in_done"], 16)
            for k in range(KT):
                if k < 4:
                    pe.wait_ge(sem["xt_done"], 5 + k)
                else:
                    pe.wait_ge(sem["ctx_t"], k - 3)
                for tt in range(2):
                    ins = turn(ps[:, 4 + k % 4, tt * P:(tt + 1) * P], c_in[:, tt, k * P:(k + 1) * P])
                ins.then_inc(sem["ctx_tr"], 1)

            def ada_turn(a):
                pe.wait_ge(sem["ada_rowed"], a + 1)
                if a >= 2:
                    pe.wait_ge(sem["ada_mod"], a - 1)
                for j in range(2):
                    ins = T.matmul(ps[:, 2 + a % 2, 2 * j:2 * j + 2], ada_row[:, a % 2, :][:, j * P:(j + 1) * P],
                                   const[0:2, CONST_AT["ident"]:CONST_AT["ident"] + 2], start=True, stop=True)
                ins.then_inc(sem["ada_tr"], 1)

            for a in range(1, 8):
                if a >= 2:
                    ada_mm(a)
                if a == 1:
                    pe.wait_ge(sem["ctx_t"], KT)
                    norm_sum(N_X)
                if a == 2:
                    norm_sum(N_CTX, 2)
                ada_turn(a - 1)
                if a == 3:
                    spread(N_X)
                if a == 4:
                    spread(N_CTX, 2)
            ada_turn(7)

            def ctx_there():
                pe.wait_ge(sem["n_lo"], 16)

            u = first["lat_kv"]
            wide_gemm(first["lat_q"], h_hi, h_lo, ready=after(sem["n_lo"], 0))
            pe.wait_ge(sem["ada_mod"], 8)
            gemm(u, [([(k * 256 + jj * P, x[0][:, k, :], x[1][:, k, :]) for k in range(KT)], w)
                         for x, w in (((h_hi, h_lo), S), ((c_hi, c_lo), C)) for jj in range(2)],
                 late=ctx_there)

            pe.wait_ge(sem["lat_sq"], 3)
            pe.wait_ge(sem["n_lo"], 16)
            one = const[:, CONST_AT["ones"]:CONST_AT["ones"] + 1]
            for i in range(4):
                for k in range(2):
                    T.matmul(ps[:, 4, i:i + 1], sq_q[:, k, i * P:(i + 1) * P], one, start=k == 0, stop=k == 1)
            for i in range(6):
                ins = T.matmul(ps[:, 4, 4 + i:5 + i], sq_kv[:, i * P:(i + 1) * P], one, start=True, stop=True)
            ins.then_inc(sem["lat_ss"], 1)
            pe.wait_ge(bank_stored[bank_of(u, 1)], stored_count(u, 1))
            pe.wait_ge(bank_stored[bank_of(u, 3)], stored_count(u, 3))
            for i in range(6):
                ins = turn(ps[:, 5, i * ROPE_W:(i + 1) * ROPE_W], kr_T[:, i * P:(i + 1) * P])
            ins.then_inc(sem["kr_mm"], 1)

            def qk_mm(m):
                if m == 0:
                    pe.wait_ge(sem["lat_std"], 1)
                    pe.wait_ge(sem["kr_copied"], 1)
                    pe.wait_ge(sem["lat_gained"], 3)
                    pe.wait_ge(sem["wq_done"], 16)
                    pe.wait_ge(sem["wkv_done"], 16)
                if m >= 2:
                    pe.wait_ge(sem["qk_scaled"], m - 1)
                    pe.wait_ge(sem["v_scaled"], min(m - 1, 6))
                at_ = qk_bank(m)
                for b in range(2):
                    if m < 6:
                        ins = T.matmul(ps[:, at_ + b, :], lat_kv[:, m * P:(m + 1) * P], w_kvb[:, b * 512:(b + 1) * 512],
                                       start=True, stop=True)
                    else:
                        for k in range(2):
                            ins = T.matmul(ps[:, at_ + b, 0:384], lat_q[:, k, (m - 6) * P:(m - 5) * P],
                                           w_qb[:, k, b * 384:(b + 1) * 384], start=k == 0, stop=k == 1)
                ins.then_inc(sem["qk_mm"], 1)

            def qk_turn(m):
                pe.wait_ge(sem["qk_normed"], m + 1)
                if m:
                    pe.wait_ge(sem["qk_stored"], m)
                for h in range(H1):
                    ins = turn(ps[0:QK1, 6 + h // 4, (h % 4) * P:(h % 4 + 1) * P], qk_tok[:, m % 2, h, :])
                ins.then_inc(sem["qk_turned"], 1)

            for j in range(4):
                pe.wait_ge(bank_stored[bank_of(u, j)], stored_count(u, j))
            qk_mm(0)
            qk_mm(1)
            for m in range(10):
                if m < 8:
                    qk_mm(m + 2)
                qk_turn(m)

            def modulation(b):
                pe.wait_ge(sem["ada_summed"], 8 * b + 8)
                for i in range(16):
                    ins = T.matmul(ps[:, 2 + 2 * b, i:i + 1], ada_sum[:, i // 2, (i % 2) * P:(i % 2 + 1) * P],
                                   con("ones")[:, 0:1], start=True, stop=True)
                ins.then_inc(sem["ada_batch"], 1)

            modulation(0)

            def attention(kind, ahead=()):
                a, b = ATT[kind]
                filled = [0]

                def fill(n):
                    for uu, k in ahead[filled[0]:filled[0] + n]:
                        piece(uu, k)
                    filled[0] += n

                def scores(n):
                    what, h, q = items[n]
                    nk = keys_of(n)
                    if n - 2 >= a:
                        pe.wait_ge(sem["at_exp"], n - 1)
                    tok = slice(q * P, (q + 1) * P)
                    bank = score_bank(n)
                    if what == "one":
                        T.matmul(ps[:, bank, :], qT[:, h, tok], kT[:, h, 0:S], start=True, stop=True)
                        ins = T.matmul(ps[:, bank + 1, 0:C], qT[:, h, tok], kT[:, h, S:S + C], start=True, stop=True)
                    elif what == "band":
                        row, tile = slice((h % 2) * DB, (h % 2 + 1) * DB), (h % 8) // 2
                        ins = T.matmul(ps[:, bank, 0:nk], qbT[row, tile, tok], kbT[row, tile, 0:nk], start=True, stop=True)
                    else:
                        for k in range(2):
                            ins = T.matmul(ps[:, bank, 0:nk], m_q[:, 2 * h + k, tok], m_kT[:, 2 * h + k, :],
                                           start=k == 0, stop=k == 1)
                    ins.then_inc(sem["at_scores"], 1)

                def turned(n):
                    prob = {"one": prob1, "band": prob_b, "mem": prob_m}[items[n][0]]
                    pe.wait_ge(sem["at_prob"], n + 1)
                    if n:
                        pe.wait_ge(sem["at_copied"], n)
                    for kt in range(keys_of(n) // P):
                        ins = turn(ps[:, turned_bank(n) + kt // 4, (kt % 4) * P:(kt % 4 + 1) * P], prob[:, n % 2, kt * P:(kt + 1) * P])
                    ins.then_inc(sem["at_turned"], 1)

                def values(n):
                    what, h, q = items[n]
                    g, _ = out_group(n)
                    tok = slice(q * P, (q + 1) * P)
                    pe.wait_ge(sem["at_copied"], n + 1)
                    if what == "mem":
                        pe.wait_ge(sem["at_out_lo"], max(12, 12 + 2 * (g - 13)))
                        for j in range(2):
                            for kt in range(2):
                                ins = T.matmul(ps[:, out_bank(n, j), tok], m_v[:, kt, h * 256 + j * P:h * 256 + (j + 1) * P],
                                               probT_m[:, n % 2, kt * P:(kt + 1) * P], start=kt == 0, stop=kt == 1)
                    else:
                        before = g if what == "band" else g - 1
                        if before > 0:
                            pe.wait_ge(sem["at_out_lo"], before)
                        v, pT = (v1, probT1) if what == "one" else (vb, probT_b)
                        nk = keys_of(n) // P
                        for kt in range(nk):
                            ins = T.matmul(ps[(h % 2) * 64:(h % 2 + 1) * 64, out_bank(n), tok],
                                           v[:, kt, (h % 8) * 64:(h % 8 + 1) * 64], pT[:, n % 2, kt * P:(kt + 1) * P],
                                           start=kt == 0, stop=kt == nk - 1)
                    ins.then_inc(sem["at_out"], 1)

                scores(a)
                scores(a + 1)
                fill(3)
                for n in range(a, b):
                    if n + 2 < b:
                        scores(n + 2)
                    if n % 2:
                        fill(1)
                    if n > a:
                        values(n - 1)
                    turned(n)
                values(b - 1)

            pe.wait_ge(sem["ada_mod"], 9)
            pe.wait_ge(sem["qk_stored"], 10)
            attention("one")

            modulation(1)
            pe.wait_ge(sem["at_exp"], 32)
            for j in range(2):
                wide_gemm(first["f"] + j, h_hi, h_lo)
            pe.wait_ge(sem["dft_in"], 16)
            pe.wait_ge(sem["at_out_lo"], 4)
            pe.wait_ge(sem["ada_mod"], 10)
            dft_c = dft[:, NT * 2 * S:]
            dft_n = dft[:, 0:NT * 2 * S].rearrange("p (t i c) -> p t i c", i=2, c=S)
            for i in range(8):
                g = i // 2
                pe.wait_ge(bank_stored[bank_of(first["f"] + g // 2, g % 2)], stored_count(first["f"] + g // 2, g % 2))
                if i >= 4:
                    pe.wait_ge(sem["fc_copied"], i - 3)
                for tt in range(2):
                    tok = slice((2 * (i % 2) + tt) * P, (2 * (i % 2) + tt + 1) * P)
                    ins = T.matmul(ps[:, 4 + i % 4, tt * 256:(tt + 1) * 256], f_T[:, g, tok], dft_c, start=True, stop=True)
                ins.then_inc(sem["fc_mm"], 1)
            for g in range(4):
                pe.wait_ge(sem["fc_copied"], g + 5)
                for tt in range(NT):
                    for i in range(2):
                        ins = T.matmul(ps[:, 4 + g, :], f_c[:, g, tt, i * P:(i + 1) * P], dft_n[:, tt, i, :],
                                       start=tt == 0 and i == 0, stop=tt == NT - 1 and i == 1)
                ins.then_inc(sem["fm_mm"], 1)

            for j in range(4):
                u = first["merge1"] + 3 * j
                wide_gemm(u, h_hi, h_lo)
                wide_gemm(u + 1, h_hi, h_lo)
                if j == 0:
                    pe.wait_ge(sem["fm_lo_done"], 4)
                gemm(u + 2, [([(1024 * i + k * 256 + jj * P, hi[:, k, :], lo[:, k, :]) for k in range(4)], S)
                             for i, (hi, lo) in enumerate(((fm_hi, fm_lo), (at_hi, at_lo))) for jj in range(2)])

            def out_phase(name, hi, lo, ready, n):
                for j in range(4):
                    wide_gemm(first[name] + j, hi, lo, ready=ready if j == 0 else None)
                norm_sum(n)
                spread(n)

            out_phase("out1", y_hi, y_lo, after(sem["y_lo_done"], 0), N_2)

            def mlp_chunk(u0_, count0, loop=None):
                for j in range(4):
                    wide_gemm(u0_ + j, h_hi, h_lo, loop, after(sem["n_lo"], 16) if loop is None and j == 0 else None)
                for j in range(4):
                    wide_gemm(u0_ + 4 + j, g_hi, g_lo, loop, after(sem["g_lo_done"], count0) if j == 0 else None)

            mlp_chunk(first["mlp"], 0)
            with pe.Fori(0, 2) as i:
                mlp_chunk(first["mlp"] + 8, i * 8 + 8, (i, 8))
            mlp_chunk(first["mlp"] + 24, 24)
            norm_sum(N_MIX)
            spread(N_MIX)

            u = first["ab"]
            gemm(u, [([(k * P, h_hi[:, k, :], h_lo[:, k, :]) for k in range(KT)], S)], ready=after(sem["n_lo"], 24))
            pe.wait_ge(bank_stored[bank_of(u, 0)], stored_count(u, 0))
            for tt in range(NT):
                ins = turn(ps[:, 4, tt * 16:(tt + 1) * 16], ab_T[:, tt * P:(tt + 1) * P])
            ins.then_inc(sem["ab_turned"], 1)
            wide_gemm(first["pair0"], h_hi, h_lo)
            pe.wait_ge(sem["gate_dve"], 2)
            rhs = gp[:, 4, :, :].rearrange("p t c -> p (t c)")
            T.matmul(ps[:, 5, 0:32], con("tri"), rhs, start=True, stop=True)
            T.matmul(ps[:, 5, 32:64], con("same"), rhs, start=True, stop=True).then_inc(sem["gate_cum"], 1)
            pe.wait_ge(sem["gate_dve"], 3)

            def tok(tt):
                return slice(tt * P, (tt + 1) * P)

            for p in range(4):
                u = first[f"pair{p}"]
                after_p = first[f"pair{p + 1}"] if p < 3 else first["aout"]
                ahead = [(after_p + i, k) for i in range(3 if p < 3 else 2) for k in range(KT)]
                filled = [0]

                def fill(n):
                    for uu, k in ahead[filled[0]:filled[0] + n]:
                        piece(uu, k)
                    filled[0] += n

                if p == 0:
                    for kind in range(1, 4):
                        wide_gemm(u + kind, h_hi, h_lo)
                for j in range(4):
                    g = 4 + 4 * p + j
                    pe.wait_ge(sem["c_sq"], 4 * p + j + 1)
                    sum_of(g, sq2[:, j % 2, :])
                    if p and j < 2:
                        piece(u + 3, 6 + j)
                    if j:
                        if g - 1 >= 6:
                            pe.wait_ge(sem["c_normed"], g - 6)
                        spread(g - 1)
                pe.wait_ge(sem["c_normed"], 4 * p + 2)
                spread(7 + 4 * p)
                pe.wait_ge(sem["c_normed"], 4 * p + 4)
                pe.wait_ge(sem["c_silued"], 6 * p + 6)
                for a in range(2):
                    for tt in range(NT):
                        ins = turn(ps[:, 4 + a, tok(tt)], conv[:, 2 + a, tok(tt)])
                    ins.then_inc(sem["kv_turned"], 1)
                    for tt in range(NT):
                        ins = turn(ps[:, 6 + a, tok(tt)], conv[:, 4 + a, tok(tt)])
                    ins.then_inc(sem["kv_turned"], 1)
                for a in range(2):
                    h = 2 * p + a
                    pe.wait_ge(sem["k_scaled"], 2 * h + 1)
                    for tt in range(NT):
                        ins = T.matmul(ps[:, 4 + a, tok(tt)], gp[:, 4, tt, h:h + 1].broadcast_to([P, P]), con("tri"),
                                       start=True, stop=True)
                    ins.then_inc(sem["Gb_mm"], 1)
                for a in range(2):
                    h = 2 * p + a
                    pe.wait_ge(sem["k_scaled"], 2 * h + 2)
                    for tt in range(NT):
                        ins = T.matmul(ps[:, 6 + a, tok(tt)], conv[:, 2 + a, tok(tt)], conv[:, 2 + a, tok(tt)], start=True, stop=True)
                    ins.then_inc(sem["kk_mm"], 1)
                    pe.wait_ge(sem["Gb_exp"], h + 1)
                    pe.wait_ge(sem["d_diff"], h + 1)
                    for tt in range(NT):
                        ins = T.matmul(ps[:, 4 + a, tok(tt)], conv[:, a, tok(tt)], conv[:, 2 + a, tok(tt)], start=True, stop=True)
                    ins.then_inc(sem["kk_mm"], 1)
                fill(3)
                for a in range(2):
                    for i, src in enumerate((nL, pr)):
                        pe.wait_ge(sem["nL_done"], 4 * p + 2 * a + i + 1)
                        for tt in range(NT):
                            ins = turn(ps[:, (6 if i == 0 else 4) + a, tok(tt)], src[:, a, tt, :])
                        ins.then_inc(sem["nL_turned"], 1)
                fill(2)
                pe.wait_ge(sem["nLT_done"], 4 * p + 4)
                for s in range(1, LEVELS):
                    for a in range(2):
                        n = (p * 5 + s - 1) * 2 + a
                        if a:
                            fill(1)
                        if s == 1:
                            pe.wait_ge(sem["inv0_done"], 2 * p + a + 1)
                        else:
                            pe.wait_ge(sem["lv_done"], n - 1)
                        for tt in range(NT):
                            ins = T.matmul(ps[:, 6 + a, tok(tt)], nLT[:, a, tt, :], inv[:, a, tt, :], start=True, stop=True)
                        ins.then_inc(sem["lv_m1"], 1)
                    for a in range(2):
                        n = (p * 5 + s - 1) * 2 + a
                        pe.wait_ge(sem["lv_copied"], n + 1)
                        if s < LEVELS - 1:
                            for tt in range(NT):
                                T.matmul(ps[:, 4 + a, tok(tt)], invT[:, a, tt, :], prod[:, a, tt, :], start=True, stop=True)
                        for tt in range(NT):
                            ins = T.matmul(ps[:, 6 + a, tok(tt)], prod[:, a, tt, :], invT[:, a, tt, :], start=True, stop=True)
                        ins.then_inc(sem["lv_mm"], 1)
                for a in range(2):
                    pe.wait_ge(sem["lv_done"], (p * 5 + 4) * 2 + a + 1)
                    for tt in range(NT):
                        ins = T.matmul(ps[:, 4 + a, tok(tt)], invT[:, a, tt, :], v_b[:, a, tt, :], start=True, stop=True)
                    ins.then_inc(sem["uw_mm"], 1)
                    for tt in range(NT):
                        ins = T.matmul(ps[:, 6 + a, tok(tt)], k_bg[:, a, tt, :], invT[:, a, tt, :], start=True, stop=True)
                    ins.then_inc(sem["uw_mm"], 1)
                fill(1)
                pe.wait_ge(sem["uw_copied"], 4 * p + 4)
                pe.wait_ge(sem["r_init"], p + 1)
                for n in range(N_CHUNKS):
                    R, tt, r0_ = 8 * p + n, n // 2, (n % 2) * CHUNK
                    row, ch = slice(r0_, r0_ + CHUNK), slice(n * CHUNK, (n + 1) * CHUNK)
                    ob = 5 + 2 * (tt % 2)
                    if n:
                        if p < 3 and n < 6:
                            fill(1)
                        pe.wait_ge(sem["r_st"], R)
                    for a in range(2):
                        ins = T.matmul(ps[row, 4, a * P:(a + 1) * P], wT[:, a, ch], state[:, a, :], start=True, stop=True)
                    ins.then_inc(sem["r_ws"], 1)
                    if tt >= 2:
                        pe.wait_ge(sem["r_oc"], 4 * p + tt - 1)
                    for a in range(2):
                        T.matmul(ps[row, ob, a * P:(a + 1) * P], q_dec[:, a, ch], state[:, a, :], start=a == 0, stop=False,
                                 skip_group_check=True)
                    fill(1)
                    pe.wait_ge(sem["r_u"], R + 1)
                    for a in range(2):
                        T.matmul(ps[row, ob, a * P:(a + 1) * P], prT[row, a, tt, ch.start - tt * P:ch.stop - tt * P], u_new[row, a, :],
                                 start=False, stop=True, skip_group_check=True)
                    for a in range(2):
                        ins = T.matmul(ps[:, 6, a * P:(a + 1) * P], k_dec[row, a, tt, :], u_new[row, a, :], start=True, stop=True)
                    ins.then_inc(sem["r_su"], 1)
                if p < 3:
                    for k in range(4):
                        piece(first[f"pair{p + 1}"] + 3, k)
                pe.wait_ge(sem["o_scaled"], p + 1)
                for a in range(2):
                    for tt in range(NT):
                        ins = turn(ps[:, 4 + a, tok(tt)], o_tok[:, a, tt, :])
                    ins.then_inc(sem["o_turned"], 1)
                if p < 3:
                    for k in range(4, 6):
                        piece(first[f"pair{p + 1}"] + 3, k)
                    pe.wait_ge(sem["o_done"], 2 * p + 2)

            def gated_out(name, hi, lo, done, base):
                for n, (kind, j) in enumerate(GATED):
                    if n >= 2 and kind == "sig":
                        wide_gemm(first[name] + n, h_hi, h_lo)
                    elif n >= 2:
                        wide_gemm(first[name] + n, hi, lo, ready=after(done, base) if j == 0 else None)

            gated_out("aout", oa_hi, oa_lo, sem["oa_lo_done"], 0)

            for g in range(2):
                u = first[f"band{g}"]
                for j in range(2 * g, 6):
                    wide_gemm(u + j, h_hi, h_lo)
                for j in range(6):
                    pe.wait_ge(bank_stored[bank_of(u + j, 0)], stored_count(u + j, 0))
                    pe.wait_ge(bank_stored[bank_of(u + j, 1)], stored_count(u + j, 1))
                if g:
                    pe.wait_ge(sem["at_out_lo"], 8)
                pe.wait_ge(sem["o_done"], 8)
                for tt in range(NT):
                    for i in range(4):
                        ins = turn(ps[:, 4 + tt, i * P:(i + 1) * P], vbT[:, i, tok(tt)])
                    ins.then_inc(sem["vb_turned"], 1)
                pe.wait_ge(sem["vb_copied"], 4 * g + 4)
                attention(f"band{g}", [(last_of[f"band{g}"] + i, k) for i in range(2) for k in range(KT)])
            gated_out("bout", ob_hi, ob_lo, sem["at_out_lo"], 4)
            out_phase("out2", h_hi, h_lo, after(sem["y_lo_done"], 8), N_XATTN)

            for j in range(3):
                wide_gemm(first["mq"] + j, h_hi, h_lo, ready=after(sem["n_lo"], 32) if j == 0 else None)
                if j == 1:
                    pe.wait_ge(sem["m_in_done"], 16)
                    pe.wait_ge(sem["n_t"], 8 * NORM_INDEX[N_XATTN] + 8)
                for k in range(4 * (j - 1), 4 * j) if j else ():
                    if k >= 4:
                        pe.wait_ge(sem["m_T_done"], k - 3)
                    for tt in range(2):
                        ins = turn(ps[:, 4 + k % 4, tok(tt)], m_in[:, tt, k * P:(k + 1) * P])
                    ins.then_inc(sem["m_tr"], 1)
            for k in range(5):
                piece(first["mq"] + 3, k)
            pe.wait_ge(sem["m_T_done"], KT)
            norm_sum(N_MEM, 2)
            for k in range(5, KT):
                piece(first["mq"] + 3, k)
            spread(N_MEM, 2)
            for j in range(8):
                wide_gemm(first["mkv"] + j, m_hi, m_lo, ready=after(sem["n_lo"], 40) if j == 0 else None, cols=C)
            for j in range(8):
                pe.wait_ge(bank_stored[bank_of(first["mkv"] + j, 0)], stored_count(first["mkv"] + j, 0))
                pe.wait_ge(bank_stored[bank_of(first["mkv"] + j, 1)], stored_count(first["mkv"] + j, 1))
            for i in range(2):
                for k in range(KT):
                    ins = turn(ps[:, 4 + 2 * i + k // 4, (k % 4) * P:(k % 4 + 1) * P], m_vT[:, k, tok(i)])
                ins.then_inc(sem["mv_turned"], 1)
            pe.wait_ge(sem["mv_copied"], 2)
            attention("mem")
            out_phase("mo", om_hi, om_lo, after(sem["at_out_lo"], 12), N_FFN)

            def gu_round(u0_, loop=None):
                for j in range(2):
                    wide_gemm(u0_ + j, h_hi, h_lo, loop, after(sem["n_lo"], 48) if loop is None and j == 0 else None)

            gu_round(first["gu"])
            with pe.Fori(0, 10) as i:
                gu_round(first["gu"] + 2, (i, 2))

            def down(j, loop=None):
                u = first["down2"] + j
                pe.wait_ge(sem["w_lo_done"], val(split_at, u, loop) + 1)
                pe.wait_ge(sem["s_lo_done"], (2 * j if loop is None else i_ * 4 + 2 * j) + 2)
                s = split_at[u] % 2
                for o in range(8):
                    for k in range(2):
                        if loop is None:
                            hi, lo = s_hi[:, 2 * j + k, :], s_lo[:, 2 * j + k, :]
                        else:
                            at_ = bass.ds(i_ * (4 * S) + (2 * j + k) * S, S)
                            hi, lo = (x[:, :, :].rearrange("p k c -> p (k c)")[:, at_] for x in (s_hi, s_lo))
                        ins = mm3(ps[:, o, :], k * D + o * P, P, s, hi, lo, j == 0 and k == 0, False)
                ins.then_inc(sem["w_mm_done"], 1)

            for j in range(2):
                pe.wait_ge(bank_stored[bank_of(first["gu"] + 20, j)], stored_count(first["gu"] + 20, j))
                pe.wait_ge(bank_stored[bank_of(first["gu"] + 21, j)], stored_count(first["gu"] + 21, j))
            pe.wait_ge(sem["n_t"], 8 * NORM_INDEX[N_FFN] + 8)
            down(0)
            with pe.Fori(0, 4) as i_:
                for j in range(2):
                    down(1 + j, (i_, 2))
            down(9)
            u = first["down2"] + 10
            pe.wait_ge(sem["w_lo_done"], split_at[u] + 1)
            pe.wait_ge(sem["s_lo_done"], 22)
            for o in range(8):
                for k in range(2):
                    ins = mm3(ps[:, o, :], k * D + o * P, P, split_at[u] % 2, s_hi[:, 20 + k, :], s_lo[:, 20 + k, :],
                              False, k == 1)
                ins.then_inc(sem["last_mm"], 1)
            pe.wait_ge(sem["x_last"], KT)
            norm_sum(N_FINAL)
            spread(N_FINAL)
            for half in range(2):
                pe.wait_ge(sem["n_t"], 8 * NORM_INDEX[N_FINAL] + 4 * half + 4)
                for q in range(NT):
                    if half:
                        pe.wait_ge(sem["y_copied"], q + 1)
                    for k in range(4):
                        ins = turn(ps[:, q, k * P:(k + 1) * P], yT[:, 4 * half + k, tok(q)])
                    ins.then_inc(sem["y_turned"], 1)


_TWO_D = ["ada_w", "w_in", "w_fourier", "w_qb", "w_kvb", "w_mla_o", "w_out", "w_up", "w_down", "w_in_2", "w_a_out_2",
          "w_b_out_2", "w_o_2", "w_mq_2", "w_mkv_2", "w_mo_2", "w_gate_up_2", "w_down_2", "x", "ctx", "mem_2"]


def kernel(**inputs):
    import concourse.bacc as bacc
    from concourse.bass_utils import run_bass_kernel_spmd

    arrays = {}
    for name in _TWO_D:
        a = np.asarray(inputs[name])
        arrays[name] = np.ascontiguousarray(a.reshape(a.shape[-2:]))
    rows = [np.asarray(inputs[name]).reshape(-1, P) for name, _ in VEC_ROWS]
    arrays["vec"] = np.ascontiguousarray(np.concatenate(rows, axis=0))
    wide = [np.asarray(inputs[n]).reshape(1, -1) for n in ("q_gain", "k_gain", "dt_bias_2", "a_log_2")]
    arrays["bc"] = np.ascontiguousarray(np.broadcast_to(np.concatenate(wide, axis=1), (P, 2 * QK1 + 2 * HA)))
    dist = 384 + np.arange(P)[:, None] - np.arange(S)[None, :]
    arrays["bias_band"] = np.ascontiguousarray(
        np.asarray(inputs["rel_bias_2"])[:, np.clip(dist, -(CHUNK - 1), MAX_REL) + (CHUNK - 1)])
    arrays.update(shape_constants())

    nc = bacc.Bacc("TRN2", target_bir_lowering=False, num_devices=1)
    t = {n: nc.dram_tensor(n, a.shape, mybir.dt.from_np(a.dtype), kind="ExternalInput").ap() for n, a in arrays.items()}
    out = nc.dram_tensor("out", (S, D), F32, kind="ExternalOutput").ap()
    build(nc, t, out)
    got = run_bass_kernel_spmd(nc, [arrays], core_ids=[0])
    return got.results[0]["out"].reshape(1, S, D)
```
